# Optimizing a Trainium2 kernel written in Bass

```python
import math
import jax
import jax.numpy as jnp
from jax import lax
import numpy as np

D_MODEL = 2048
BATCH = 1
SEQ = 256
DEPTH = 1
DEC_BATCH = 8
DEC_SEQ = 4
PAST_LEN = 2048
PAGE_SIZE = 128

N_META = 16
HEAD_DIM = 64
RWKV_WIDTH = D_MODEL // 2
ATTN_WIDTH = D_MODEL - RWKV_WIDTH
RWKV_HEADS = RWKV_WIDTH // HEAD_DIM
ATTN_HEADS = ATTN_WIDTH // HEAD_DIM
KV_HEADS = 4
GROUP = ATTN_HEADS // KV_HEADS
KV_WIDTH = KV_HEADS * HEAD_DIM
DECAY_LORA = 64
ICLR_LORA = 64
GATE_LORA = 160
RWKV_COLS = 3 * RWKV_WIDTH + DECAY_LORA + ICLR_LORA + GATE_LORA
RWKV_SPLITS = (RWKV_WIDTH, 2 * RWKV_WIDTH, 3 * RWKV_WIDTH, 3 * RWKV_WIDTH + DECAY_LORA,
               3 * RWKV_WIDTH + DECAY_LORA + ICLR_LORA)
GN_EPS = 64e-5
IDX_HEADS = 8
IDX_DIM = 128
IDX_TOPK = 256
ATTN_COLS = ATTN_WIDTH + 2 * KV_WIDTH + IDX_HEADS * IDX_DIM + IDX_DIM + IDX_HEADS
ATTN_SPLITS = (ATTN_WIDTH, ATTN_WIDTH + KV_WIDTH, ATTN_WIDTH + 2 * KV_WIDTH,
               ATTN_WIDTH + 2 * KV_WIDTH + IDX_HEADS * IDX_DIM,
               ATTN_WIDTH + 2 * KV_WIDTH + IDX_HEADS * IDX_DIM + IDX_DIM)
IN_COLS = RWKV_COLS + ATTN_COLS
ATTN_Q_BLOCK = 16
REL_BUCKETS = 32
REL_MAX_DIST = 128
PEER_HEADS = 8
PEER_NKEYS = 128
PEER_EXPERTS = PEER_NKEYS * PEER_NKEYS
PEER_QUERY = 256
PEER_HALF = PEER_QUERY // 2
PEER_TOPK = 16
PEER_BLOCK = 128
DN_ALPHA = (2 * DEPTH) ** 0.25
DN_BETA = (8 * DEPTH) ** -0.25
LN_EPS = 1e-5

kernel_name = 'hymba_rwkv7_dsa_peer_decode_step'

def layer_norm(x, g, b):
    xf = x.astype(jnp.float32)
    mu = jnp.mean(xf, axis=-1, keepdims=True)
    var = jnp.mean(jnp.square(xf - mu), axis=-1, keepdims=True)
    y = (xf - mu) * lax.rsqrt(var + LN_EPS) * g.astype(jnp.float32) + b.astype(jnp.float32)
    return y.astype(x.dtype)

def rel_bucket(dist):
    max_exact = REL_BUCKETS // 2
    d = jnp.maximum(dist, 0)
    log_b = max_exact + (jnp.log(jnp.maximum(d, 1).astype(jnp.float32) / max_exact)
                         / math.log(REL_MAX_DIST / max_exact) * (REL_BUCKETS - max_exact)).astype(jnp.int32)
    return jnp.where(d < max_exact, d, jnp.minimum(log_b, REL_BUCKETS - 1))

def take_rows(a, idx):
    return jax.vmap(lambda rows, i: rows[i])(a, idx)

def rwkv7_mix(feat, shift_prev, wkv_prev, mu, w0, w_up, a0, a_up, g_up, k_k, k_a, r_k, gn_g, gn_b):
    f32 = jnp.float32
    B, L, _ = feat.shape
    prev = jnp.concatenate([shift_prev[:, None].astype(feat.dtype), feat[:, :-1]], axis=1)
    xm = feat + (prev - feat) * mu
    r, k, v, w_lo, a_lo, g_lo = jnp.split(xm, list(RWKV_SPLITS), axis=-1)
    logw = -jax.nn.softplus(-(w0 + jnp.tanh(w_lo) @ w_up).astype(f32)) - 0.5
    decay = jnp.exp(-jnp.exp(logw))
    a = jax.nn.sigmoid((a0 + a_lo @ a_up).astype(f32))
    g = (jax.nn.sigmoid(g_lo) @ g_up).astype(f32)
    hs = (B, L, RWKV_HEADS, HEAD_DIM)
    kk = (k.astype(f32) * k_k.astype(f32)).reshape(hs)
    kk = kk / jnp.maximum(jnp.linalg.norm(kk, axis=-1, keepdims=True), 1e-12)
    k_h = (k.astype(f32) * (1.0 + (a - 1.0) * k_a.astype(f32))).reshape(hs)
    r_h = r.astype(f32).reshape(hs)
    v_h = v.astype(f32).reshape(hs)
    w_h = decay.reshape(hs)
    b_h = kk * a.reshape(hs)

    def step(S, inp):
        r_t, w_t, k_t, v_t, kk_t, b_t = inp
        s_kk = jnp.einsum('bhvk,bhk->bhv', S, kk_t)
        S = (S * w_t[:, :, None, :] - s_kk[..., None] * b_t[:, :, None, :]
             + v_t[..., None] * k_t[:, :, None, :])
        return S, jnp.einsum('bhvk,bhk->bhv', S, r_t)

    seq_in = tuple(jnp.moveaxis(t, 1, 0) for t in (r_h, w_h, k_h, v_h, kk, b_h))
    s_fin, y = lax.scan(step, wkv_prev.astype(f32), seq_in)
    y = jnp.moveaxis(y, 0, 1)
    y_mu = jnp.mean(y, axis=-1, keepdims=True)
    y_var = jnp.mean(jnp.square(y - y_mu), axis=-1, keepdims=True)
    y = ((y - y_mu) * lax.rsqrt(y_var + GN_EPS)).reshape(B, L, RWKV_WIDTH)
    y = y * gn_g.astype(f32) + gn_b.astype(f32)
    bonus = jnp.sum(r_h * k_h * r_k.astype(f32), axis=-1, keepdims=True) * v_h
    y = (y + bonus.reshape(B, L, RWKV_WIDTH)) * g
    return y.astype(feat.dtype), feat[:, -1], s_fin.astype(wkv_prev.dtype)

def split_attn(feat):
    B, L, _ = feat.shape
    q, k, v, qi, ki, wi = jnp.split(feat, list(ATTN_SPLITS), axis=-1)
    return (q.reshape(B, L, KV_HEADS, GROUP, HEAD_DIM), k.reshape(B, L, KV_HEADS, HEAD_DIM),
            v.reshape(B, L, KV_HEADS, HEAD_DIM), qi.reshape(B, L, IDX_HEADS, IDX_DIM), ki, wi)

def index_scores(q_idx, w_idx, k_idx):
    f32 = jnp.float32
    rel = jax.nn.relu(jnp.einsum('bqhd,bsd->bqhs', q_idx, k_idx, preferred_element_type=f32))
    return jnp.einsum('bqh,bqhs->bqs', w_idx.astype(f32), rel)

def sparse_attend(q, k_sel, v_sel, q_pos, sel_pos, rel_bias):
    f32 = jnp.float32
    B, Q, K = sel_pos.shape
    dist = q_pos[None, :, None] - sel_pos
    bias = rel_bias[rel_bucket(dist)].astype(f32)
    bias = jnp.moveaxis(bias, 2, -1).reshape(B, Q, KV_HEADS, GROUP, K)
    s = jnp.einsum('bqngd,bqknd->bqngk', q, k_sel, preferred_element_type=f32) * (HEAD_DIM ** -0.5) + bias
    s = jnp.where((dist >= 0)[:, :, None, None, :], s, -jnp.inf)
    p = jax.nn.softmax(s, axis=-1)
    o = jnp.einsum('bqngk,bqknd->bqngd', p.astype(v_sel.dtype), v_sel)
    return o.reshape(B, Q, ATTN_WIDTH)

def prompt_sparse_attention(q, k, v, q_idx, k_idx, w_idx, rel_bias):
    B, T = q.shape[:2]
    nb = T // ATTN_Q_BLOCK
    n_sel = min(IDX_TOPK, T // 4)
    key_pos = jnp.arange(T, dtype=jnp.int32)

    def blocks(t):
        return jnp.moveaxis(t.reshape(B, nb, ATTN_Q_BLOCK, *t.shape[2:]), 1, 0)

    def one_block(args):
        qb, qib, wb, qpos = args
        sc = index_scores(qib, wb, k_idx)
        sc = jnp.where(key_pos[None, None, :] <= qpos[None, :, None], sc, -jnp.inf)
        _, sel = lax.top_k(sc, n_sel)
        return sparse_attend(qb, take_rows(k, sel), take_rows(v, sel), qpos, sel, rel_bias)

    out = lax.map(one_block, (blocks(q), blocks(q_idx), blocks(w_idx), key_pos.reshape(nb, ATTN_Q_BLOCK)))
    return jnp.moveaxis(out, 0, 1).reshape(B, T, ATTN_WIDTH)

def sample_sparse_attention(q, k_new, v_new, q_idx, kidx_new, w_idx, cache_k, cache_v, cache_kidx,
                            page_table, layer, rel_bias):
    Bd, S = q.shape[:2]
    L = PAST_LEN + S
    n_sel = min(IDX_TOPK, L // 4)
    kidx_past = cache_kidx[layer, page_table].reshape(Bd, PAST_LEN, IDX_DIM)
    kidx_all = jnp.concatenate([kidx_past.astype(kidx_new.dtype), kidx_new], axis=1)
    q_pos = PAST_LEN + jnp.arange(S, dtype=jnp.int32)
    key_pos = jnp.arange(L, dtype=jnp.int32)
    sc = index_scores(q_idx, w_idx, kidx_all)
    sc = jnp.where(key_pos[None, None, :] <= q_pos[None, :, None], sc, -jnp.inf)
    _, sel = lax.top_k(sc, n_sel)
    past = jnp.minimum(sel, PAST_LEN - 1)
    phys = jnp.take_along_axis(page_table, (past // PAGE_SIZE).reshape(Bd, -1), axis=1).reshape(sel.shape)
    off = past % PAGE_SIZE
    new = jnp.clip(sel - PAST_LEN, 0, S - 1)
    is_new = (sel >= PAST_LEN)[..., None, None]
    k_sel = jnp.where(is_new, take_rows(k_new, new), cache_k[layer, phys, off].astype(k_new.dtype))
    v_sel = jnp.where(is_new, take_rows(v_new, new), cache_v[layer, phys, off].astype(v_new.dtype))
    return sparse_attend(q, k_sel, v_sel, q_pos, sel, rel_bias)

def peer_ffn(x, wq, subkeys, u_tab, v_tab):
    f32 = jnp.float32
    shp = x.shape
    xf = x.reshape(-1, D_MODEL)
    n = xf.shape[0]
    q = (xf @ wq).astype(f32).reshape(n, PEER_HEADS, 2, PEER_HALF)
    s = jnp.einsum('nhpd,hpkd->nhpk', q, subkeys.astype(f32))
    top_s, top_i = lax.top_k(s, PEER_TOPK)
    cand_s = (top_s[:, :, 0, :, None] + top_s[:, :, 1, None, :]).reshape(n, PEER_HEADS, PEER_TOPK * PEER_TOPK)
    cand_i = (top_i[:, :, 0, :, None] * PEER_NKEYS + top_i[:, :, 1, None, :]).reshape(n, PEER_HEADS, PEER_TOPK * PEER_TOPK)
    best_s, best_j = lax.top_k(cand_s, PEER_TOPK)
    expert = jnp.take_along_axis(cand_i, best_j, axis=-1)
    gate = jax.nn.softmax(best_s, axis=-1)
    n_pad = (-n) % PEER_BLOCK
    nb = (n + n_pad) // PEER_BLOCK

    def pad(t):
        t = jnp.pad(t, [(0, n_pad)] + [(0, 0)] * (t.ndim - 1))
        return t.reshape(nb, PEER_BLOCK, *t.shape[1:])

    def one_block(args):
        xb, eb, gb = args
        h = jax.nn.gelu(jnp.einsum('nd,nhkd->nhk', xb, u_tab[eb], preferred_element_type=f32), approximate=False)
        return jnp.einsum('nhk,nhkd->nd', (gb * h).astype(xb.dtype), v_tab[eb])

    y = lax.map(one_block, (pad(xf), pad(expert), pad(gate)))
    return y.reshape(-1, D_MODEL)[:n].reshape(shp)

def finish_layer(x, y_rwkv, y_attn, w_o, ln1_g, ln1_b, peer_wq, peer_subkeys, peer_u, peer_v, ln2_g, ln2_b):
    mix = jnp.concatenate([y_rwkv, y_attn], axis=-1) @ w_o
    x = layer_norm(DN_ALPHA * x + mix, ln1_g, ln1_b)
    return layer_norm(DN_ALPHA * x + peer_ffn(x, peer_wq, peer_subkeys, peer_u, peer_v), ln2_g, ln2_b)

def setup_inputs(seed: int = 0) -> dict:
    key = jax.random.key(seed)
    keys = list(jax.random.split(key, 48))
    f32 = jnp.float32

    def nrm(shape, scale):
        return jax.random.normal(keys.pop(), shape, f32) * scale

    def unif(shape, lo, hi):
        return jax.random.uniform(keys.pop(), shape, f32, lo, hi)

    n_pages = PAST_LEN // PAGE_SIZE
    used = DEC_BATCH * n_pages
    n_pool = used + max(1, used // 4)
    T = DEPTH
    return {
        'x_prompt': nrm((BATCH, SEQ, D_MODEL), 1.0),
        'x_sample': nrm((DEC_BATCH, DEC_SEQ, D_MODEL), 1.0),
        'cache_k': nrm((T, n_pool, PAGE_SIZE, KV_HEADS, HEAD_DIM), 1.0),
        'cache_v': nrm((T, n_pool, PAGE_SIZE, KV_HEADS, HEAD_DIM), 1.0),
        'cache_kidx': nrm((T, n_pool, PAGE_SIZE, IDX_DIM), 1.0),
        'state_wkv': nrm((T, DEC_BATCH, RWKV_HEADS, HEAD_DIM, HEAD_DIM), 0.5),
        'state_shift': nrm((T, DEC_BATCH, RWKV_COLS), 1.0),
        'page_table': jax.random.permutation(keys.pop(), n_pool)[:used].reshape(DEC_BATCH, n_pages).astype(jnp.int32),
        'meta_tokens': nrm((N_META, D_MODEL), 1.0),
        'ln_in_g': 1.0 + nrm((D_MODEL,), 0.02),
        'ln_in_b': nrm((D_MODEL,), 0.02),
        'rel_bias': nrm((REL_BUCKETS, ATTN_HEADS), 0.5),
        'w_in': nrm((T, D_MODEL, IN_COLS), D_MODEL ** -0.5),
        'mu_shift': unif((T, RWKV_COLS), 0.0, 1.0),
        'w0': unif((T, RWKV_WIDTH), -6.5, -1.5),
        'w_up': nrm((T, DECAY_LORA, RWKV_WIDTH), 0.5 * DECAY_LORA ** -0.5),
        'a0': nrm((T, RWKV_WIDTH), 0.1),
        'a_up': nrm((T, ICLR_LORA, RWKV_WIDTH), 0.5 * ICLR_LORA ** -0.5),
        'g_up': nrm((T, GATE_LORA, RWKV_WIDTH), GATE_LORA ** -0.5),
        'k_k': 0.85 + nrm((T, RWKV_WIDTH), 0.05),
        'k_a': 1.0 + nrm((T, RWKV_WIDTH), 0.05),
        'r_k': nrm((T, RWKV_HEADS, HEAD_DIM), 0.1),
        'gn_g': 1.0 + nrm((T, RWKV_WIDTH), 0.02),
        'gn_b': nrm((T, RWKV_WIDTH), 0.02),
        'w_o': nrm((T, RWKV_WIDTH + ATTN_WIDTH, D_MODEL), DN_BETA * (RWKV_WIDTH + ATTN_WIDTH) ** -0.5),
        'ln1_g': 1.0 + nrm((T, D_MODEL), 0.02),
        'ln1_b': nrm((T, D_MODEL), 0.02),
        'peer_wq': nrm((T, D_MODEL, PEER_HEADS * PEER_QUERY), D_MODEL ** -0.5),
        'peer_subkeys': nrm((T, PEER_HEADS, 2, PEER_NKEYS, PEER_HALF), PEER_HALF ** -0.5),
        'peer_u': nrm((T, PEER_EXPERTS, D_MODEL), D_MODEL ** -0.5),
        'peer_v': nrm((T, PEER_EXPERTS, D_MODEL), DN_BETA * PEER_HEADS ** -0.5),
        'ln2_g': 1.0 + nrm((T, D_MODEL), 0.02),
        'ln2_b': nrm((T, D_MODEL), 0.02),
    }

def reference(x_prompt, x_sample, cache_k, cache_v, cache_kidx, state_wkv, state_shift, page_table,
              meta_tokens, ln_in_g, ln_in_b, rel_bias, w_in, mu_shift, w0, w_up, a0, a_up, g_up,
              k_k, k_a, r_k, gn_g, gn_b, w_o, ln1_g, ln1_b, peer_wq, peer_subkeys, peer_u, peer_v,
              ln2_g, ln2_b):
    B = x_prompt.shape[0]
    meta = jnp.broadcast_to(meta_tokens[None].astype(x_prompt.dtype), (B, N_META, D_MODEL))
    x_p = layer_norm(jnp.concatenate([meta, x_prompt], axis=1), ln_in_g, ln_in_b)
    x_s = layer_norm(x_sample, ln_in_g, ln_in_b)
    nk_p, nv_p, nki_p, nwkv_p, nsh_p = [], [], [], [], []
    nk_s, nv_s, nki_s, nwkv_s, nsh_s = [], [], [], [], []
    for l in range(DEPTH):
        rw = (mu_shift[l], w0[l], w_up[l], a0[l], a_up[l], g_up[l], k_k[l], k_a[l], r_k[l], gn_g[l], gn_b[l])
        fin = (w_o[l], ln1_g[l], ln1_b[l], peer_wq[l], peer_subkeys[l], peer_u[l], peer_v[l], ln2_g[l], ln2_b[l])
        proj = x_p @ w_in[l]
        y_r, sh_p, wkv_p = rwkv7_mix(proj[..., :RWKV_COLS], jnp.zeros((B, RWKV_COLS), proj.dtype),
                                     jnp.zeros((B, RWKV_HEADS, HEAD_DIM, HEAD_DIM), jnp.float32), *rw)
        q, k, v, qi, ki, wi = split_attn(proj[..., RWKV_COLS:])
        y_a = prompt_sparse_attention(q, k, v, qi, ki, wi, rel_bias)
        x_p = finish_layer(x_p, y_r, y_a, *fin)
        nk_p.append(k); nv_p.append(v); nki_p.append(ki); nwkv_p.append(wkv_p); nsh_p.append(sh_p)
        proj = x_s @ w_in[l]
        y_r, sh_s, wkv_s = rwkv7_mix(proj[..., :RWKV_COLS], state_shift[l], state_wkv[l], *rw)
        q, k, v, qi, ki, wi = split_attn(proj[..., RWKV_COLS:])
        y_a = sample_sparse_attention(q, k, v, qi, ki, wi, cache_k, cache_v, cache_kidx, page_table, l, rel_bias)
        x_s = finish_layer(x_s, y_r, y_a, *fin)
        nk_s.append(k); nv_s.append(v); nki_s.append(ki); nwkv_s.append(wkv_s); nsh_s.append(sh_s)
    y_prompt = x_p[:, N_META:]
    return (y_prompt, x_s,
            jnp.stack(nk_p), jnp.stack(nv_p), jnp.stack(nki_p), jnp.stack(nwkv_p), jnp.stack(nsh_p),
            jnp.stack(nk_s), jnp.stack(nv_s), jnp.stack(nki_s), jnp.stack(nwkv_s), jnp.stack(nsh_s))


_drawn_inputs = setup_inputs


def setup_inputs(seed=0):
    import zlib

    import numpy as np

    out = dict(_drawn_inputs(seed))
    spreads = {}
    factors = {'w_up': 2.719,
     'gn_g': 22.505,
     'gn_b': 22.43,
     'ln2_g': 24.265,
     'ln2_b': 23.036,
     'cache_k': 2.848,
     'rel_bias': 4.971,
     'r_k': 4.176}
    for name, (base, spread) in spreads.items():
        noise = np.random.default_rng([zlib.crc32(name.encode()), seed]).standard_normal(out[name].shape)
        drawn = base * np.exp(spread * noise) if base else spread * noise
        out[name] = jnp.asarray(drawn.astype(out[name].dtype))
    for name, factor in factors.items():
        out[name] = (out[name] * factor).astype(out[name].dtype)
    return out
```

```python
from contextlib import ExitStack, contextmanager

import numpy as np
import concourse.bass as bass
from concourse import mybir

F32 = mybir.dt.float32
BF16 = mybir.dt.bfloat16
U32 = mybir.dt.uint32
I32 = mybir.dt.int32
ALU = mybir.AluOpType
ACT = mybir.ActivationFunctionType
AX = mybir.AxisListType.X

P = 128
D = 2048
KT = D // P
META, SEQ = 16, 256
TP = META + SEQ
B, S = 8, 4
TS = B * S
N = TP + TS
PAST, PAGE = 2048, 128
PAGES = PAST // PAGE
HD = 64
RW = 1024
RC = 3 * RW + 64 + 64 + 160
KVH, GROUP = 4, 4
IH, ID = 8, 128
TOPK_P = min(256, TP // 4)
TOPK_S = min(256, (PAST + S) // 4)
NB_BUCKETS, MAX_DIST = 32, 128
PH, NK, EK = 8, 128, 16
ALPHA = 2 ** 0.25
LN_EPS, GN_EPS = 1e-5, 64e-5
DECAY = float(np.exp(-0.5))

C_R, C_K, C_V, C_WA, C_G = 0, 8, 16, 24, 25
RWC = 27
C_Q, C_AK, C_AV, C_QI, C_KI, C_WI = 27, 35, 37, 39, 47, 48
NC_IN = 49

CH = 32
TILES = ((0, 128), (128, 128), (256, 48))
NEG = -1e30
PAD = -1e38
MARK = -3e38


class Ctx:

    def __init__(self, nc):
        self.nc = nc
        self.own = None

    def sem(self, name):
        s = self.own.enter_context(self.nc.semaphore(name))
        self.used.append(s)
        return s

    def count(self, name):
        s = self.sem(name)
        self.counts.append(s)
        return s

    def wait(self, eng, s, value, gate=None):
        assert any(s is c for c in self.counts)
        if gate is None:
            eng.wait_ge(s, value + 1)
        else:
            wait_loop(eng, s, value + 1, gate)

    @contextmanager
    def block(self):
        with self.nc.Block() as block:
            if self.counts:
                @block.gpsimd
                def _(pool):
                    for s in self.counts:
                        pool.sem_inc(s, 1)
            yield block

    def phase(self, build, *args, **kwargs):
        with ExitStack() as own:
            self.own, self.used, self.counts = own, [], []
            build(self, *args, **kwargs)
            used = self.used
            with self.nc.Block() as block:
                @block.sync
                def _(sp):
                    for s in used:
                        sp.sem_clear(s)


def wait_loop(eng, sem, value, gate):
    eng.wait_ge(sem, value)
    eng.sem_inc(gate, 1)


class Link:

    def __init__(self, eng, sem, gate=None):
        self.eng, self.sem, self.n, self.at, self.gate = eng, sem, 0, None, gate

    def value(self):
        return self.n if self.at is None else self.at + self.n

    def __call__(self, ins):
        ins.then_inc(self.sem, 1)
        self.n += 1
        if self.gate and self.at is not None:
            wait_loop(self.eng, self.sem, self.value(), self.gate)
        else:
            self.eng.wait_ge(self.sem, self.value())

    def enter(self, i, per):
        self.start, self.per = self.n, per
        self.at = i * per + self.start
        self.n = 0

    def leave(self, turns):
        assert self.n == self.per, (self.n, self.per)
        self.n, self.at = self.start + turns * self.per, None


def load_all(block_eng, nc, sem, pairs):
    n = 0
    for dst, src in pairs:
        block_eng.dma_start(dst, src).then_inc(sem, 16)
        n += 16
    return n


def load(cx, name, pairs):
    loaded = cx.sem(f"{name}_loaded")
    with cx.nc.Block() as block:
        @block.sync
        def _(sp):
            sp.wait_ge(loaded, load_all(sp, cx.nc, loaded, pairs))


def layer_norm(cx, name, xT, gb, ones, out=None, into=None):
    into = xT if into is None else into
    nc = cx.nc
    with ExitStack() as st:
        sq = st.enter_context(nc.sbuf_tensor(f"{name}_sq", [P, KT, N], F32))
        rs = st.enter_context(nc.sbuf_tensor(f"{name}_rs", [P, 3, N], F32))
        mean = st.enter_context(nc.psum_tensor(f"{name}_mean", [P, 512], F32))
        var = st.enter_context(nc.psum_tensor(f"{name}_var", [P, 512], F32))
        mean_done, centered, squared, var_done = (cx.sem(f"{name}_{x}") for x in
                                                  ("mean_done", "centered", "squared", "var_done"))
        inv_done, rstd_done, link = cx.sem(f"{name}_inv"), cx.sem(f"{name}_rstd"), cx.sem(f"{name}_link")
        stored = cx.sem(f"{name}_stored")
        scaled = cx.sem(f"{name}_scaled")
        with nc.Block() as block:
            @block.tensor
            def _(pe):
                for k in range(KT):
                    mm = pe.matmul(mean[:, 0:N], ones[:], xT[:, k, :], start=k == 0, stop=k == KT - 1)
                mm.then_inc(mean_done, 1)
                for k in range(KT):
                    pe.wait_ge(squared, k // 4 + 1)
                    mm = pe.matmul(var[:, 0:N], ones[:], sq[:, k, :], start=k == 0, stop=k == KT - 1)
                mm.then_inc(var_done, 1)

            @block.vector
            def _(v):
                lk = Link(v, link)
                v.wait_ge(mean_done, 1)
                lk(v.tensor_copy(rs[:, 2, :], mean[:, 0:N]))
                for q in range(4):
                    v.tensor_tensor(xT[:, 4 * q:4 * q + 4, :], xT[:, 4 * q:4 * q + 4, :],
                                    rs[:, 2:3, :].to_broadcast([P, 4, N]), ALU.subtract).then_inc(centered, 1)
                v.wait_ge(var_done, 1)
                lk(v.tensor_scalar(rs[:, 0, :], var[:, 0:N], LN_EPS, None, ALU.add))
                v.reciprocal(rs[:, 0, :], rs[:, 0, :]).then_inc(inv_done, 1)
                v.wait_ge(rstd_done, 1)
                v.wait_ge(centered, 4)
                for k in range(KT):
                    lk(v.scalar_tensor_tensor(xT[:, k, :], xT[:, k, :], gb[:, 0, k:k + 1], rs[:, 1, :],
                                              ALU.mult, ALU.mult))
                    v.tensor_scalar(into[:, k, :], xT[:, k, :], gb[:, 1, k:k + 1], None,
                                    ALU.add).then_inc(scaled, 1)

            @block.scalar
            def _(act):
                for q in range(4):
                    act.wait_ge(centered, q + 1)
                    act.activation(sq[:, 4 * q:4 * q + 4, :], xT[:, 4 * q:4 * q + 4, :],
                                   ACT.Square).then_inc(squared, 1)
                act.wait_ge(inv_done, 1)
                act.activation(rs[:, 1, :], rs[:, 0, :], ACT.Sqrt).then_inc(rstd_done, 1)

            if out is not None:
                @block.sync
                def _(sp):
                    sp.wait_ge(scaled, KT)
                    sp.dma_start(out, into[:]).then_inc(stored, 16)
                    sp.wait_ge(stored, 16)


def project(cx, name, chunks, w_dram, rhsT, evacuate):
    nc = cx.nc
    SL = 4
    turns = -(-chunks // SL)
    with ExitStack() as st:
        w = [st.enter_context(nc.sbuf_tensor(f"{name}_w{s}", [P, KT, P], F32)) for s in range(SL)]
        acc = [st.enter_context(nc.psum_tensor(f"{name}_acc{s}", [P, 512], F32)) for s in range(SL)]
        loaded = [cx.sem(f"{name}_loaded{s}") for s in range(SL)]
        summed = [cx.count(f"{name}_summed{s}") for s in range(SL)]
        emptied = [cx.count(f"{name}_emptied{s}") for s in range(SL)]
        full, rest = chunks // SL, chunks % SL

        def body(one, eng):
            if full:
                with eng.Fori(0, full) as i:
                    for s in range(SL):
                        one(i, s)
            for s in range(rest):
                one(full, s)

        with cx.block() as block:
            @block.sync
            def _(sp):
                def one(i, s):
                    cx.wait(sp, summed[s], i)
                    sp.dma_start(w[s][:], w_dram[i * SL + s]).then_inc(loaded[s], 16)
                body(one, sp)

            @block.tensor
            def _(pe):
                def one(i, s):
                    pe.wait_ge(loaded[s], i * 16 + 16)
                    cx.wait(pe, emptied[s], i)
                    for k in range(KT):
                        mm = pe.matmul(acc[s][:, 0:N], w[s][:, k, :], rhsT[:, k, :],
                                       start=k == 0, stop=k == KT - 1)
                    mm.then_inc(summed[s], 1)
                body(one, pe)

            @block.vector
            def _(v):
                def one(i, s):
                    cx.wait(v, summed[s], i + 1)
                    evacuate(v, i * SL + s, acc[s][:, 0:N]).then_inc(emptied[s], 1)
                body(one, v)


def build(nc, a, o):
    cx = Ctx(nc)
    with ExitStack() as top:
        def sb(name, shape, dt=F32, stack=top):
            return stack.enter_context(nc.sbuf_tensor(name, shape, dt))

        x_rest = nc.dram_tensor("x_rest", [P, KT, N], F32, kind="Internal").ap()
        mixT = sb("mixT", [P, KT, N])
        ones = sb("ones", [P, P])
        ident = sb("ident", [P, P])
        ln_gb = sb("ln_gb", [P, 3, 2, KT])
        with ExitStack() as mixer:
            projT = sb("projT", [P, NC_IN, N], stack=mixer)
            with ExitStack() as early:
                xT = sb("x_inT", [P, KT, N], stack=early)
                cx.phase(load, "first", ((xT[:], a["xT"]), (ones[:], a["ones"]), (ident[:], a["ident"]),
                                   (ln_gb[:], a["ln_gb"])))
                cx.phase(layer_norm, "ln_in", xT, ln_gb[:, 0], ones, out=x_rest)
                cx.phase(project, "in", NC_IN, a["w_in"], xT,
                        lambda v, c, acc: v.tensor_copy(projT[:, c, :], acc))
            cx.phase(store_projection, projT, o)
            rwkv(cx, a, o, projT, mixT, ident)
            attention(cx, a, o, projT, mixT, ident)
        with ExitStack() as late:
            xT = sb("x_midT", [P, KT, N], stack=late)
            cx.phase(load, "rest", ((xT[:], x_rest),))
            cx.phase(project, "out", KT, a["w_o"], mixT,
                    lambda v, c, acc: v.scalar_tensor_tensor(xT[:, c, :], xT[:, c, :], ALPHA, acc,
                                                             ALU.mult, ALU.add))
            cx.phase(layer_norm, "ln1", xT, ln_gb[:, 1], ones, into=mixT)
        xT = mixT
        peer(cx, a, xT, ident)
        cx.phase(layer_norm, "ln2", xT, ln_gb[:, 2], ones, out=o["yT"])


def store_projection(cx, projT, o):
    nc = cx.nc
    with ExitStack() as st:
        last = st.enter_context(nc.sbuf_tensor("last_rows", [P, RWC, B + 1], F32))
        picked, stored = cx.sem("last_rows_picked"), cx.sem("projection_stored")
        with nc.Block() as block:
            @block.vector
            def _(v):
                v.tensor_copy(last[:], projT[:, 0:RWC, TP - 1:N:S]).then_inc(picked, 1)

            @block.sync
            def _(sp):
                sp.dma_start(o["kvT"], projT[:, C_AK:C_QI, :]).then_inc(stored, 16)
                sp.dma_start(o["kiT"], projT[:, C_KI, :]).then_inc(stored, 16)
                sp.wait_ge(picked, 1)
                sp.dma_start(o["shiftT"], last[:]).then_inc(stored, 16)
                sp.wait_ge(stored, 48)


def block_mask(seq):
    return (seq[:, None] == seq[None, :]).astype(np.float32)


def rwkv_masks():
    main = np.arange(P) // CH
    tail = np.concatenate([np.zeros(CH // 2), 10 + np.arange(TS) // S, 100 + np.arange(P - CH // 2 - TS)])
    whole = np.stack([block_mask(main), block_mask(main), block_mask(tail)])
    half = np.stack([block_mask(np.arange(P) // (CH // 2))] * 2 + [block_mask(tail)])
    s, t = np.arange(P)[:, None], np.arange(P)[None, :]
    which = [-half * (s < t), -half * (s > t), (whole - half) * (s < t), whole * (s < t), whole * (s <= t)]
    return np.stack(which).transpose(2, 0, 1, 3).astype(np.float32)


M_XT, M_X, M_OFF, M_LT, M_LE = range(5)

def rwkv_features(cx, a, projT, masks, seqmask, halves, cols, mu, shift, lw, la, ag, gg):
    nc = cx.nc
    NH = 8
    loaded, mixed, squashed, up_done, up_read = (cx.sem(f"rw_{x}") for x in
                                                 ("loaded", "mixed", "squashed", "up_done", "up_read"))
    link0 = cx.sem("rw_link0")

    def shifted(v, lk, out, feat, c0, nch):
        lk(v.tensor_tensor(out[:, :, 1:N], feat[:, :, 0:N - 1], feat[:, :, 1:N], ALU.subtract))
        lk(v.tensor_scalar(out[:, :, 0:1], feat[:, :, 0:1], -1.0, None, ALU.mult))
        lk(v.tensor_tensor(out[:, :, TP:N:S], shift[:, c0:c0 + nch, :], feat[:, :, TP:N:S], ALU.subtract))

    with ExitStack() as ps:
        def early(name, shape):
            return ps.enter_context(nc.sbuf_tensor(f"rw_{name}", shape, F32))

        w_up, g_up, g_up2 = early("w_up", [P, RW]), early("g_up", [P, RW]), early("g_up2", [32, RW])
        xl, dl = early("xl", [P, 3, N]), early("dl", [P, 3, N])
        lb = early("lb", [P, NH, N])
        block = ps.enter_context(nc.Block())
        up = [ps.enter_context(nc.psum_tensor(f"rw_up{i}", [P, 512], F32)) for i in range(2)]

        @block.sync
        def _(sp):
            n = load_all(sp, nc, loaded, (
                (masks[:], a["rw_masks"]), (seqmask[:], a["seqmask"]), (halves[:], a["halves"]),
                (cols[:], a["rw_cols"]), (mu[:], a["mu"]), (shift[:], a["shiftT_in"]),
                (w_up[:], a["wa_up"]), (g_up[:], a["g_up"][0:P]), (g_up2[:], a["g_up"][P:P + 32])))
            assert n == 144

        @block.vector
        def _(v):
            lk = Link(v, link0)
            v.wait_ge(loaded, 144)
            shifted(v, lk, dl, projT[:, C_WA:RWC, :], C_WA, 3)
            for c in range(3):
                v.scalar_tensor_tensor(xl[:, c, :], dl[:, c, :], mu[:, C_WA + c:C_WA + c + 1],
                                       projT[:, C_WA + c, :], ALU.mult, ALU.add).then_inc(mixed, 1)
            v.wait_ge(up_read, 3 * NH)
            lk(v.tensor_scalar(lw[:], lw[:], -DECAY, None, ALU.mult))
            src, dst = lw, la
            main = lambda q: q[:, :, 0:256].rearrange("p j (c t) -> p (j c) t", t=CH)
            for level, step in enumerate((1, 2, 4, 8, 16)):
                parts = []
                for j in range(NH):
                    parts.append((lambda q, j=j: q[:, j, 0:256].rearrange("p (c t) -> p c t", t=CH)))
                if step < 16:
                    parts.append(lambda q: q[:, :, 256:TP])
                if step < 4:
                    for j in range(NH):
                        parts.append((lambda q, j=j: q[:, j, TP:N].rearrange("p (c t) -> p c t", t=S)))
                lk(v.tensor_copy(dst[:], src[:]))
                for part in parts:
                    a_, b_ = part(dst), part(src)
                    lk(v.tensor_tensor(a_[:, :, step:], b_[:, :, step:], b_[:, :, :a_.shape[2] - step], ALU.add))
                src, dst = dst, (lb if dst is la else la)
            assert src is la

        @block.scalar
        def _(act):
            act.wait_ge(mixed, 3)
            act.activation(xl[0:HD, 0, :], xl[0:HD, 0, :], ACT.Tanh).then_inc(squashed, 1)
            act.activation(xl[:, 1, :], xl[:, 1, :], ACT.Sigmoid).then_inc(squashed, 1)
            act.activation(xl[0:32, 2, :], xl[0:32, 2, :], ACT.Sigmoid).then_inc(squashed, 1)
            for j in range(NH):
                for n, (dst, bias) in enumerate(((lw, 6), (ag, 7), (gg, None))):
                    u = 3 * j + n
                    act.wait_ge(up_done, u + 1)
                    if bias is None:
                        ins = act.activation(dst[:, j, :], up[u % 2][:, 0:N], ACT.Copy)
                    else:
                        ins = act.activation(dst[:, j, :], up[u % 2][:, 0:N], ACT.Sigmoid,
                                             bias=cols[:, j, bias:bias + 1])
                    ins.then_inc(up_read, 1)

        @block.tensor
        def _(pe):
            pe.wait_ge(loaded, 144)
            pe.wait_ge(squashed, 3)
            for j in range(NH):
                c = slice(j * P, j * P + P)
                for n in range(3):
                    u = 3 * j + n
                    if u >= 2:
                        pe.wait_ge(up_read, u - 1)
                    if n == 0:
                        mm = pe.matmul(up[u % 2][:, 0:N], w_up[0:HD, c], xl[0:HD, 0, :], start=True, stop=True)
                    elif n == 1:
                        mm = pe.matmul(up[u % 2][:, 0:N], w_up[HD:P, c], xl[HD:P, 0, :], start=True, stop=True)
                    else:
                        pe.matmul(up[u % 2][:, 0:N], g_up[:, c], xl[:, 1, :], start=True, stop=False)
                        mm = pe.matmul(up[u % 2][:, 0:N], g_up2[:, c], xl[0:32, 2, :], start=False, stop=True)
                    mm.then_inc(up_done, 1)


def rwkv(cx, a, o, projT, mixT, ident):
    nc = cx.nc
    NH = 8
    with ExitStack() as st:
        def sb(name, shape, dt=F32):
            return st.enter_context(nc.sbuf_tensor(f"rw_{name}", shape, dt))

        masks = sb("masks", [P, 5, 3, P])
        seqmask = sb("seqmask", [P, B])
        halves = sb("halves", [P, P])
        cols = sb("cols", [P, 8, 10])
        mu = sb("mu", [P, RWC])
        shift = sb("shift", [P, RWC, B])
        lw, ag, gg = sb("lw", [P, NH, N]), sb("ag", [P, NH, N]), sb("gg", [P, NH, N])
        la = sb("la", [P, NH, N])
        cx.phase(rwkv_features, a, projT, masks, seqmask, halves, cols, mu, shift, lw, la, ag, gg)
        cx.phase(rwkv_heads, a, o, projT, mixT, ident, masks, seqmask, halves, cols, shift, lw, la, ag)
        cx.phase(rwkv_finish, mixT, halves, cols, gg)


def rwkv_heads(cx, a, o, projT, mixT, ident, masks, seqmask, halves, cols, shift, lw, la, ag):
    nc = cx.nc
    NH = 8
    N3 = 3 * P
    pe_names = ["norms", "pairs", "lk", "x2", "x4", "x8", "rowsa", "t8", "rowsb", "pre", "a1", "z2", "wu", "mix",
                "g"] + [f"state{c}" for c in range(9)] + ["samples"]
    dv_names = ["products", "features", "x", "lk", "x2", "x4", "t2", "x8", "t3", "rowsa", "rowsb", "kl", "a1",
                "z2", "wu", "mix", "g"] + [f"state{c}" for c in range(9)] + ["samples"]
    ac_names = ["roots", "exps"]
    with ExitStack() as st:
        def sb(name, shape, dt=F32):
            return st.enter_context(nc.sbuf_tensor(f"rh_{name}", shape, dt))

        df = sb("df", [P, 3, N])
        rkv = sb("rkv", [P, 3, N3])
        xx = sb("xx", [P, 2, N])
        kk, kh, bh = sb("kk", [P, N]), sb("kh", [P, N]), sb("bh", [P, N])
        lbef = sb("lbef", [P, N])
        dec, decb, inv = sb("dec", [P, N]), sb("decb", [P, N]), sb("inv", [P, N])
        KT_, RT_, kT_, bT_ = sb("K", [P, N3]), sb("R", [P, N3]), sb("k", [P, N3]), sb("b", [P, N3])
        cs = sb("colsj", [P, 10])
        arena = sb("arena", [P, 11, 6 * P])
        X, XT, X4, WU, X4T, X2, X2T, T0, T1, OFF, LkT = (
            arena[:, n, :].rearrange("p (h t c) -> p h t c", h=2, t=3) for n in range(11))
        MkT, MbT = X, XT
        WU = arena[:, 3, :].rearrange("p (t a c) -> p t a c", t=3, a=2)
        late = arena[:].rearrange("p n c -> p (n c)")[:, 4 * 6 * P:]
        rows = sb("rows", [P, 4, 3, P])
        KL, A1 = X2, X2T
        QT = sb("QT", [P, N3])
        G = late[:, 0:9 * P].rearrange("p (c d) -> p c d", d=P)
        GS, bx, vx, ux = (late[:, (9 + 8 * n) * P:(17 + 8 * n) * P].rearrange("p (b d) -> p b d", d=P)
                          for n in range(4))
        state = sb("state", [P, 10, P])
        ss_in, ss_out = sb("ss_in", [P, B, P]), sb("ss_out", [P, B, P])
        twice = lambda name: st.enter_context(nc.psum_tensor(f"rh_{name}", [P, 2, 512], F32))
        once = lambda name: st.enter_context(nc.psum_tensor(f"rh_{name}", [P, 512], F32))
        pA, pB, pC, pY, pS = twice("pA"), twice("pB"), twice("pC"), once("pY"), once("pS")
        flat = lambda bank: bank[:].rearrange("p a c -> p (a c)")
        mats = lambda bank: bank[:, :, 0:3 * P].rearrange("p h (t c) -> p h t c", t=3)
        mat = lambda bank, t, h: bank[:, h, t * P:t * P + P]
        mask = lambda which: masks[:, which:which + 1, :, :].to_broadcast([P, 2, 3, P])
        pe_step, dv_step, ac_step = cx.sem("rh_pe_step"), cx.sem("rh_dve_step"), cx.sem("rh_act_step")
        link, gate = cx.sem("rh_link"), cx.sem("rh_gate")
        ss_loaded, stored = cx.sem("rh_ss_loaded"), cx.sem("rh_stored")

        def at(names, i, name):
            return i * len(names) + names.index(name) + 1

        def stepper(sem, names):
            left = list(names)

            def done(ins, name):
                assert left.pop(0) == name, name
                ins.then_inc(sem, 1)
            return done, left

        halves_of = [(0, slice(0, HD)), (1, slice(HD, P))]
        tiles = range(3)

        def chunk_rows(c):
            n = CH if c < 8 else CH // 2
            return slice(c * CH, c * CH + n), c // 4, slice((c % 4) * CH, (c % 4) * CH + n)

        with nc.Block() as block:
            @block.tensor
            def _(pe):
                with pe.Fori(0, NH) as i:
                    done, left = stepper(pe_step, pe_names)
                    need = lambda name: pe.wait_ge(dv_step, at(dv_names, i, name))

                    def every(bank, lhs, rhs):
                        for t in tiles:
                            for h, r in halves_of:
                                mm = pe.matmul(mat(bank, t, h), lhs(t, h, r), rhs(t, h, r), start=True, stop=True)
                        return mm

                    feat = lambda q: (lambda t, h, r: q[r, t * P:t * P + P])
                    sq = lambda q: (lambda t, h, r: q[:, h, t, :])
                    need("products")
                    pe.matmul(pY[:, 0:N], halves[:], xx[:, 0, :], start=True, stop=True)
                    done(pe.matmul(pS[:, 0:N], halves[:], xx[:, 1, :], start=True, stop=True), "norms")
                    need("features")
                    every(pA, feat(bT_), feat(KT_))
                    done(every(pB, feat(KT_), feat(bT_)), "pairs")
                    done(every(pC, feat(kT_), feat(KT_)), "lk")
                    need("x")
                    every(pA, sq(XT), sq(X))
                    done(every(pB, sq(X), sq(XT)), "x2")
                    need("x2")
                    every(pA, sq(X2T), sq(X2))
                    every(pB, sq(X2), sq(X2T))
                    done(every(pC, sq(X2), sq(T0)), "x4")
                    need("x4")
                    need("t2")
                    every(pA, sq(X4T), sq(X4))
                    done(every(pC, sq(X4), sq(T1)), "x8")
                    for n, src in enumerate((KT_, kT_)):
                        for t in tiles:
                            at_ = (n * 3 + t) * P
                            mm = pe.transpose(pB[:, at_ // 512, at_ % 512:at_ % 512 + P], src[:, t * P:t * P + P],
                                              ident[:])
                    done(mm, "rowsa")
                    need("x8")
                    done(every(pC, sq(X2), sq(T0)), "t8")
                    need("rowsa")
                    for n, src in enumerate((bT_, rkv[:, 2, :])):
                        for t in tiles:
                            at_ = (n * 3 + t) * P
                            mm = pe.transpose(pB[:, at_ // 512, at_ % 512:at_ % 512 + P], src[:, t * P:t * P + P],
                                              ident[:])
                    done(mm, "rowsb")
                    need("rowsb")
                    for t in tiles:
                        for h, r in halves_of:
                            mm = pe.matmul(mat(pA, t, h)[:, 0:HD], LkT[:, h, t, :], rows[:, 3, t, r],
                                           start=True, stop=True)
                    done(mm, "pre")
                    need("t3")
                    need("kl")
                    done(every(pB, sq(T1), sq(KL)), "a1")
                    need("a1")
                    done(every(pA, sq(OFF), sq(A1)), "z2")
                    need("z2")
                    done(every(pB, sq(T1), sq(KL)), "wu")
                    every(pC, feat(kT_), feat(RT_))
                    done(every(pA, feat(bT_), feat(RT_)), "mix")
                    need("wu")
                    need("mix")
                    for h, r in halves_of:
                        for t in tiles:
                            pe.matmul(pS[r, t * P:t * P + P], WU[:, t, 0, r], MbT[:, h, t, :],
                                      start=t == 0, stop=True, skip_group_check=True)
                            pe.matmul(pY[r, t * P:t * P + P], rows[:, 3, t, r], MkT[:, h, t, :],
                                      start=t == 0, stop=False, skip_group_check=True)
                            pe.matmul(pY[r, t * P:t * P + P], WU[:, t, 1, r], MbT[:, h, t, :],
                                      start=False, stop=False, skip_group_check=True)
                    gbank = (pB[:, 0], pB[:, 1], pC[:, 0], pC[:, 1])
                    for c in range(9):
                        _, t, cr = chunk_rows(c)
                        pe.matmul(gbank[c % 4][:, (c // 4) * P:(c // 4) * P + P], WU[cr, t, 0, :],
                                  rows[cr, 2, t, :], start=True, stop=True)
                    for q in range(2):
                        mm = pe.matmul(pA[:, q, :], WU[:, 2, 0, :], bx[:, 4 * q:4 * q + 4, :].rearrange("p b d -> p (b d)"),
                                       start=True, stop=True)
                    done(mm, "g")
                    need("g")
                    for c in range(9):
                        toks, t, cr = chunk_rows(c)
                        if c:
                            need(f"state{c - 1}")
                        q = pS[:, 0:P]
                        pe.matmul(q, rows[cr, 1, t, :], rows[cr, 3, t, :], start=True, stop=False)
                        pe.matmul(q, rows[cr, 2, t, :], WU[cr, t, 1, :], start=False, stop=False)
                        pe.matmul(q, G[:, c, :], state[:, c, :], start=False, stop=True)
                        done(pe.matmul(pY[:, toks], state[:, c, :], QT[:, toks], start=False, stop=True,
                                       skip_group_check=True), f"state{c}")
                    pe.wait_ge(ss_loaded, i * 16 + 16)
                    for q in range(2):
                        four = lambda x: x[:, 4 * q:4 * q + 4, :].rearrange("p b d -> p (b d)")
                        pe.matmul(pC[:, q, :], rows[:, 1, 2, :], four(vx), start=True, stop=False,
                                  skip_group_check=True)
                        pe.matmul(pC[:, q, :], rows[:, 2, 2, :], four(ux), start=False, stop=False,
                                  skip_group_check=True)
                    for b in range(B):
                        toks = slice(TP + b * S, TP + b * S + S)
                        pe.matmul(pC[:, b // 4, (b % 4) * P:(b % 4) * P + P], GS[:, b, :], ss_in[:, b, :],
                                  start=False, stop=True, skip_group_check=True)
                        mm = pe.matmul(pY[:, toks], ss_in[:, b, :], QT[:, toks], start=False, stop=True,
                                       skip_group_check=True)
                    done(mm, "samples")
                    assert not left

            @block.scalar
            def _(act):
                with act.Fori(0, NH) as i:
                    done, left = stepper(ac_step, ac_names)
                    act.wait_ge(pe_step, at(pe_names, i, "norms"))
                    done(act.activation(bh[:], pY[:, 0:N], ACT.Sqrt), "roots")
                    act.wait_ge(dv_step, at(dv_names, i, "products"))
                    act.activation(dec[:], la[:, i, :], ACT.Exp)
                    act.activation(inv[:], la[:, i, :], ACT.Exp, scale=-1.0)
                    done(act.activation(decb[:], lbef[:], ACT.Exp), "exps")

            @block.vector
            def _(v):
                lk = Link(v, link)
                for q in (KT_, RT_, kT_, bT_):
                    lk(v.memset(q[:, N:N3], 0.0))
                lk(v.memset(rkv[:, :, N:N3], 0.0))
                lk(v.memset(state[:, 0, :], 0.0))
                proj3 = projT[:, 0:24, :].rearrange("p (a j) n -> p a j n", j=NH)
                shift3 = shift[:, 0:24, :].rearrange("p (a j) b -> p a j b", j=NH)
                with v.Fori(0, NH) as i:
                    lk.enter(i, LINKS_RW)
                    signal, left = stepper(dv_step, dv_names)

                    def done(ins, name):
                        signal(ins, name)
                        own(name)
                    own = lambda name: v.wait_ge(dv_step, at(dv_names, i, name))
                    need = lambda name: v.wait_ge(pe_step, at(pe_names, i, name))
                    f = proj3[:, :, i, :]
                    lk(v.tensor_copy(cs[:], cols[:, i, :]))
                    lk(v.tensor_tensor(df[:, :, 1:N], f[:, :, 0:N - 1], f[:, :, 1:N], ALU.subtract))
                    lk(v.tensor_scalar(df[:, :, 0:1], f[:, :, 0:1], -1.0, None, ALU.mult))
                    lk(v.tensor_tensor(df[:, :, TP:N:S], shift3[:, :, i, :], f[:, :, TP:N:S], ALU.subtract))
                    for n in range(3):
                        lk(v.scalar_tensor_tensor(rkv[:, n, 0:N], df[:, n, :], cs[:, n:n + 1], f[:, n, :],
                                                  ALU.mult, ALU.add))
                    r_, k_, v_ = (rkv[:, n, 0:N] for n in range(3))
                    lk(v.tensor_tensor(lbef[:], la[:, i, :], lw[:, i, :], ALU.subtract))
                    lk(v.tensor_scalar(kk[:], k_, cs[:, 3:4], None, ALU.mult))
                    lk(v.tensor_tensor(xx[:, 0, :], kk[:], kk[:], ALU.mult))
                    lk(v.tensor_scalar(kh[:], ag[:, i, :], -1.0, cs[:, 4:5], ALU.add, ALU.mult))
                    lk(v.scalar_tensor_tensor(kh[:], kh[:], 1.0, k_, ALU.add, ALU.mult))
                    done(v.scalar_tensor_tensor(xx[:, 1, :], r_, cs[:, 5:6], kh[:], ALU.mult, ALU.mult), "products")
                    v.wait_ge(ac_step, at(ac_names, i, "exps"))
                    lk(v.tensor_scalar(bh[:], bh[:], 1e-12, None, ALU.max))
                    lk(v.reciprocal(bh[:], bh[:]))
                    lk(v.tensor_tensor(kk[:], kk[:], bh[:], ALU.mult))
                    lk(v.tensor_tensor(mixT[:, 8 + i, :], v_, pS[:, 0:N], ALU.mult))
                    lk(v.tensor_tensor(KT_[:, 0:N], kk[:], decb[:], ALU.mult))
                    lk(v.tensor_tensor(bh[:], kk[:], ag[:, i, :], ALU.mult))
                    lk(v.tensor_tensor(RT_[:, 0:N], r_, dec[:], ALU.mult))
                    lk(v.tensor_tensor(kT_[:, 0:N], kh[:], inv[:], ALU.mult))
                    done(v.tensor_tensor(bT_[:, 0:N], bh[:], inv[:], ALU.mult), "features")
                    need("pairs")
                    lk(v.tensor_tensor(XT[:], mats(pA), mask(M_XT), ALU.mult))
                    lk(v.tensor_tensor(OFF[:], mats(pA), mask(M_OFF), ALU.mult))
                    lk(v.tensor_tensor(T0[:], XT[:], ident[:].rearrange("p (a b c) -> p a b c", a=1, b=1)
                                       .to_broadcast([P, 2, 3, P]), ALU.add))
                    done(v.tensor_tensor(X[:], mats(pB), mask(M_X), ALU.mult), "x")
                    need("lk")
                    done(v.tensor_tensor(LkT[:], mats(pC), mask(M_LT), ALU.mult), "lk")
                    need("x2")
                    lk(v.tensor_copy(X2[:], mats(pA)))
                    done(v.tensor_copy(X2T[:], mats(pB)), "x2")
                    need("x4")
                    lk(v.tensor_copy(X4[:], mats(pA)))
                    done(v.tensor_copy(X4T[:], mats(pB)), "x4")
                    done(v.tensor_tensor(T1[:], T0[:], mats(pC), ALU.add), "t2")
                    need("x8")
                    lk(v.tensor_copy(X2[:], mats(pA)))
                    done(v.tensor_tensor(T0[:], T1[:], mats(pC), ALU.add), "x8")
                    need("t8")
                    done(v.tensor_tensor(T1[:], T0[:], mats(pC), ALU.add), "t3")
                    need("rowsa")
                    both = flat(pB)[:, 0:6 * P].rearrange("p (n t c) -> p n t c", n=2, t=3)
                    done(v.tensor_copy(rows[:, 0:2], both), "rowsa")
                    need("rowsb")
                    done(v.tensor_copy(rows[:, 2:4], both), "rowsb")
                    need("pre")
                    lk(v.tensor_copy(KL[:, :, :, 0:HD], rows[:, 0].rearrange("p t (h c) -> p h t c", h=2)))
                    done(v.tensor_copy(KL[:, :, :, HD:P], mats(pA)[:, :, :, 0:HD]), "kl")
                    need("a1")
                    done(v.tensor_copy(A1[:], mats(pB)), "a1")
                    need("z2")
                    done(v.tensor_tensor(KL[:], KL[:], mats(pA), ALU.subtract), "z2")
                    need("wu")
                    w4 = WU.rearrange("p t a (h d) -> p a h t d", h=2)
                    lk(v.tensor_scalar(w4[:, 0], mats(pB)[:, :, :, 0:HD], -1.0, None, ALU.mult))
                    done(v.tensor_scalar(w4[:, 1], mats(pB)[:, :, :, HD:P], -1.0, None, ALU.mult), "wu")
                    need("mix")
                    lk(v.tensor_tensor(MkT[:], mats(pC), mask(M_LE), ALU.mult))
                    seq = seqmask[:].rearrange("p (b o) -> p b o", o=1).to_broadcast([P, B, P])
                    for dst, src in ((bx, rows[:, 2, 2:3, :]), (vx, rows[:, 3, 2:3, :]), (ux, WU[:, 2:3, 1, :])):
                        lk(v.tensor_tensor(dst[:], src.to_broadcast([P, B, P]), seq, ALU.mult))
                    done(v.tensor_tensor(MbT[:], mats(pA), mask(M_LE), ALU.mult), "mix")
                    need("g")
                    lk(v.tensor_tensor(QT[:], RT_[:], pS[:, 0:N3], ALU.add))
                    one = ident[:].rearrange("p (o d) -> p o d", o=1)
                    for q, bank in enumerate((pB[:, 0], pB[:, 1], pC[:, 0], pC[:, 1])):
                        n = 3 if q == 0 else 2
                        lk(v.tensor_tensor(G[:, q:9:4, :], bank[:, 0:n * P].rearrange("p (c d) -> p c d", d=P),
                                           one.to_broadcast([P, n, P]), ALU.add))
                    done(v.tensor_tensor(GS[:], pA[:].rearrange("p a (c d) -> p (a c) d", d=P),
                                         one.to_broadcast([P, B, P]), ALU.add), "g")
                    for c in range(9):
                        toks, _, _ = chunk_rows(c)
                        need(f"state{c}")
                        done(v.scalar_tensor_tensor(state[:, c + 1, :], pS[:, 0:P], dec[:, toks.stop - 1:toks.stop],
                                                    halves[:], ALU.mult, ALU.mult), f"state{c}")
                    need("samples")
                    lk(v.tensor_tensor(ss_out[:], pC[:].rearrange("p a (c d) -> p (a c) d", d=P),
                                       dec[:, TP + S - 1:N:S].rearrange("p (b o) -> p b o", o=1)
                                       .to_broadcast([P, B, P]), ALU.mult))
                    done(v.tensor_copy(mixT[:, i, :], pY[:, 0:N]), "samples")
                    assert not left
                    v.wait_ge(stored, i * 64 + 64)
                    lk.leave(NH)

            @block.sync
            def _(sp):
                with sp.Fori(0, NH) as i:
                    sp.dma_start(ss_in[:], a["wkvT"][i]).then_inc(ss_loaded, 16)
                    sp.wait_ge(dv_step, at(dv_names, i, "samples"))
                    for h, r in halves_of:
                        sp.dma_start(o["wkvT_s"][i, r], ss_out[r, :, r]).then_inc(stored, 16)
                        sp.dma_start(o["wkvT_p"][i, r], state[r, 9, r]).then_inc(stored, 16)
                    wait_loop(sp, stored, i * 64 + 64, gate)


LINKS_RW = 38


def rwkv_finish(cx, mixT, halves, cols, gg):
    nc = cx.nc
    with ExitStack() as st:
        sq = st.enter_context(nc.sbuf_tensor("rf_sq", [P, 2, N], F32))
        rs = st.enter_context(nc.sbuf_tensor("rf_rs", [P, 2, N], F32))
        pm = [st.enter_context(nc.psum_tensor(f"rf_m{k}", [P, 512], F32)) for k in range(2)]
        pv = [st.enter_context(nc.psum_tensor(f"rf_v{k}", [P, 512], F32)) for k in range(2)]
        mean, squared, var, inv, root, link, centered = (cx.sem(f"rf_{q}") for q in
            ("mean", "squared", "var", "inv", "root", "link", "centered"))
        with nc.Block() as block:
            @block.tensor
            def _(pe):
                for j in range(8):
                    if j >= 2:
                        pe.wait_ge(centered, j - 1)
                    pe.matmul(pm[j % 2][:, 0:N], halves[:], mixT[:, j, :], start=True, stop=True).then_inc(mean, 1)
                    pe.wait_ge(squared, j + 1)
                    if j >= 2:
                        pe.wait_ge(inv, j - 1)
                    pe.matmul(pv[j % 2][:, 0:N], halves[:], sq[:, j % 2, :], start=True, stop=True).then_inc(var, 1)

            @block.vector
            def _(v):
                lk = Link(v, link)
                for j in range(8):
                    y = mixT[:, j, :]
                    v.wait_ge(mean, j + 1)
                    v.scalar_tensor_tensor(y, pm[j % 2][:, 0:N], -1.0 / HD, y, ALU.mult, ALU.add).then_inc(centered, 1)
                    v.wait_ge(var, j + 1)
                    lk(v.tensor_scalar(rs[:, 0, :], pv[j % 2][:, 0:N], 1.0 / HD, GN_EPS, ALU.mult, ALU.add))
                    v.reciprocal(rs[:, 0, :], rs[:, 0, :]).then_inc(inv, 1)
                    v.wait_ge(root, j + 1)
                    lk(v.scalar_tensor_tensor(y, y, cols[:, j, 8:9], rs[:, 1, :], ALU.mult, ALU.mult))
                    lk(v.scalar_tensor_tensor(y, y, cols[:, j, 9:10], mixT[:, 8 + j, :], ALU.add, ALU.add))
                    lk(v.tensor_tensor(y, y, gg[:, j, :], ALU.mult))

            @block.scalar
            def _(act):
                for j in range(8):
                    act.wait_ge(centered, j + 1)
                    act.activation(sq[:, j % 2, :], mixT[:, j, :], ACT.Square).then_inc(squared, 1)
                    act.wait_ge(inv, j + 1)
                    act.activation(rs[:, 1, :], rs[:, 0, :], ACT.Sqrt).then_inc(root, 1)


FAR = PAST - PAGE
QT_TILES = ((0, 128), (128, 128), (256, 16))
SCORE_COLS = 480
WORK_S = PAST + S + 8


def bucket(dist):
    exact = NB_BUCKETS // 2
    d = np.maximum(dist, 0)
    far = exact + (np.log(np.maximum(d, 1).astype(np.float32) / exact) / np.log(MAX_DIST / exact)
                   * (NB_BUCKETS - exact)).astype(np.int32)
    return np.where(d < exact, d, np.minimum(far, NB_BUCKETS - 1))


def attention(cx, a, o, projT, mixT, ident):
    nc = cx.nc
    bias_rows = nc.dram_tensor("bias_rows", [16, 2 * TP], F32, kind="Internal").ap()
    with ExitStack() as st:
        def sb(name, shape, dt=F32):
            return st.enter_context(nc.sbuf_tensor(f"at_{name}", shape, dt))

        wrow = sb("wrow", [P, 3, IH])
        wsel = sb("wsel", [TS, B, TS])
        vrows = sb("vrows", [P, 3, 2 * P])
        vnew = sb("vnew", [S, B, 2 * P])
        mask_p = sb("mask_p", [P, 3, TP])
        mask_s = sb("mask_s", [TS + 1, PAST + S])
        sel = sb("sel", [TS + 1, B, 64])
        near = sb("near", [P, 64])
        rel = sb("rel", [P, 16])
        onehot = sb("onehot", [P, PAGE + S])
        cx.phase(attention_tables, a, projT, ident, bias_rows, wrow, wsel, vrows, vnew, sel, near, rel, onehot)
        cx.phase(index_prompt, a, projT, wrow, mask_p)
        cx.phase(attend_prompt, a, projT, mixT, ident, mask_p, vrows, bias_rows)
        cx.phase(index_sampled, a, projT, wsel, mask_s)
        cx.phase(attend_sampled, a, projT, mixT, ident, mask_s, sel, near, onehot, vnew)


def attention_tables(cx, a, projT, ident, bias_rows, wrow, wsel, vrows, vnew, sel, near, rel, onehot):
    nc = cx.nc
    with ExitStack() as st:
        def sb(name, shape, dt=F32):
            return st.enter_context(nc.sbuf_tensor(f"tb_{name}", shape, dt))

        pv = st.enter_context(nc.psum_tensor("tb_pv", [P, 2, 512], F32))
        pn = st.enter_context(nc.psum_tensor("tb_pn", [P, 4, 512], F32))
        pw = st.enter_context(nc.psum_tensor("tb_pw", [P, 512], F32))
        pr = st.enter_context(nc.psum_tensor("tb_pr", [P, 512], F32))
        spread = sb("spread", [IH, TS])
        wpick = sb("wpick", [TS, B, TS])
        spick = sb("spick", [P, 16, S])
        table = sb("table", [NB_BUCKETS, 2 * TP])
        brow = sb("brow", [16, 2 * TP])
        far = sb("far", [TS + 1, 16])
        loaded, turned, biased, moved, brow_done, stored = (cx.sem(f"tb_{x}") for x in
                                                    ("loaded", "turned", "biased", "moved", "brow", "stored"))
        with nc.Block() as block:
            @block.sync
            def _(sp):
                rb = a["rel_bias"]
                n = load_all(sp, nc, loaded, (
                    (spread[:], a["spread"]), (wpick[:], a["wpick"]), (spick[:], a["spick"]),
                    (table[:], a["bucket_table"]), (sel[0:TS], a["sel"]), (onehot[:], a["near_onehot"]),
                    (far[TS:TS + 1, :], rb[NB_BUCKETS - 1:NB_BUCKETS, :]),
                    *((rel[s * 32:s * 32 + 32, :], rb) for s in range(S))))
                assert n == 176
                sp.wait_ge(brow_done, 2)
                sp.dma_start(bias_rows, brow[:]).then_inc(stored, 16)
                sp.wait_ge(stored, 16)

            @block.tensor
            def _(pe):
                pe.wait_ge(loaded, 176)
                for t, (t0, m) in enumerate(QT_TILES):
                    pe.transpose(pw[0:m, t * 8:t * 8 + 8], projT[0:IH, C_WI, t0:t0 + m], ident[0:IH, 0:IH])
                pe.matmul(pw[0:TS, 64:64 + TS], spread[:], projT[0:IH, C_WI, TP:N], start=True, stop=True)
                for t, (t0, m) in enumerate(QT_TILES):
                    for p in range(2):
                        q = (2 * t + p) * P
                        pe.transpose(pv[0:m, q // 512, q % 512:q % 512 + P], projT[:, C_AV + p, t0:t0 + m], ident[:])
                for b in range(B):
                    for p in range(2):
                        q = (2 * b + p) * P
                        mm = pe.transpose(pn[0:S, q // 512, q % 512:q % 512 + P],
                                          projT[:, C_AV + p, TP + b * S:TP + b * S + S], ident[:])
                mm.then_inc(turned, 1)
                for h in range(2):
                    if h:
                        pe.wait_ge(brow_done, 1)
                    pe.matmul(pr[0:16, 0:TP], rel[0:NB_BUCKETS, :], table[:, h * TP:h * TP + TP],
                              start=True, stop=True).then_inc(biased, 1)

            @block.vector
            def _(v):
                v.wait_ge(turned, 1)
                for t, (t0, m) in enumerate(QT_TILES):
                    v.tensor_copy(wrow[0:m, t, :], pw[0:m, t * 8:t * 8 + 8])
                    for p in range(2):
                        q = (2 * t + p) * P
                        v.tensor_copy(vrows[0:m, t, p * P:p * P + P], pv[0:m, q // 512, q % 512:q % 512 + P])
                v.tensor_tensor(wsel[:], wpick[:], pw[0:TS, 64:64 + TS].rearrange("p (o n) -> p o n", o=1)
                                .to_broadcast([TS, B, TS]), ALU.mult)
                v.tensor_copy(vnew[:].rearrange("p b c -> p (b c)"), pn[0:S].rearrange("p a c -> p (a c)"))
                v.tensor_tensor(near[:].rearrange("p (h s) -> p h s", s=S), spick[:],
                                rel[:].rearrange("p (h o) -> p h o", o=1).to_broadcast([P, 16, S]), ALU.mult)
                for b in range(B):
                    v.tensor_copy(sel[TS:TS + 1, b, :].rearrange("p (h s) -> p h s", s=S),
                                  far[TS:TS + 1, :].rearrange("p (h o) -> p h o", o=1).to_broadcast([1, 16, S]))
                for h in range(2):
                    v.wait_ge(biased, h + 1)
                    v.tensor_copy(brow[:, h * TP:h * TP + TP], pr[0:16, 0:TP]).then_inc(brow_done, 1)


def take_top(v, lk, best, work, rounds, last=None):
    for n in range(rounds):
        lk(v.max(best, work))
        lk(v.match_replace(work, best, work, MARK))
    if last:
        lk(v.max(best, work))
        lk(v.memset(best[:, last:8], PAD))
        lk(v.match_replace(work, best, work, MARK))


def index_prompt(cx, a, projT, wrow, mask_p):
    nc = cx.nc
    with ExitStack() as st:
        def sb(name, shape, dt=F32):
            return st.enter_context(nc.sbuf_tensor(f"ip_{name}", shape, dt))

        relu = [sb(f"relu{k}", [P, TP]) for k in range(3)]
        work = sb("work", [P, 3, TP + 8])
        causal = sb("causal", [P, 3, TP])
        best = sb("best", [P, 8])
        banks = [st.enter_context(nc.psum_tensor(f"ip_p{k}", [P, 512], F32)) for k in range(4)]
        loaded, scored, relued, added, link = (cx.sem(f"ip_{x}") for x in
                                               ("loaded", "scored", "relued", "added", "link"))
        with nc.Block() as block:
            @block.sync
            def _(sp):
                sp.dma_start(causal[:], a["causal"]).then_inc(loaded, 16)

            @block.tensor
            def _(pe):
                for t, (t0, m) in enumerate(QT_TILES):
                    for h in range(IH):
                        u = t * IH + h
                        if u >= 4:
                            pe.wait_ge(relued, u - 3)
                        pe.matmul(banks[u % 4][0:m, 0:TP], projT[:, C_QI + h, t0:t0 + m], projT[:, C_KI, 0:TP],
                                  start=True, stop=True).then_inc(scored, 1)

            @block.scalar
            def _(act):
                for t, (t0, m) in enumerate(QT_TILES):
                    for h in range(IH):
                        u = t * IH + h
                        act.wait_ge(scored, u + 1)
                        if u >= 3:
                            act.wait_ge(added, u - 2)
                        act.activation(relu[u % 3][0:m, :], banks[u % 4][0:m, 0:TP], ACT.Relu).then_inc(relued, 1)

            @block.vector
            def _(v):
                lk = Link(v, link)
                v.wait_ge(loaded, 16)
                lk(v.memset(work[:, :, TP:TP + 8], PAD))
                for t, (t0, m) in enumerate(QT_TILES):
                    w = work[0:m, t, 0:TP]
                    for h in range(IH):
                        u = t * IH + h
                        v.wait_ge(relued, u + 1)
                        if h:
                            v.wait_ge(added, u)
                        prev = w if h else causal[0:m, t, :]
                        v.scalar_tensor_tensor(w, relu[u % 3][0:m, :], wrow[0:m, t, h:h + 1], prev,
                                               ALU.mult, ALU.add).then_inc(added, 1)
                    v.wait_ge(added, t * IH + IH)
                    take_top(v, lk, best[0:m, :], work[0:m, t, :], TOPK_P // 8, TOPK_P % 8)
                    lk(v.tensor_scalar(mask_p[0:m, t, :], w, MARK / 2, NEG, ALU.is_gt, ALU.mult))
                    lk(v.tensor_tensor(mask_p[0:m, t, :], mask_p[0:m, t, :], causal[0:m, t, :], ALU.add))


def attend_prompt(cx, a, projT, mixT, ident, mask_p, vrows, bias_rows):
    nc = cx.nc
    with ExitStack() as st:
        def sb(name, shape, dt=F32):
            return st.enter_context(nc.sbuf_tensor(f"pp_{name}", shape, dt))

        bias = sb("bias", [P, 3, 16, TP])
        flip = sb("flip", [P, 2, P])
        qs = [sb(f"q{k}", [P, TP]) for k in range(2)]
        prob = [sb(f"prob{k}", [P, TP]) for k in range(2)]
        stat = [sb(f"stat{k}", [P, 4]) for k in range(2)]
        pT = [sb(f"pT{k}", [P, 3, TP]) for k in range(2)]
        banks = [st.enter_context(nc.psum_tensor(f"pp_s{k}", [P, 512], F32)) for k in range(3)]
        tbank = [st.enter_context(nc.psum_tensor(f"pp_t{k}", [P, 512], F32)) for k in range(2)]
        obank = [st.enter_context(nc.psum_tensor(f"pp_o{k}", [P, 512], F32)) for k in range(2)]
        names = ("loaded", "staged", "scored", "maxed", "exped", "normed", "turned", "moved", "summed", "mixed", "link", "zeroed", "gate")
        loaded, staged, scored, maxed, exped, normed, turned, moved, summed, mixed, link, zeroed, gate = (
            (cx.count if x in ("scored", "exped") else cx.sem)(f"pp_{x}") for x in names)
        U = 6
        units = [(t, hf) for t in range(3) for hf in range(2)]

        def every_chunk(eng, one):
            for p in range(2):
                with eng.Fori(0, 2) as gi:
                    for k in range(2):
                        one(p, gi * 2 + k, gi * 2 + (p * 4 + k), k)

        with cx.block() as block:
            @block.sync
            def _(sp):
                sp.dma_start(flip[:], a["flip"]).then_inc(loaded, 16)
                sp.wait_ge(zeroed, 3)
                for t, (t0, m) in enumerate(QT_TILES):
                    base = bias_rows[:, TP - t0 - m:]
                    src = bass.AP(base.tensor, base.offset, [[1, m], [2 * TP, 16], [1, TP]])
                    sp.dma_start(bias[0:m, t], src).then_inc(loaded, 16)

            @block.vector
            def _(v):
                def one(p, g, n, k):
                    cx.wait(v, scored, n * U)
                    v.tensor_scalar(qs[k][:], projT[:, C_Q + p * 4:C_Q + p * 4 + 4, 0:TP][:, g, :], HD ** -0.5, None,
                                    ALU.mult).then_inc(staged, 1)
                    for u, (t, hf) in enumerate(units):
                        t0, m = QT_TILES[t]
                        w = t0 + m
                        at = n * U + u
                        s = banks[u % 3]
                        cx.wait(v, scored, at + 1)
                        v.tensor_reduce(stat[u % 2][0:m, 0:1], s[0:m, 0:w], AX, ALU.max).then_inc(link, 1)
                        v.wait_ge(link, at * 2 + 1)
                        v.tensor_scalar(stat[u % 2][0:m, 1:2], stat[u % 2][0:m, 0:1], -1.0, None,
                                        ALU.mult).then_inc(maxed, 1)
                        cx.wait(v, exped, at + 1)
                        v.reciprocal(stat[u % 2][0:m, 3:4], stat[u % 2][0:m, 2:3]).then_inc(link, 1)
                        v.wait_ge(link, at * 2 + 2)
                        v.tensor_scalar(prob[u % 2][0:m, 0:w], prob[u % 2][0:m, 0:w], stat[u % 2][0:m, 3:4], None,
                                        ALU.mult).then_inc(normed, 1)
                        v.wait_ge(turned, at + 1)
                        v.tensor_copy(pT[hf][:, 0:t + 1, t0:w],
                                      tbank[u % 2][:, 0:(t + 1) * m].rearrange("p (k q) -> p k q", q=m)) \
                            .then_inc(moved, 1)
                    v.wait_ge(summed, n + 1)
                    v.tensor_copy(mixT[:, 8 + p * 4:12 + p * 4, 0:TP][:, g, :], obank[k][:, 0:TP]).then_inc(mixed, 1)
                v.memset(bias[:, 2], 0.0).then_inc(zeroed, 1)
                for k in range(2):
                    v.memset(pT[k][:], 0.0).then_inc(zeroed, 1)
                v.wait_ge(zeroed, 3)
                every_chunk(v, one)

            @block.scalar
            def _(act):
                def one(p, g, n, k):
                    for u, (t, hf) in enumerate(units):
                        t0, m = QT_TILES[t]
                        act.wait_ge(maxed, n * U + u + 1)
                        act.activation(prob[u % 2][0:m, 0:t0 + m], banks[u % 3][0:m, 0:t0 + m], ACT.Exp,
                                       bias=stat[u % 2][0:m, 1:2], accum_out=stat[u % 2][0:m, 2:3]) \
                            .then_inc(exped, 1)
                every_chunk(act, one)

            @block.tensor
            def _(pe):
                pe.wait_ge(loaded, 64)
                pe.wait_ge(zeroed, 3)

                def score(p, g, n, k, u):
                    t, hf = units[u]
                    t0, m = QT_TILES[t]
                    w = t0 + m
                    r = slice(hf * HD, hf * HD + HD)
                    s = banks[u % 3][0:m, 0:w]
                    if u >= 3:
                        cx.wait(pe, exped, n * U + u - 2, gate)
                    fl = flip[:, t // 2, 0:m]
                    heads = bias[:, t].rearrange("p (n g) k -> p n g k", g=GROUP)
                    pe.matmul(s, fl, heads[:, 2 * p + hf, :, 0:w][:, g, :], start=True, stop=False)
                    pe.matmul(s, ident[0:m, 0:m], mask_p[0:m, t, 0:w], start=False, stop=False)
                    pe.matmul(s, qs[k][r, t0:w], projT[r, C_AK + p, 0:w], start=False, stop=True).then_inc(scored, 1)

                def turn(n, u):
                    t, hf = units[u]
                    t0, m = QT_TILES[t]
                    wait_loop(pe, normed, n * U + u + 1, gate)
                    for kt in range(t + 1):
                        kw = QT_TILES[kt][1]
                        mm = pe.transpose(tbank[u % 2][0:kw, kt * m:kt * m + m],
                                          prob[u % 2][0:m, kt * P:kt * P + kw], ident[0:m, 0:m])
                    mm.then_inc(turned, 1)

                def one(p, g, n, k):
                    pe.wait_ge(staged, n + 1)
                    cx.wait(pe, exped, n * U)
                    for u in range(U + 1):
                        if u < U:
                            score(p, g, n, k, u)
                        if u:
                            if u >= 3:
                                pe.wait_ge(moved, n * U + u - 2)
                            turn(n, u - 1)
                    pe.wait_ge(moved, n * U + U)
                    for hf in range(2):
                        r = slice(hf * HD, hf * HD + HD)
                        for kt, (k0, kw) in enumerate(QT_TILES):
                            mm = pe.matmul(obank[k][r, k0:TP], vrows[0:kw, kt, p * P + hf * HD:p * P + hf * HD + HD],
                                           pT[hf][0:kw, kt, k0:TP], start=kt == 0, stop=kt == 2)
                    mm.then_inc(summed, 1)
                every_chunk(pe, one)


def load_pages(eng, table, pool, b, place, sem, registers):
    for j in range(PAGES):
        page = eng.value_load(table[0:1, bass.ds(b * PAGES + j, 1)], min_val=0, max_val=pool.shape[0] - 1)
        eng.dma_start(place(j), pool[bass.ds(page, 1)].rearrange("o p c -> (o p) c") if len(pool.shape) == 3
                      else pool[bass.ds(page, 1)].rearrange("o p a c -> (o p) a c")).then_inc(sem, 16)


def index_sampled(cx, a, projT, wsel, mask_s):
    nc = cx.nc
    with ExitStack() as st:
        def sb(name, shape, dt=F32):
            return st.enter_context(nc.sbuf_tensor(f"is_{name}", shape, dt))

        keys = [sb(f"keys{k}", [P, PAST + S]) for k in range(2)]
        qi = [sb(f"qi{k}", [P, IH * S]) for k in range(2)]
        ws = [sb(f"ws{k}", [TS, TS]) for k in range(2)]
        relu = [sb(f"relu{k}", [TS, 512]) for k in range(2)]
        work = sb("work", [TS, WORK_S])
        best = sb("best", [TS, 8])
        newmask = sb("newmask", [TS, S])
        table = sb("table", [1, B * PAGES], I32)
        banks = [st.enter_context(nc.psum_tensor(f"is_s{k}", [P, 512], F32)) for k in range(2)]
        wbanks = [st.enter_context(nc.psum_tensor(f"is_w{k}", [P, 512], F32)) for k in range(2)]
        tabled, small, scored, relued, weighted, added, staged, link, gate = (
            (cx.count if x in ("scored", "relued", "weighted", "added") else cx.sem)(f"is_{x}") for x in ("tabled", "small", "scored", "relued", "weighted", "added", "staged", "link",
                                        "gate"))
        loaded = [cx.sem(f"is_loaded{k}") for k in range(2)]
        C = 5
        block_of = lambda c: slice(c * 512, min(c * 512 + 512, PAST + S))

        with cx.block() as block:
            @block.sync
            def _(sp):
                sp.dma_start(newmask[:], a["newmask"]).then_inc(small, 16)
                sp.dma_start(table[:], a["page_table"]).then_inc(tabled, 16)
                sp.wait_ge(tabled, 16)
                with sp.Fori(0, B // 2) as i:
                    for k in range(2):
                        b = i * 2 + k
                        cx.wait(sp, scored, (i * 2 + k - 1) * C if k else i * 2 * C)
                        load_pages(sp, table, a["kidxT"], b,
                                   lambda j: keys[k][:, j * PAGE:j * PAGE + PAGE], loaded[k], None)

            @block.tensor
            def _(pe):
                with pe.Fori(0, B // 2) as i:
                    for k in range(2):
                        at = (i * 2 + k) * C
                        pe.wait_ge(loaded[k], i * 16 * PAGES + 16 * PAGES)
                        pe.wait_ge(staged, i * 2 + k + 1)
                        for c in range(C + 1):
                            if c < C:
                                cols = block_of(c)
                                cx.wait(pe, relued, at + c - 1 if c else at)
                                pe.matmul(banks[c % 2][0:TS, 0:cols.stop - cols.start], qi[k][:], keys[k][:, cols],
                                          start=True, stop=True).then_inc(scored, 1)
                            if c:
                                cols = block_of(c - 1)
                                cx.wait(pe, added, at + c - 2 if c > 1 else at)
                                cx.wait(pe, relued, at + c, gate)
                                w = cols.stop - cols.start
                                pe.matmul(wbanks[(c - 1) % 2][0:TS, 0:w], ws[k][:], relu[(c - 1) % 2][:, 0:w],
                                          start=True, stop=True).then_inc(weighted, 1)

            @block.scalar
            def _(act):
                with act.Fori(0, B // 2) as i:
                    for k in range(2):
                        at = (i * 2 + k) * C
                        for c in range(C):
                            w = block_of(c).stop - block_of(c).start
                            cx.wait(act, scored, at + c + 1)
                            cx.wait(act, weighted, at + c - 1 if c else at)
                            act.activation(relu[c % 2][:, 0:w], banks[c % 2][0:TS, 0:w], ACT.Relu).then_inc(relued, 1)

            @block.vector
            def _(v):
                lk = Link(v, link)
                lk(v.memset(work[:, 0:PAST + S], 0.0))
                lk(v.memset(work[:, PAST + S:WORK_S], PAD))
                lk(v.memset(mask_s[TS:TS + 1, 0:FAR], 1.0))
                lk(v.memset(mask_s[TS:TS + 1, FAR:PAST + S], 0.0))
                with v.Fori(0, B // 2) as i:
                    for k in range(2):
                        at = (i * 2 + k) * C
                        b = i * 2 + k
                        new = slice(TP, N)
                        cx.wait(v, weighted, (i * 2 + k - 1) * C if k else i * 2 * C)
                        v.tensor_copy(ws[k][:], wsel[:, b, :])
                        v.tensor_copy(keys[k][:, PAST:PAST + S], projT[:, C_KI, TP:N].rearrange(
                            "p (b s) -> p b s", s=S)[:, b, :])
                        v.tensor_copy(qi[k][:].rearrange("p (h s) -> p h s", s=S),
                                      projT[:, C_QI:C_QI + IH, TP:N].rearrange("p h (b s) -> p h b s", s=S)[:, :, b, :]) \
                            .then_inc(staged, 1)
                        for c in range(C):
                            cols = block_of(c)
                            cx.wait(v, weighted, at + c + 1)
                            if c == 0:
                                cx.wait(v, added, at)
                            v.tensor_tensor(work[:, cols], work[:, cols], wbanks[c % 2][0:TS, 0:cols.stop - cols.start],
                                            ALU.add).then_inc(added, 1)
                cx.wait(v, added, B * C)
                v.wait_ge(small, 16)
                lk(v.tensor_tensor(work[:, PAST:PAST + S], work[:, PAST:PAST + S], newmask[:], ALU.add))
                take_top(v, lk, best[:], work[:], TOPK_S // 8, TOPK_S % 8)
                lk(v.tensor_scalar(mask_s[0:TS, :], work[:, 0:PAST + S], MARK / 2, NEG, ALU.is_gt, ALU.mult))
                lk(v.tensor_tensor(mask_s[0:TS, PAST:PAST + S], mask_s[0:TS, PAST:PAST + S], newmask[:], ALU.add))


def attend_sampled(cx, a, projT, mixT, ident, mask_s, sel, near, onehot, vnew):
    nc = cx.nc
    Q = 64
    with ExitStack() as st:
        def sb(name, shape, dt=F32):
            return st.enter_context(nc.sbuf_tensor(f"as_{name}", shape, dt))

        keys = [sb(f"keys{k}", [P, 2, PAST + S]) for k in range(2)]
        vals = [sb(f"vals{k}", [P, PAGES, 2 * P]) for k in range(2)]
        vn = [sb(f"vn{k}", [S, 2 * P]) for k in range(2)]
        qb = [sb(f"qb{k}", [P, 2, Q]) for k in range(2)]
        ss = [sb(f"sel{k}", [TS + 1, Q]) for k in range(2)]
        prob = sb("prob", [Q, PAST + S])
        stat = sb("stat", [Q, 8])
        pT = sb("pT", [P, PAGES + 1, Q])
        table = sb("table", [1, B * PAGES], I32)
        sbank = st.enter_context(nc.psum_tensor("as_s", [P, 5, 512], F32))
        tbank = st.enter_context(nc.psum_tensor("as_t", [P, 2, 512], F32))
        obank = st.enter_context(nc.psum_tensor("as_o", [P, 512], F32))
        tabled, staged, scored, maxed, exped, normed, turned, moved, summed, mixed, link, gate = (
            (cx.count if x in ("exped", "moved", "summed", "mixed") else cx.sem)(f"as_{x}") for x in ("tabled", "staged", "scored", "maxed", "exped", "normed", "turned", "moved",
                                        "summed", "mixed", "link", "gate"))
        loaded = [cx.sem(f"as_loaded{k}") for k in range(2)]
        REST = PAST + S - 4 * SCORE_COLS
        LK = 5

        with cx.block() as block:
            @block.sync
            def _(sp):
                sp.dma_start(table[:], a["page_table"]).then_inc(tabled, 16)
                sp.wait_ge(tabled, 16)
                with sp.Fori(0, B // 2) as i:
                    for k in range(2):
                        b = i * 2 + k
                        cx.wait(sp, summed, i * 2 + k - 1 if k else i * 2)
                        load_pages(sp, table, a["keysT"], b,
                                   lambda j: keys[k][:, :, j * PAGE:j * PAGE + PAGE], loaded[k], None)
                        load_pages(sp, table, a["values"], b, lambda j: vals[k][:, j, :], loaded[k], None)

            @block.vector
            def _(v):
                lk = Link(v, link)
                for k in range(2):
                    lk(v.memset(qb[k][:], 0.0))
                new = projT[:, :, TP:N].rearrange("p c (b s) -> p c b s", s=S)
                with v.Fori(0, B // 2) as i:
                    lk.enter(i, 2 * LK)
                    for k in range(2):
                        b = i * 2 + k
                        cx.wait(v, summed, b - 1 if k else i * 2)
                        for p in range(2):
                            for hf in range(2):
                                r = slice(hf * HD, hf * HD + HD)
                                c0 = (2 * p + hf) * 16
                                v.tensor_scalar(qb[k][r, p, c0:c0 + 16].rearrange("p (g s) -> p g s", s=S),
                                                new[r, C_Q + p * 4:C_Q + p * 4 + 4, b, :], HD ** -0.5, None, ALU.mult)
                        v.tensor_copy(keys[k][:, :, PAST:PAST + S], new[:, C_AK:C_AK + 2, b, :])
                        v.tensor_copy(vn[k][:], vnew[:, b, :])
                        v.tensor_copy(ss[k][:], sel[:, b, :]).then_inc(staged, 1)
                        v.wait_ge(scored, b + 1)
                        lk(v.tensor_reduce(stat[:, 0:4], sbank[0:Q, 0:4, 0:SCORE_COLS], AX, ALU.max))
                        lk(v.tensor_reduce(stat[:, 4:5], sbank[0:Q, 4, 0:REST], AX, ALU.max))
                        lk(v.tensor_reduce(stat[:, 5:6], stat[:, 0:5], AX, ALU.max))
                        v.tensor_scalar(stat[:, 5:6], stat[:, 5:6], -1.0, None, ALU.mult).then_inc(maxed, 1)
                        cx.wait(v, exped, b + 1)
                        lk(v.tensor_tensor(stat[:, 6:7], stat[:, 6:7], stat[:, 7:8], ALU.add))
                        lk(v.reciprocal(stat[:, 6:7], stat[:, 6:7]))
                        v.tensor_scalar(prob[:], prob[:], stat[:, 6:7], None, ALU.mult).then_inc(normed, 1)
                        v.wait_ge(turned, i * 6 + 3 * k + 2)
                        v.tensor_copy(pT[:, 0:PAGES, :], tbank[:].rearrange("p a (c q) -> p (a c) q", q=Q)) \
                            .then_inc(moved, 1)
                        v.wait_ge(turned, i * 6 + 3 * k + 3)
                        v.tensor_copy(pT[0:S, PAGES, :], tbank[0:S, 0, 0:Q]).then_inc(moved, 1)
                        cx.wait(v, summed, b + 1)
                        for p in range(2):
                            for hf in range(2):
                                r = slice(hf * HD, hf * HD + HD)
                                c0 = p * Q + (2 * p + hf) * 16
                                ins = v.tensor_copy(
                                    mixT[r, 8 + p * 4:12 + p * 4, TP:N].rearrange("p c (b s) -> p c b s", s=S)[:, :, b, :],
                                    obank[r, c0:c0 + 16].rearrange("p (g s) -> p g s", s=S))
                        ins.then_inc(mixed, 1)
                    lk.leave(B // 2)

            @block.scalar
            def _(act):
                with act.Fori(0, B // 2) as i:
                    for k in range(2):
                        b = i * 2 + k
                        act.wait_ge(maxed, b + 1)
                        act.activation(prob[:, 0:4 * SCORE_COLS].rearrange("p (a c) -> p a c", a=4),
                                       sbank[0:Q, 0:4, 0:SCORE_COLS], ACT.Exp, bias=stat[:, 5:6],
                                       accum_out=stat[:, 6:7])
                        act.activation(prob[:, 4 * SCORE_COLS:PAST + S], sbank[0:Q, 4, 0:REST], ACT.Exp,
                                       bias=stat[:, 5:6], accum_out=stat[:, 7:8]).then_inc(exped, 1)

            @block.tensor
            def _(pe):
                with pe.Fori(0, B // 2) as i:
                    for k in range(2):
                        b = i * 2 + k
                        pe.wait_ge(loaded[k], (i + 1) * (2 * 16 * PAGES))
                        pe.wait_ge(staged, b + 1)
                        cx.wait(pe, exped, b)
                        for c in range(5):
                            c0 = c * SCORE_COLS
                            w = SCORE_COLS if c < 4 else REST
                            s = sbank[0:Q, c, 0:w]
                            for p in range(2):
                                pe.matmul(s, qb[k][:, p, :], keys[k][:, p, c0:c0 + w], start=p == 0, stop=False)
                            mm = pe.matmul(s, ss[k][:], mask_s[:, c0:c0 + w], start=False, stop=c < 4)
                        mm = pe.matmul(sbank[0:Q, 4, 0:REST], near[:], onehot[:], start=False, stop=True)
                        mm.then_inc(scored, 1)
                        pe.wait_ge(normed, b + 1)
                        cx.wait(pe, moved, b * 2, gate)
                        for j in range(PAGES):
                            mm = pe.transpose(tbank[:, j // 8, (j % 8) * Q:(j % 8) * Q + Q],
                                              prob[:, j * PAGE:j * PAGE + PAGE], ident[0:Q, 0:Q])
                        mm.then_inc(turned, 2)
                        cx.wait(pe, moved, b * 2 + 1, gate)
                        pe.transpose(tbank[0:S, 0, 0:Q], prob[:, PAST:PAST + S], ident[0:Q, 0:Q]).then_inc(turned, 1)
                        cx.wait(pe, moved, b * 2 + 2)
                        cx.wait(pe, mixed, b)
                        for p in range(2):
                            for j in range(PAGES):
                                pe.matmul(obank[:, p * Q:p * Q + Q], vals[k][:, j, p * P:p * P + P], pT[:, j, :],
                                          start=j == 0, stop=False)
                            mm = pe.matmul(obank[:, p * Q:p * Q + Q], vn[k][:, p * P:p * P + P], pT[0:S, PAGES, :],
                                           start=False, stop=True)
                        mm.then_inc(summed, 1)


def peer(cx, a, xT, ident):
    nc = cx.nc
    with ExitStack() as st:
        gates = st.enter_context(nc.sbuf_tensor("pe_gates", [P, NK, N], F32))
        with ExitStack() as chosen:
            picks = chosen.enter_context(nc.sbuf_tensor("pe_picks", [P, 3, N], F32))
            cx.phase(peer_select, a, xT, ident, picks, gates)
            cx.phase(peer_gates, a, picks, gates)
        cx.phase(peer_up, a, xT, gates)
        cx.phase(peer_down, a, xT, gates)


def peer_select(cx, a, xT, ident, picks, gates):
    nc = cx.nc
    SL = 4
    with ExitStack() as st:
        room = gates[:].rearrange("p k n -> p (k n)")
        taken = [0]

        def sb(name, shape, dt=F32):
            size = int(np.prod(shape[1:]))
            flat = room[:, taken[0]:taken[0] + size]
            taken[0] += size
            if dt != F32:
                flat = flat.bitcast(dt)
            if len(shape) == 2:
                return flat
            names = "abcd"[:len(shape) - 1]
            return flat.rearrange(f"p ({' '.join(names)}) -> p {' '.join(names)}",
                                  **{n: s for n, s in zip(names, shape[1:])})

        w = [sb(f"w{s}", [P, KT, P]) for s in range(SL)]
        sk = [sb(f"sk{s}", [P, P]) for s in range(SL)]
        q = [sb(f"q{s}", [P, 3 * P]) for s in range(SL)]
        score = sb("score", [P, 3, NK])
        top = [sb(f"top{h}", [P, 3, EK]) for h in range(2)]
        topi = sb("topi", [P, 3, EK], U32)
        keyf = [sb(f"keyf{h}", [P, 3, EK]) for h in range(2)]
        cand = sb("cand", [P, 3, EK * EK])
        best = sb("best", [P, 3, EK])
        diff = sb("diff", [P, 3, EK])
        bi = sb("bi", [P, 3, EK], U32)
        part = sb("part", [P, 3, EK], U32)
        partf = sb("partf", [P, 3, EK])
        hit = sb("hit", [P, 3 * EK, EK])
        total = sb("total", [P, 3, 1])
        iota = sb("iota", [P, EK])
        chosen = sb("chosen", [P, 3, 3, PH * EK])
        acc = [st.enter_context(nc.psum_tensor(f"ps_acc{s}", [P, 512], F32)) for s in range(SL)]
        sbank = [st.enter_context(nc.psum_tensor(f"ps_s{s}", [P, 512], F32)) for s in range(2)]
        tbank = [st.enter_context(nc.psum_tensor(f"ps_t{s}", [P, 512], F32)) for s in range(2)]
        loaded = [cx.sem(f"ps_loaded{s}") for s in range(SL)]
        summed = [cx.sem(f"ps_summed{s}") for s in range(SL)]
        emptied = [cx.count(f"ps_emptied{s}") for s in range(SL)]
        scored = [cx.count(f"ps_scored{s}") for s in range(SL)]
        read = [cx.count(f"ps_read{s}") for s in range(2)]
        small, gate, link, diffed, exped, turned, moved = (cx.sem(f"ps_{x}") for x in
                                                     ("small", "gate", "link", "diffed", "exped", "turned", "moved"))

        with cx.block() as block:
            @block.sync
            def _(sp):
                sp.dma_start(iota, a["iota"][:, 0:EK]).then_inc(small, 16)
                with sp.Fori(0, 2 * PH // SL) as i:
                    for s in range(SL):
                        cx.wait(sp, scored[s], i)
                        sp.dma_start(w[s], a["peer_wq"][i * SL + s]).then_inc(loaded[s], 16)
                        sp.dma_start(sk[s], a["subkeysT"][i * SL + s]).then_inc(loaded[s], 16)

            @block.tensor
            def _(pe):
                def project_chunk(i, s):
                    pe.wait_ge(loaded[s], i * 32 + 32)
                    cx.wait(pe, emptied[s], i)
                    for k in range(KT):
                        mm = pe.matmul(acc[s][:, 0:N], w[s][:, k, :], xT[:, k, :], start=k == 0, stop=k == KT - 1)
                    mm.then_inc(summed[s], 1)

                def score_chunk(i, s):
                    cx.wait(pe, emptied[s], i + 1)
                    cx.wait(pe, read[s % 2], i * 2 + s // 2)
                    for t in range(3):
                        mm = pe.matmul(sbank[s % 2][:, t * P:t * P + P], q[s][:, t * P:t * P + P], sk[s],
                                       start=True, stop=True)
                    mm.then_inc(scored[s], 1)

                with pe.Fori(0, 2 * PH // SL) as i:
                    for s in range(SL):
                        project_chunk(i, s)
                        if s:
                            score_chunk(i, s - 1)
                    score_chunk(i, SL - 1)
                pe.wait_ge(link, SL + (2 * PH // SL) * LINKS_PS)
                for which in range(3):
                    if which == 2:
                        pe.wait_ge(moved, 1)
                    for t in range(3):
                        mm = pe.transpose(tbank[which % 2][:, t * P:t * P + P], chosen[:, which, t, :], ident[:])
                    mm.then_inc(turned, 1)

            @block.scalar
            def _(act):
                with act.Fori(0, PH) as h:
                    act.wait_ge(diffed, h + 1)
                    act.activation(diff, diff, ACT.Exp).then_inc(exped, 1)

            @block.vector
            def _(v):
                lk = Link(v, link, gate)
                v.wait_ge(small, 16)
                for s in range(SL):
                    lk(v.memset(q[s][:, N:3 * P], 0.0))

                def half(i, s):
                    v.wait_ge(summed[s], i + 1)
                    v.tensor_copy(q[s][:, 0:N], acc[s][:, 0:N]).then_inc(emptied[s], 1)
                    cx.wait(v, scored[s], i + 1)
                    v.tensor_copy(score.rearrange("p t k -> p (t k)"), sbank[s % 2][:, 0:3 * P]).then_inc(read[s % 2], 1)
                    cx.wait(v, read[s % 2], i * 2 + s // 2 + 1, gate)
                    tp = top[s % 2]
                    sixteen(lambda t: score[:, t, :], tp)
                    lk(v.tensor_copy(keyf[s % 2], topi))

                def sixteen(values, tp):
                    idx = topi
                    for n in range(2):
                        for t in range(3):
                            ins = v.max(tp[:, t, 8 * n:8 * n + 8], values(t))
                        lk(ins)
                        for t in range(3):
                            ins = v.max_index(idx[:, t, 8 * n:8 * n + 8], tp[:, t, 8 * n:8 * n + 8], values(t))
                        lk(ins)
                        if n == 0:
                            for t in range(3):
                                ins = v.match_replace(values(t), tp[:, t, 0:8], values(t), MARK)
                            lk(ins)

                def head(h):
                    ax = lambda q, where: q.rearrange("p t (k o) -> p t k o" if where else "p t (o k) -> p t o k", o=1)
                    grid = cand.rearrange("p t (x y) -> p t x y", y=EK)
                    for t in range(3):
                        ins = v.tensor_tensor(grid[:, t], ax(top[0], 1)[:, t].to_broadcast([P, EK, EK]),
                                              ax(top[1], 0)[:, t].to_broadcast([P, EK, EK]), ALU.add)
                    lk(ins)
                    sixteen(lambda t: cand[:, t, :], best)
                    lk(v.tensor_copy(bi, topi))
                    v.tensor_tensor(diff, best, best[:, :, 0:1].to_broadcast([P, 3, EK]), ALU.subtract) \
                        .then_inc(diffed, 1)
                    for half_, (op, by) in enumerate(((ALU.logical_shift_right, 4), (ALU.bitwise_and, EK - 1))):
                        lk(v.tensor_scalar(part, bi, by, None, op))
                        lk(v.tensor_copy(partf, part))
                        lk(v.tensor_tensor(hit, partf.rearrange("p t (k o) -> p (t k) o", o=1)
                                           .to_broadcast([P, 3 * EK, EK]),
                                           iota.rearrange("p (o k) -> p o k", o=1).to_broadcast([P, 3 * EK, EK]),
                                           ALU.is_equal))
                        hit4 = hit.rearrange("p (t k) x -> p t k x", t=3)
                        for t in range(3):
                            ins = v.tensor_tensor(hit4[:, t], hit4[:, t],
                                                  ax(keyf[half_], 0)[:, t].to_broadcast([P, EK, EK]), ALU.mult)
                        lk(ins)
                        lk(v.tensor_reduce(chosen[:, half_].rearrange("p t (h k) -> p t h k", h=PH)[:, :, h, :],
                                           hit4, AX, ALU.add))
                    v.wait_ge(exped, h + 1)
                    lk(v.tensor_reduce(total, diff, AX, ALU.add))
                    lk(v.reciprocal(total, total))
                    lk(v.tensor_tensor(chosen[:, 2].rearrange("p t (h k) -> p t h k", h=PH)[:, :, h, :], diff,
                                       total.to_broadcast([P, 3, EK]), ALU.mult))

                with v.Fori(0, 2 * PH // SL) as i:
                    lk.enter(i, LINKS_PS)
                    for s in range(SL):
                        half(i, s)
                        if s % 2:
                            head(i * 2 + s // 2)
                    lk.leave(2 * PH // SL)
                for which in range(3):
                    v.wait_ge(turned, which + 1)
                    v.tensor_copy(picks[:, which, :], tbank[which % 2][:, 0:N]).then_inc(moved, 1)


def peer_gates(cx, a, picks, gates):
    nc = cx.nc
    G4 = 4
    with ExitStack() as st:
        iota = st.enter_context(nc.sbuf_tensor("pg_iota", [P, NK], F32))
        first = [st.enter_context(nc.sbuf_tensor(f"pg_first{k}", [P, G4, NK], F32)) for k in range(2)]
        second = [st.enter_context(nc.sbuf_tensor(f"pg_second{k}", [P, G4, NK], F32)) for k in range(2)]
        banks = [st.enter_context(nc.psum_tensor(f"pg_b{k}", [P, 512], F32)) for k in range(2)]
        loaded, built = cx.sem("pg_loaded"), cx.sem("pg_built")
        summed, moved = cx.count("pg_summed"), cx.count("pg_moved")
        turns = N // (2 * G4)
        with cx.block() as block:
            @block.sync
            def _(sp):
                sp.dma_start(iota[:], a["iota"]).then_inc(loaded, 16)

            @block.vector
            def _(v):
                v.wait_ge(loaded, 16)
                with v.Fori(0, turns) as i:
                    for k in range(2):
                        cx.wait(v, summed, i * 2 + k - 1 if k else i * 2)
                        for n in range(G4):
                            tok = i * (2 * G4) + (k * G4 + n)
                            v.tensor_scalar(first[k][:, n, :], iota[:], picks[:, 0, bass.ds(tok, 1)],
                                            picks[:, 2, bass.ds(tok, 1)], ALU.is_equal, ALU.mult)
                            ins = v.tensor_scalar(second[k][:, n, :], iota[:], picks[:, 1, bass.ds(tok, 1)], None,
                                                  ALU.is_equal)
                        ins.then_inc(built, 1)

            @block.tensor
            def _(pe):
                with pe.Fori(0, turns) as i:
                    for k in range(2):
                        pe.wait_ge(built, i * 2 + k + 1)
                        cx.wait(pe, moved, i * 2 + k - 1 if k else i * 2)
                        for n in range(G4):
                            mm = pe.matmul(banks[k][:, n * NK:n * NK + NK], second[k][:, n, :], first[k][:, n, :],
                                           start=True, stop=True)
                        mm.then_inc(summed, 1)

            @block.scalar
            def _(act):
                with act.Fori(0, turns) as i:
                    for k in range(2):
                        cx.wait(act, summed, i * 2 + k + 1)
                        act.activation(gates[:, :, bass.ds(i * (2 * G4) + k * G4, G4)],
                                       banks[k][:].rearrange("p (n i) -> p i n", n=G4), ACT.Copy).then_inc(moved, 1)


def peer_up(cx, a, xT, gates):
    nc = cx.nc
    SL = 3
    with ExitStack() as st:
        u = [st.enter_context(nc.sbuf_tensor(f"pu_u{s}", [P, KT, P], F32)) for s in range(SL)]
        h = [st.enter_context(nc.sbuf_tensor(f"pu_h{s}", [P, N], F32)) for s in range(SL)]
        acc = [st.enter_context(nc.psum_tensor(f"pu_acc{s}", [P, 512], F32)) for s in range(SL)]
        loaded = [cx.sem(f"pu_loaded{s}") for s in range(SL)]
        summed, curved, weighed = ([cx.count(f"pu_{x}{s}") for s in range(SL)] for x in ("summed", "curved", "weighed"))

        def every(eng, one):
            with eng.Fori(0, NK // SL) as i:
                for s in range(SL):
                    one(i, s)
            for s in range(NK % SL):
                one(NK // SL, s)

        with cx.block() as block:
            @block.sync
            def _(sp):
                def one(i, s):
                    cx.wait(sp, summed[s], i)
                    sp.dma_start(u[s][:], a["peer_u"][i * SL + s]).then_inc(loaded[s], 16)
                every(sp, one)

            @block.tensor
            def _(pe):
                def one(i, s):
                    pe.wait_ge(loaded[s], i * 16 + 16)
                    cx.wait(pe, curved[s], i)
                    for k in range(KT):
                        mm = pe.matmul(acc[s][:, 0:N], u[s][:, k, :], xT[:, k, :], start=k == 0, stop=k == KT - 1)
                    mm.then_inc(summed[s], 1)
                every(pe, one)

            @block.scalar
            def _(act):
                def one(i, s):
                    cx.wait(act, summed[s], i + 1)
                    cx.wait(act, weighed[s], i)
                    act.activation(h[s][:], acc[s][:, 0:N], ACT.Gelu).then_inc(curved[s], 1)
                every(act, one)

            @block.vector
            def _(v):
                def one(i, s):
                    cx.wait(v, curved[s], i + 1)
                    g = gates[:, i * SL + s, :]
                    v.tensor_tensor(g, g, h[s][:], ALU.mult).then_inc(weighed[s], 1)
                every(v, one)


def peer_down(cx, a, xT, gates):
    nc = cx.nc
    SL, E2 = 3, 2
    HALF = D // 2
    groups = NK // E2
    with ExitStack() as st:
        w = [st.enter_context(nc.sbuf_tensor(f"pd_v{s}", [P, E2, HALF], F32)) for s in range(SL)]
        acc = [st.enter_context(nc.psum_tensor(f"pd_acc{s}", [P, 512], F32)) for s in range(8)]
        loaded = [[cx.sem(f"pd_loaded{h}{s}") for s in range(SL)] for h in range(2)]
        used = [[cx.count(f"pd_used{h}{s}") for s in range(SL)] for h in range(2)]
        summed, emptied = cx.sem("pd_summed"), cx.sem("pd_emptied")
        assert (groups - 1) % SL == 0

        def every(eng, one):
            for half in range(2):
                one(half, 0, 0, 0)
                with eng.Fori(0, (groups - 1) // SL) as i:
                    for s in range(SL):
                        one(half, i * SL + (1 + s), (1 + s) % SL, i + (1 if s == SL - 1 else 0))

        with cx.block() as block:
            @block.sync
            def _(sp):
                def one(half, g, s, turn):
                    if half:
                        cx.wait(sp, used[0][s], groups // SL + (1 if s == 0 else 0))
                    cx.wait(sp, used[half][s], turn)
                    sp.dma_start(w[s][:], a["peer_v"][:, :, half][bass.ds(g, 1)].rearrange("o p e d -> (o p) e d")) \
                        .then_inc(loaded[half][s], 16)
                every(sp, one)

            @block.tensor
            def _(pe):
                def one(half, g, s, turn):
                    static = isinstance(g, int)
                    pe.wait_ge(loaded[half][s], turn * 16 + 16)
                    if static and half:
                        pe.wait_ge(emptied, 8)
                    for e in range(E2):
                        for d in range(8):
                            mm = pe.matmul(acc[d][:, 0:N], w[s][:, e, d * P:d * P + P],
                                           gates[:, g * E2 + e, :], start=static and e == 0, stop=False,
                                           skip_group_check=True)
                    mm.then_inc(used[half][s], 1)
                every(pe, one)

            @block.vector
            def _(v):
                for half in range(2):
                    for s in range(SL):
                        cx.wait(v, used[half][s], groups // SL + (1 if s == 0 else 0))
                    for d in range(8):
                        x = xT[:, half * 8 + d, :]
                        v.scalar_tensor_tensor(x, x, ALPHA, acc[d][:, 0:N], ALU.mult, ALU.add).then_inc(emptied, 1)


LINKS_PS = 64

def chunked(w, cols):
    w = np.asarray(w)
    out = np.zeros((w.shape[0], len(cols)), w.dtype)
    ok = cols >= 0
    out[:, ok] = w[:, cols[ok]]
    return np.ascontiguousarray(out.reshape(w.shape[0] // P, P, len(cols) // P, P).transpose(2, 1, 0, 3))


def in_columns():
    cols = list(range(RC)) + [-1] * (RWC * P - RC)
    cols += [RC + x for x in q_order()]
    cols += list(range(RC + 1024, RC + 1024 + 512 + IH * ID + ID + IH)) + [-1] * (P - IH)
    return np.array(cols)


def q_order():
    return [((2 * p + hf) * GROUP + g) * HD + d for p in range(2) for g in range(GROUP) for hf in range(2)
            for d in range(HD)]


def fold(v, chunks):
    v = np.asarray(v).reshape(-1)
    return np.ascontiguousarray(np.pad(v, (0, chunks * P - v.size)).reshape(chunks, P).T)


def across(s):
    out = np.zeros((8, 2, HD, B, 2, HD), s.dtype)
    for h in range(2):
        out[:, h, :, :, h, :] = s[:, h]
    return out.reshape(8, P, B, P)


def attention_layouts(x):
    f = np.float32
    e = np.eye
    hs = np.arange(TS)
    t = np.arange(2 * TP)
    s, key = np.arange(S)[:, None], FAR + np.arange(PAGE + S)[None, :]
    near = bucket(PAST + s - key)
    q, kpos = np.arange(3 * P), np.arange(TP)
    flip = np.zeros((P, 2, P), f)
    flip[:, 0] = e(P)[::-1]
    flip[:16, 1, :16] = e(16)[::-1]
    n_pool = x["cache_k"].shape[1]
    qn = np.arange(64)
    return {
        "spread": (np.arange(IH)[:, None] == hs[None, :] // S).astype(f),
        "wpick": ((hs[:, None, None] % S == hs[None, None, :] % S)
                  & (np.arange(B)[None, :, None] == hs[None, None, :] // S)).astype(f),
        "spick": np.broadcast_to(np.arange(P)[:, None, None] // 32 == np.arange(S)[None, None, :], (P, 16, S)).astype(f),
        "bucket_table": (np.arange(NB_BUCKETS)[:, None] == bucket(TP - 1 - t)[None, :]).astype(f),
        "near_onehot": (near[:, None, :] == np.arange(NB_BUCKETS)[None, :, None]).reshape(P, PAGE + S).astype(f),
        "sel": ((hs[:, None, None] // S == np.arange(B)[None, :, None])
                & (hs[:, None, None] % S == qn[None, None, :] % S)).astype(f),
        "rel_bias": x["rel_bias"],
        "causal": np.where(kpos[None, :] <= q[:, None], 0, NEG).reshape(3, P, TP).transpose(1, 0, 2).astype(f),
        "newmask": np.where(np.arange(S)[None, :] <= (hs % S)[:, None], 0, NEG).astype(f),
        "flip": flip,
        "page_table": x["page_table"].reshape(1, -1).astype(np.int32),
        "kidxT": x["cache_kidx"][0].transpose(0, 2, 1),
        "keysT": x["cache_k"][0].reshape(n_pool, PAGE, 2, P).transpose(0, 3, 2, 1),
        "values": x["cache_v"][0].reshape(n_pool, PAGE, 2 * P),
    }


def layouts(x):
    f = np.float32
    rows = np.concatenate([x["meta_tokens"], x["x_prompt"][0], x["x_sample"].reshape(TS, D)])
    a = {
        "xT": rows.T.reshape(KT, P, N).transpose(1, 0, 2),
        "ones": np.full((P, P), 1 / D, f),
        "ident": np.eye(P, dtype=f),
        "ln_gb": np.stack([np.stack([fold(x[g], KT), fold(x[b], KT)], 1)
                           for g, b in (("ln_in_g", "ln_in_b"), ("ln1_g", "ln1_b"), ("ln2_g", "ln2_b"))], 1),
        "rw_masks": rwkv_masks(),
        "seqmask": (np.arange(P)[:, None] // S - CH // 2 // S == np.arange(B)[None, :]).astype(f),
        "halves": (np.arange(P)[:, None] // HD == np.arange(P)[None, :] // HD).astype(f),
        "rw_cols": np.stack([fold(x["mu_shift"][0][:RW], 8), fold(x["mu_shift"][0][RW:2 * RW], 8),
                             fold(x["mu_shift"][0][2 * RW:3 * RW], 8)]
                            + [fold(x[q], 8) for q in ("k_k", "k_a", "r_k", "w0", "a0", "gn_g", "gn_b")], 2),
        "mu": fold(x["mu_shift"], RWC),
        "shiftT_in": np.stack([fold(x["state_shift"][0, b], RWC) for b in range(B)], 2),
        "wa_up": np.concatenate([x["w_up"][0], x["a_up"][0]]),
        "g_up": x["g_up"][0],
        "wkvT": across(x["state_wkv"][0].reshape(B, 8, 2, HD, HD).transpose(1, 2, 4, 0, 3)),
        **attention_layouts(x),
        "iota": np.broadcast_to(np.arange(NK), (P, NK)).astype(f),
        "peer_wq": chunked(x["peer_wq"][0], np.arange(D)),
        "subkeysT": x["peer_subkeys"][0].reshape(2 * PH, NK, P).transpose(0, 2, 1),
        "peer_u": x["peer_u"][0].reshape(NK, NK, KT, P).transpose(0, 3, 2, 1),
        "peer_v": x["peer_v"][0].reshape(NK // 2, 2, NK, 2, D // 2).transpose(0, 2, 3, 1, 4),
        "w_in": chunked(x["w_in"][0], in_columns()),
        "w_o": chunked(np.concatenate([x["w_o"][0][:RW], x["w_o"][0][RW:][q_order()]]), np.arange(D)),
    }
    return a


def outputs():
    return {"yT": (P, KT, N), "kvT": (P, 4, N), "kiT": (P, N), "shiftT": (P, RWC, B + 1),
            "wkvT_p": (8, P, HD), "wkvT_s": (8, P, B, HD)}


def kernel(**inputs):
    import concourse.bacc as bacc
    from concourse.bass_utils import run_bass_kernel_spmd as run

    x = {k: np.asarray(v) for k, v in inputs.items()}
    arrays = {k: np.ascontiguousarray(v) for k, v in layouts(x).items()}
    nc = bacc.Bacc("TRN2", target_bir_lowering=False, num_devices=1)
    a = {k: nc.dram_tensor(f"in_{k}", v.shape, mybir.dt.from_np(v.dtype), kind="ExternalInput").ap()
         for k, v in arrays.items()}
    o = {k: nc.dram_tensor(f"out_{k}", s, F32, kind="ExternalOutput").ap() for k, s in outputs().items()}
    build(nc, a, o)
    r = run(nc, [{f"in_{k}": v for k, v in arrays.items()}], core_ids=[0]).results[0]
    r = {k: np.asarray(r[f"out_{k}"]) for k in o}

    y = r["yT"].transpose(2, 1, 0).reshape(N, D)
    kv = r["kvT"].transpose(2, 1, 0).reshape(N, 2, KVH, HD)
    ki = r["kiT"].T
    shift = r["shiftT"].transpose(2, 1, 0).reshape(B + 1, RWC * P)[:, :RC]
    wkv_p = r["wkvT_p"].reshape(16, HD, HD).transpose(0, 2, 1)
    wkv_s = r["wkvT_s"].reshape(16, HD, B, HD).transpose(2, 0, 3, 1)
    c = np.ascontiguousarray
    return (c(y[META:TP])[None], c(y[TP:]).reshape(B, S, D),
            c(kv[:TP, 0])[None, None], c(kv[:TP, 1])[None, None], c(ki[:TP])[None, None],
            c(wkv_p)[None, None], c(shift[0])[None, None],
            c(kv[TP:, 0]).reshape(1, B, S, KVH, HD), c(kv[TP:, 1]).reshape(1, B, S, KVH, HD),
            c(ki[TP:]).reshape(1, B, S, ID), c(wkv_s)[None], c(shift[1:])[None])
```

```python
from contextlib import ExitStack, contextmanager

import numpy as np
import concourse.bass as bass
from concourse import mybir

F32 = mybir.dt.float32
F32R = mybir.dt.float32r
BF16 = mybir.dt.bfloat16
U32 = mybir.dt.uint32
I32 = mybir.dt.int32
ALU = mybir.AluOpType
ACT = mybir.ActivationFunctionType
AX = mybir.AxisListType.X

P = 128
D = 2048
KT = D // P
META, SEQ = 16, 256
TP = META + SEQ
B, S = 8, 4
TS = B * S
N = TP + TS
PAST, PAGE = 2048, 128
PAGES = PAST // PAGE
HD = 64
RW = 1024
RC = 3 * RW + 64 + 64 + 160
KVH, GROUP = 4, 4
IH, ID = 8, 128
TOPK_P = min(256, TP // 4)
TOPK_S = min(256, (PAST + S) // 4)
NB_BUCKETS, MAX_DIST = 32, 128
PH, NK, EK = 8, 128, 16
ALPHA = 2 ** 0.25
LN_EPS, GN_EPS = 1e-5, 64e-5
DECAY = float(np.exp(-0.5))

C_R, C_K, C_V, C_WA, C_G = 0, 8, 16, 24, 25
RWC = 27
C_Q, C_AK, C_AV, C_QI, C_KI, C_WI = 27, 35, 37, 39, 47, 48
NC_IN = 49

CH = 32
TILES = ((0, 128), (128, 128), (256, 48))
NEG = -1e30
PAD = -1e38
MARK = -3e38


class Ctx:

    def __init__(self, nc):
        self.nc = nc
        self.own = None

    def sem(self, name):
        s = self.own.enter_context(self.nc.semaphore(name))
        self.used.append(s)
        return s

    def count(self, name):
        s = self.sem(name)
        self.counts.append(s)
        return s

    def wait(self, eng, s, value, gate=None):
        assert any(s is c for c in self.counts)
        if gate is None:
            eng.wait_ge(s, value + 1)
        else:
            wait_loop(eng, s, value + 1, gate)

    @contextmanager
    def block(self):
        with self.nc.Block() as block:
            if self.counts:
                @block.gpsimd
                def _(pool):
                    for s in self.counts:
                        pool.sem_inc(s, 1)
            yield block

    def phase(self, build, *args, **kwargs):
        with ExitStack() as own:
            self.own, self.used, self.counts = own, [], []
            build(self, *args, **kwargs)
            used = self.used
            with self.nc.Block() as block:
                @block.sync
                def _(sp):
                    for s in used:
                        sp.sem_clear(s)


def wait_loop(eng, sem, value, gate):
    eng.wait_ge(sem, value)
    eng.sem_inc(gate, 1)


class Link:

    def __init__(self, eng, sem, gate=None):
        self.eng, self.sem, self.n, self.at, self.gate = eng, sem, 0, None, gate

    def value(self):
        return self.n if self.at is None else self.at + self.n

    def __call__(self, ins):
        ins.then_inc(self.sem, 1)
        self.n += 1
        if self.gate and self.at is not None:
            wait_loop(self.eng, self.sem, self.value(), self.gate)
        else:
            self.eng.wait_ge(self.sem, self.value())

    def enter(self, i, per):
        self.start, self.per = self.n, per
        self.at = i * per + self.start
        self.n = 0

    def leave(self, turns):
        assert self.n == self.per, (self.n, self.per)
        self.n, self.at = self.start + turns * self.per, None


def load_all(block_eng, nc, sem, pairs):
    n = 0
    for dst, src in pairs:
        block_eng.dma_start(dst, src).then_inc(sem, 16)
        n += 16
    return n


def load(cx, name, pairs):
    loaded = cx.sem(f"{name}_loaded")
    with cx.nc.Block() as block:
        @block.sync
        def _(sp):
            sp.wait_ge(loaded, load_all(sp, cx.nc, loaded, pairs))


def layer_norm(cx, name, xT, gb, ones, out=None, into=None):
    into = xT if into is None else into
    nc = cx.nc
    with ExitStack() as st:
        sq = st.enter_context(nc.sbuf_tensor(f"{name}_sq", [P, KT, N], F32))
        rs = st.enter_context(nc.sbuf_tensor(f"{name}_rs", [P, 3, N], F32))
        mean = st.enter_context(nc.psum_tensor(f"{name}_mean", [P, 512], F32))
        var = st.enter_context(nc.psum_tensor(f"{name}_var", [P, 512], F32))
        mean_done, centered, squared, var_done = (cx.sem(f"{name}_{x}") for x in
                                                  ("mean_done", "centered", "squared", "var_done"))
        inv_done, rstd_done, link = cx.sem(f"{name}_inv"), cx.sem(f"{name}_rstd"), cx.sem(f"{name}_link")
        stored = cx.sem(f"{name}_stored")
        scaled = cx.sem(f"{name}_scaled")
        with nc.Block() as block:
            @block.tensor
            def _(pe):
                for k in range(KT):
                    mm = pe.matmul(mean[:, 0:N], ones[:], xT[:, k, :], start=k == 0, stop=k == KT - 1)
                mm.then_inc(mean_done, 1)
                for k in range(KT):
                    pe.wait_ge(squared, k // 4 + 1)
                    mm = pe.matmul(var[:, 0:N], ones[:], sq[:, k, :], start=k == 0, stop=k == KT - 1)
                mm.then_inc(var_done, 1)

            @block.vector
            def _(v):
                lk = Link(v, link)
                v.wait_ge(mean_done, 1)
                lk(v.tensor_copy(rs[:, 2, :], mean[:, 0:N]))
                for q in range(4):
                    v.tensor_tensor(xT[:, 4 * q:4 * q + 4, :], xT[:, 4 * q:4 * q + 4, :],
                                    rs[:, 2:3, :].to_broadcast([P, 4, N]), ALU.subtract).then_inc(centered, 1)
                v.wait_ge(var_done, 1)
                lk(v.tensor_scalar(rs[:, 0, :], var[:, 0:N], LN_EPS, None, ALU.add))
                v.reciprocal(rs[:, 0, :], rs[:, 0, :]).then_inc(inv_done, 1)
                v.wait_ge(rstd_done, 1)
                v.wait_ge(centered, 4)
                for k in range(KT):
                    lk(v.scalar_tensor_tensor(xT[:, k, :], xT[:, k, :], gb[:, 0, k:k + 1], rs[:, 1, :],
                                              ALU.mult, ALU.mult))
                    v.tensor_scalar(into[:, k, :], xT[:, k, :], gb[:, 1, k:k + 1], None,
                                    ALU.add).then_inc(scaled, 1)

            @block.scalar
            def _(act):
                for q in range(4):
                    act.wait_ge(centered, q + 1)
                    act.activation(sq[:, 4 * q:4 * q + 4, :], xT[:, 4 * q:4 * q + 4, :],
                                   ACT.Square).then_inc(squared, 1)
                act.wait_ge(inv_done, 1)
                act.activation(rs[:, 1, :], rs[:, 0, :], ACT.Sqrt).then_inc(rstd_done, 1)

            if out is not None:
                @block.sync
                def _(sp):
                    sp.wait_ge(scaled, KT)
                    sp.dma_start(out, into[:]).then_inc(stored, 16)
                    sp.wait_ge(stored, 16)


def sbuf_both(nc, st, name, shape):
    at = -(-nc.sbuf_base // 32) * 32
    whole = st.enter_context(nc.sbuf_tensor(name, shape, F32))
    return whole, nc.alloc_sbuf_tensor_at(f"{name}_r", shape, F32R, offset=at)


def split(cx, name, whole, high, low):
    written, done = cx.sem(f"{name}_high"), cx.sem(f"{name}_low")
    with cx.nc.Block() as block:
        @block.scalar
        def _(act):
            for q in range(4):
                act.activation(high[:, 4 * q:4 * q + 4, :], whole[:, 4 * q:4 * q + 4, :], ACT.Copy).then_inc(written, 1)

        @block.vector
        def _(v):
            for q in range(4):
                v.wait_ge(written, q + 1)
                v.tensor_tensor(low[:, 4 * q:4 * q + 4, :], whole[:, 4 * q:4 * q + 4, :],
                                high[:, 4 * q:4 * q + 4, :], ALU.subtract).then_inc(done, 1)
            v.wait_ge(done, 4)


def split_product(pe, out, w_high, w_low, high, low, start, stop):
    pe.matmul(out, w_high, high, start=start, stop=False, skip_group_check=True)
    pe.matmul(out, w_high, low, start=False, stop=False, skip_group_check=True)
    return pe.matmul(out, w_low, high, start=False, stop=stop, skip_group_check=True)


def project(cx, name, chunks, w_dram, high, low, evacuate):
    nc = cx.nc
    SL = 4
    with ExitStack() as st:
        w, w_low = zip(*(sbuf_both(nc, st, f"{name}_w{s}", [P, KT, P]) for s in range(SL)))
        w_high = [st.enter_context(nc.sbuf_tensor(f"{name}_wh{s}", [P, KT, P], F32R)) for s in range(2)]
        acc = [st.enter_context(nc.psum_tensor(f"{name}_acc{s}", [P, 512], F32)) for s in range(SL)]
        loaded = [cx.sem(f"{name}_loaded{s}") for s in range(SL)]
        summed = [cx.count(f"{name}_summed{s}") for s in range(SL)]
        emptied = [cx.count(f"{name}_emptied{s}") for s in range(SL)]
        raised = [cx.sem(f"{name}_high{s}") for s in range(SL)]
        lowered = [cx.sem(f"{name}_low{s}") for s in range(SL)]

        def body(one, eng, count):
            full = count // SL
            with eng.Fori(0, full) as i:
                for s in range(SL):
                    one(i, s)
            for s in range(count % SL):
                one(full, s)

        with cx.block() as block:
            @block.sync
            def _(sp):
                def one(i, s):
                    cx.wait(sp, summed[s], i)
                    sp.dma_start(w[s][:], w_dram[i * SL + s]).then_inc(loaded[s], 16)
                body(one, sp, chunks)

            @block.scalar
            def _(act):
                def one(i, s):
                    act.wait_ge(loaded[s], i * 16 + 16)
                    cx.wait(act, summed[(s + 2) % SL], i + 1 if s >= 2 else i)
                    act.activation(w_high[s % 2][:], w[s][:], ACT.Copy).then_inc(raised[s], 1)
                body(one, act, chunks)

            @block.tensor
            def _(pe):
                def one(i, s):
                    pe.wait_ge(lowered[s], i + 1)
                    cx.wait(pe, emptied[s], i)
                    for k in range(KT):
                        mm = split_product(pe, acc[s][:, 0:N], w_high[s % 2][:, k, :], w_low[s][:, k, :],
                                           high[:, k, :], low[:, k, :], k == 0, k == KT - 1)
                    mm.then_inc(summed[s], 1)
                body(one, pe, chunks)

            @block.vector
            def _(v):
                def lower(i, s):
                    v.wait_ge(raised[s], i + 1)
                    v.tensor_tensor(w_low[s][:], w[s][:], w_high[s % 2][:], ALU.subtract).then_inc(lowered[s], 1)

                def out(i, s):
                    cx.wait(v, summed[s], i + 1)
                    evacuate(v, i * SL + s, acc[s][:, 0:N]).then_inc(emptied[s], 1)

                def one(i, s):
                    lower(*((i, s + 1) if s < SL - 1 else (i + 1, 0)))
                    out(i, s)
                lower(0, 0)
                body(one, v, chunks - 1)
                out((chunks - 1) // SL, (chunks - 1) % SL)


def build(nc, a, o):
    cx = Ctx(nc)
    with ExitStack() as top:
        def sb(name, shape, dt=F32, stack=top):
            return stack.enter_context(nc.sbuf_tensor(name, shape, dt))

        x_rest = nc.dram_tensor("x_rest", [P, KT, N], F32, kind="Internal").ap()
        mixT, before_mix = sbuf_both(nc, top, "mixT", [P, KT, N])
        ones = sb("ones", [P, P])
        ident = sb("ident", [P, P])
        ln_gb = sb("ln_gb", [P, 3, 2, KT])
        with ExitStack() as mixer:
            projT = sb("projT", [P, NC_IN, N], stack=mixer)
            with ExitStack() as early:
                xT, x_low = sbuf_both(nc, early, "x_inT", [P, KT, N])
                cx.phase(load, "first", ((xT[:], a["xT"]), (ones[:], a["ones"]), (ident[:], a["ident"]),
                                   (ln_gb[:], a["ln_gb"])))
                cx.phase(layer_norm, "ln_in", xT, ln_gb[:, 0], ones, out=x_rest)
                cx.phase(split, "x_in", xT, before_mix, x_low)
                cx.phase(project, "in", NC_IN, a["w_in"], before_mix, x_low,
                        lambda v, c, acc: v.tensor_copy(projT[:, c, :], acc))
            cx.phase(store_projection, projT, o)
            rwkv(cx, a, o, projT, mixT, ident)
            attention(cx, a, o, projT, mixT, ident)
        with ExitStack() as late:
            xT = sb("x_midT", [P, KT, N], stack=late)
            cx.phase(load, "rest", ((xT[:], x_rest),))
            high, low = sb("mix_high", [P, KT, N], F32R, late), sb("mix_low", [P, KT, N], F32R, late)
            cx.phase(split, "mix", mixT, high, low)
            cx.phase(project, "out", KT, a["w_o"], high, low,
                    lambda v, c, acc: v.scalar_tensor_tensor(xT[:, c, :], xT[:, c, :], ALPHA, acc,
                                                             ALU.mult, ALU.add))
            cx.phase(layer_norm, "ln1", xT, ln_gb[:, 1], ones, into=mixT)
        xT = mixT
        peer(cx, a, xT, ident)
        cx.phase(layer_norm, "ln2", xT, ln_gb[:, 2], ones, out=o["yT"])


def store_projection(cx, projT, o):
    nc = cx.nc
    with ExitStack() as st:
        last = st.enter_context(nc.sbuf_tensor("last_rows", [P, RWC, B + 1], F32))
        picked, stored = cx.sem("last_rows_picked"), cx.sem("projection_stored")
        with nc.Block() as block:
            @block.vector
            def _(v):
                v.tensor_copy(last[:], projT[:, 0:RWC, TP - 1:N:S]).then_inc(picked, 1)

            @block.sync
            def _(sp):
                sp.dma_start(o["kvT"], projT[:, C_AK:C_QI, :]).then_inc(stored, 16)
                sp.dma_start(o["kiT"], projT[:, C_KI, :]).then_inc(stored, 16)
                sp.wait_ge(picked, 1)
                sp.dma_start(o["shiftT"], last[:]).then_inc(stored, 16)
                sp.wait_ge(stored, 48)


def block_mask(seq):
    return (seq[:, None] == seq[None, :]).astype(np.float32)


def rwkv_masks():
    main = np.arange(P) // CH
    tail = np.concatenate([np.zeros(CH // 2), 10 + np.arange(TS) // S, 100 + np.arange(P - CH // 2 - TS)])
    whole = np.stack([block_mask(main), block_mask(main), block_mask(tail)])
    half = np.stack([block_mask(np.arange(P) // (CH // 2))] * 2 + [block_mask(tail)])
    s, t = np.arange(P)[:, None], np.arange(P)[None, :]
    which = [-half * (s < t), -half * (s > t), (whole - half) * (s < t), whole * (s < t), whole * (s <= t)]
    return np.stack(which).transpose(2, 0, 1, 3).astype(np.float32)


M_XT, M_X, M_OFF, M_LT, M_LE = range(5)

def rwkv_features(cx, a, projT, masks, seqmask, halves, cols, mu, shift, lw, la, ag, gg):
    nc = cx.nc
    NH = 8
    loaded, mixed, squashed, up_done, up_read = (cx.sem(f"rw_{x}") for x in
                                                 ("loaded", "mixed", "squashed", "up_done", "up_read"))
    link0 = cx.sem("rw_link0")

    def shifted(v, lk, out, feat, c0, nch):
        lk(v.tensor_tensor(out[:, :, 1:N], feat[:, :, 0:N - 1], feat[:, :, 1:N], ALU.subtract))
        lk(v.tensor_scalar(out[:, :, 0:1], feat[:, :, 0:1], -1.0, None, ALU.mult))
        lk(v.tensor_tensor(out[:, :, TP:N:S], shift[:, c0:c0 + nch, :], feat[:, :, TP:N:S], ALU.subtract))

    with ExitStack() as ps:
        def early(name, shape):
            return ps.enter_context(nc.sbuf_tensor(f"rw_{name}", shape, F32))

        w_up, g_up, g_up2 = early("w_up", [P, RW]), early("g_up", [P, RW]), early("g_up2", [32, RW])
        xl, dl = early("xl", [P, 3, N]), early("dl", [P, 3, N])
        lb = early("lb", [P, NH, N])
        block = ps.enter_context(nc.Block())
        up = [ps.enter_context(nc.psum_tensor(f"rw_up{i}", [P, 512], F32)) for i in range(2)]

        @block.sync
        def _(sp):
            n = load_all(sp, nc, loaded, (
                (masks[:], a["rw_masks"]), (seqmask[:], a["seqmask"]), (halves[:], a["halves"]),
                (cols[:], a["rw_cols"]), (mu[:], a["mu"]), (shift[:], a["shiftT_in"]),
                (w_up[:], a["wa_up"]), (g_up[:], a["g_up"][0:P]), (g_up2[:], a["g_up"][P:P + 32])))
            assert n == 144

        @block.vector
        def _(v):
            lk = Link(v, link0)
            v.wait_ge(loaded, 144)
            shifted(v, lk, dl, projT[:, C_WA:RWC, :], C_WA, 3)
            for c in range(3):
                v.scalar_tensor_tensor(xl[:, c, :], dl[:, c, :], mu[:, C_WA + c:C_WA + c + 1],
                                       projT[:, C_WA + c, :], ALU.mult, ALU.add).then_inc(mixed, 1)
            v.wait_ge(up_read, 3 * NH)
            lk(v.tensor_scalar(lw[:], lw[:], -DECAY, None, ALU.mult))
            src, dst = lw, la
            main = lambda q: q[:, :, 0:256].rearrange("p j (c t) -> p (j c) t", t=CH)
            for level, step in enumerate((1, 2, 4, 8, 16)):
                parts = []
                for j in range(NH):
                    parts.append((lambda q, j=j: q[:, j, 0:256].rearrange("p (c t) -> p c t", t=CH)))
                if step < 16:
                    parts.append(lambda q: q[:, :, 256:TP])
                if step < 4:
                    for j in range(NH):
                        parts.append((lambda q, j=j: q[:, j, TP:N].rearrange("p (c t) -> p c t", t=S)))
                lk(v.tensor_copy(dst[:], src[:]))
                for part in parts:
                    a_, b_ = part(dst), part(src)
                    lk(v.tensor_tensor(a_[:, :, step:], b_[:, :, step:], b_[:, :, :a_.shape[2] - step], ALU.add))
                src, dst = dst, (lb if dst is la else la)
            assert src is la

        @block.scalar
        def _(act):
            act.wait_ge(mixed, 3)
            act.activation(xl[0:HD, 0, :], xl[0:HD, 0, :], ACT.Tanh).then_inc(squashed, 1)
            act.activation(xl[:, 1, :], xl[:, 1, :], ACT.Sigmoid).then_inc(squashed, 1)
            act.activation(xl[0:32, 2, :], xl[0:32, 2, :], ACT.Sigmoid).then_inc(squashed, 1)
            for j in range(NH):
                for n, (dst, bias) in enumerate(((lw, 6), (ag, 7), (gg, None))):
                    u = 3 * j + n
                    act.wait_ge(up_done, u + 1)
                    if bias is None:
                        ins = act.activation(dst[:, j, :], up[u % 2][:, 0:N], ACT.Copy)
                    else:
                        ins = act.activation(dst[:, j, :], up[u % 2][:, 0:N], ACT.Sigmoid,
                                             bias=cols[:, j, bias:bias + 1])
                    ins.then_inc(up_read, 1)

        @block.tensor
        def _(pe):
            pe.wait_ge(loaded, 144)
            pe.wait_ge(squashed, 3)
            for j in range(NH):
                c = slice(j * P, j * P + P)
                for n in range(3):
                    u = 3 * j + n
                    if u >= 2:
                        pe.wait_ge(up_read, u - 1)
                    if n == 0:
                        mm = pe.matmul(up[u % 2][:, 0:N], w_up[0:HD, c], xl[0:HD, 0, :], start=True, stop=True)
                    elif n == 1:
                        mm = pe.matmul(up[u % 2][:, 0:N], w_up[HD:P, c], xl[HD:P, 0, :], start=True, stop=True)
                    else:
                        pe.matmul(up[u % 2][:, 0:N], g_up[:, c], xl[:, 1, :], start=True, stop=False)
                        mm = pe.matmul(up[u % 2][:, 0:N], g_up2[:, c], xl[0:32, 2, :], start=False, stop=True)
                    mm.then_inc(up_done, 1)


def rwkv(cx, a, o, projT, mixT, ident):
    nc = cx.nc
    NH = 8
    with ExitStack() as st:
        def sb(name, shape, dt=F32):
            return st.enter_context(nc.sbuf_tensor(f"rw_{name}", shape, dt))

        masks = sb("masks", [P, 5, 3, P])
        seqmask = sb("seqmask", [P, B])
        halves = sb("halves", [P, P])
        cols = sb("cols", [P, 8, 10])
        mu = sb("mu", [P, RWC])
        shift = sb("shift", [P, RWC, B])
        lw, ag, gg = sb("lw", [P, NH, N]), sb("ag", [P, NH, N]), sb("gg", [P, NH, N])
        la = sb("la", [P, NH, N])
        cx.phase(rwkv_features, a, projT, masks, seqmask, halves, cols, mu, shift, lw, la, ag, gg)
        cx.phase(rwkv_heads, a, o, projT, mixT, ident, masks, seqmask, halves, cols, shift, lw, la, ag)
        cx.phase(rwkv_finish, mixT, halves, cols, gg)


def rwkv_heads(cx, a, o, projT, mixT, ident, masks, seqmask, halves, cols, shift, lw, la, ag):
    nc = cx.nc
    NH = 8
    N3 = 3 * P
    pe_names = ["pairs", "lk", "x2", "x4", "x8", "rowsa", "t8", "rowsb", "pre", "a1", "z2", "wu", "mix",
                "q", "g", "gs"] + [f"state{c}" for c in range(9)] + ["samples"]
    dv_names = ["x", "lk", "x2", "x4", "t2", "x8", "t3", "rowsa", "rowsb", "kl", "a1",
                "z2", "wu", "mix", "g", "gs"] + [f"state{c}" for c in range(9)] + ["samples"]
    ft_names = ["products", "features"]
    ac_names = ["roots", "exps"]
    PREPARED = 5
    with ExitStack() as st:
        def sb(name, shape, dt=F32):
            return st.enter_context(nc.sbuf_tensor(f"rh_{name}", shape, dt))

        df = sb("df", [P, 3, N])
        rkv = sb("rkv", [P, 3, N3])
        xx = sb("xx", [P, 2, N])
        kk, kh, bh = sb("kk", [P, N]), sb("kh", [P, N]), sb("bh", [P, N])
        lbef = sb("lbef", [P, N])
        dec, decb, inv = sb("dec", [P, N]), sb("decb", [P, N]), sb("inv", [P, N])
        KT_, RT_, kT_, bT_ = sb("K", [P, N3]), sb("R", [P, N3]), sb("k", [P, N3]), sb("b", [P, N3])
        cs = sb("colsj", [P, 10])
        dend = sb("dend", [P, 9 + B])
        arena = sb("arena", [P, 11, 6 * P])
        X, XT, X4, WU, X4T, X2, X2T, T0, T1, OFF, LkT = (
            arena[:, n, :].rearrange("p (h t c) -> p h t c", h=2, t=3) for n in range(11))
        MkT, MbT = X, XT
        WU = arena[:, 3, :].rearrange("p (t a c) -> p t a c", t=3, a=2)
        late = arena[:].rearrange("p n c -> p (n c)")[:, 4 * 6 * P:]
        rows = sb("rows", [P, 4, 3, P])
        KL, A1 = X2, X2T
        QT = sb("QT", [P, N3])
        G = late[:, 0:9 * P].rearrange("p (c d) -> p c d", d=P)
        GS, bx, vx, ux = (late[:, (9 + 8 * n) * P:(17 + 8 * n) * P].rearrange("p (b d) -> p b d", d=P)
                          for n in range(4))
        state = sb("state", [P, 10, P])
        ss_in, ss_out = sb("ss_in", [P, B, P]), sb("ss_out", [P, B, P])
        twice = lambda name: st.enter_context(nc.psum_tensor(f"rh_{name}", [P, 2, 512], F32))
        once = lambda name: st.enter_context(nc.psum_tensor(f"rh_{name}", [P, 512], F32))
        pA, pB, pC, pY, pS = twice("pA"), twice("pB"), twice("pC"), once("pY"), once("pS")
        flat = lambda bank: bank[:].rearrange("p a c -> p (a c)")
        mats = lambda bank: bank[:, :, 0:3 * P].rearrange("p h (t c) -> p h t c", t=3)
        mat = lambda bank, t, h: bank[:, h, t * P:t * P + P]
        mask = lambda which: masks[:, which:which + 1, :, :].to_broadcast([P, 2, 3, P])
        pe_step, dv_step, ac_step = cx.sem("rh_pe_step"), cx.count("rh_dve_step"), cx.sem("rh_act_step")
        ft_step, normed = cx.sem("rh_feature_step"), cx.sem("rh_norms")
        link, gate = cx.sem("rh_link"), cx.sem("rh_gate")
        ss_loaded, stored = cx.sem("rh_ss_loaded"), cx.count("rh_stored")

        def at(names, i, name):
            return i * len(names) + names.index(name) + 1

        def stepper(sem, names):
            left = list(names)

            def done(ins, name):
                assert left.pop(0) == name, name
                ins.then_inc(sem, 1)
            return done, left

        halves_of = [(0, slice(0, HD)), (1, slice(HD, P))]
        tiles = range(3)

        def chunk_rows(c):
            n = CH if c < 8 else CH // 2
            return slice(c * CH, c * CH + n), c // 4, slice((c % 4) * CH, (c % 4) * CH + n)

        def every_pair(eng, turn):
            with eng.Fori(0, NH - 1) as i:
                turn(i, i + 1)
            turn(NH - 1, None)

        with cx.block() as block:
            @block.tensor
            def _(pe):
                def norms(j):
                    pe.wait_ge(ft_step, at(ft_names, j, "products"))
                    pe.matmul(pA[:, 0, 0:N], halves[:], xx[:, 0, :], start=True, stop=True)
                    pe.matmul(pA[:, 1, 0:N], halves[:], xx[:, 1, :], start=True, stop=True).then_inc(normed, 1)

                def turn(i, following):
                    done, left = stepper(pe_step, pe_names)
                    need = lambda name: cx.wait(pe, dv_step, at(dv_names, i, name))

                    def every(bank, lhs, rhs):
                        for t in tiles:
                            for h, r in halves_of:
                                mm = pe.matmul(mat(bank, t, h), lhs(t, h, r), rhs(t, h, r), start=True, stop=True)
                        return mm

                    feat = lambda q: (lambda t, h, r: q[r, t * P:t * P + P])
                    sq = lambda q: (lambda t, h, r: q[:, h, t, :])
                    pe.wait_ge(ft_step, at(ft_names, i, "features"))
                    every(pA, feat(bT_), feat(KT_))
                    done(every(pB, feat(KT_), feat(bT_)), "pairs")
                    done(every(pC, feat(kT_), feat(KT_)), "lk")
                    need("x")
                    every(pA, sq(XT), sq(X))
                    done(every(pB, sq(X), sq(XT)), "x2")
                    need("x2")
                    every(pA, sq(X2T), sq(X2))
                    every(pB, sq(X2), sq(X2T))
                    done(every(pC, sq(X2), sq(T0)), "x4")
                    need("x4")
                    need("t2")
                    every(pA, sq(X4T), sq(X4))
                    done(every(pC, sq(X4), sq(T1)), "x8")
                    for n, src in enumerate((KT_, kT_)):
                        for t in tiles:
                            at_ = (n * 3 + t) * P
                            mm = pe.transpose(pB[:, at_ // 512, at_ % 512:at_ % 512 + P], src[:, t * P:t * P + P],
                                              ident[:])
                    done(mm, "rowsa")
                    need("x8")
                    done(every(pC, sq(X2), sq(T0)), "t8")
                    need("rowsa")
                    for n, src in enumerate((bT_, rkv[:, 2, :])):
                        for t in tiles:
                            at_ = (n * 3 + t) * P
                            mm = pe.transpose(pB[:, at_ // 512, at_ % 512:at_ % 512 + P], src[:, t * P:t * P + P],
                                              ident[:])
                    done(mm, "rowsb")
                    need("rowsb")
                    for t in tiles:
                        for h, r in halves_of:
                            mm = pe.matmul(mat(pA, t, h)[:, 0:HD], LkT[:, h, t, :], rows[:, 3, t, r],
                                           start=True, stop=True)
                    done(mm, "pre")
                    need("t3")
                    need("kl")
                    done(every(pB, sq(T1), sq(KL)), "a1")
                    need("a1")
                    done(every(pA, sq(OFF), sq(A1)), "z2")
                    need("z2")
                    done(every(pB, sq(T1), sq(KL)), "wu")
                    every(pC, feat(kT_), feat(RT_))
                    done(every(pA, feat(bT_), feat(RT_)), "mix")
                    need("wu")
                    need("mix")
                    for h, r in halves_of:
                        for t in tiles:
                            mm = pe.matmul(pS[r, t * P:t * P + P], WU[:, t, 0, r], MbT[:, h, t, :],
                                           start=t == 0, stop=True, skip_group_check=True)
                    done(mm, "q")
                    gbank = (pB[:, 0], pB[:, 1], pC[:, 0], pC[:, 1])
                    for c in range(9):
                        _, t, cr = chunk_rows(c)
                        mm = pe.matmul(gbank[c % 4][:, (c // 4) * P:(c // 4) * P + P], WU[cr, t, 0, :],
                                       rows[cr, 2, t, :], start=True, stop=True)
                    done(mm, "g")
                    for q in range(2):
                        mm = pe.matmul(pA[:, q, :], WU[:, 2, 0, :], bx[:, 4 * q:4 * q + 4, :].rearrange("p b d -> p (b d)"),
                                       start=True, stop=True)
                    done(mm, "gs")
                    for h, r in halves_of:
                        for t in tiles:
                            pe.matmul(pY[r, t * P:t * P + P], rows[:, 3, t, r], MkT[:, h, t, :],
                                      start=t == 0, stop=False, skip_group_check=True)
                            pe.matmul(pY[r, t * P:t * P + P], WU[:, t, 1, r], MbT[:, h, t, :],
                                      start=False, stop=False, skip_group_check=True)
                    sums = (pS[:, 0:P], pB[:, 0, 0:P])

                    def begin(c):
                        _, t, cr = chunk_rows(c)
                        pe.matmul(sums[c % 2], rows[cr, 1, t, :], rows[cr, 3, t, :], start=True, stop=False)
                        pe.matmul(sums[c % 2], rows[cr, 2, t, :], WU[cr, t, 1, :], start=False, stop=False)

                    def samples(c):
                        if c == 0:
                            need("gs")
                            pe.wait_ge(ss_loaded, i * 16 + 16)
                        if c < 2:
                            four = lambda x: x[:, 4 * c:4 * c + 4, :].rearrange("p b d -> p (b d)")
                            pe.matmul(pC[:, c, :], rows[:, 1, 2, :], four(vx), start=True, stop=False,
                                      skip_group_check=True)
                            pe.matmul(pC[:, c, :], rows[:, 2, 2, :], four(ux), start=False, stop=False,
                                      skip_group_check=True)
                        elif c < 6:
                            for b in (2 * c - 4, 2 * c - 3):
                                toks = slice(TP + b * S, TP + b * S + S)
                                pe.matmul(pC[:, b // 4, (b % 4) * P:(b % 4) * P + P], GS[:, b, :], ss_in[:, b, :],
                                          start=False, stop=True, skip_group_check=True)
                                pe.matmul(pY[:, toks], ss_in[:, b, :], QT[:, toks], start=False, stop=True,
                                          skip_group_check=True)

                    need("g")
                    begin(0)
                    for c in range(9):
                        toks, t, cr = chunk_rows(c)
                        if c:
                            need(f"state{c - 1}")
                        done(pe.matmul(sums[c % 2], G[:, c, :], state[:, c, :], start=False, stop=True), f"state{c}")
                        mm = pe.matmul(pY[:, toks], state[:, c, :], QT[:, toks], start=False, stop=True,
                                       skip_group_check=True)
                        if c < 8:
                            begin(c + 1)
                            samples(c)
                        if c == PREPARED - 1 and following is not None:
                            norms(following)
                    done(mm, "samples")
                    assert not left
                norms(0)
                every_pair(pe, turn)

            @block.scalar
            def _(act):
                def features(j, before):
                    done, left = stepper(ac_step, ac_names)
                    act.wait_ge(normed, j + 1)
                    done(act.activation(bh[:], pA[:, 0, 0:N], ACT.Sqrt), "roots")
                    if before is not None:
                        cx.wait(act, dv_step, at(dv_names, before, "g"))
                    act.activation(dec[:], la[:, j, :], ACT.Exp)
                    act.activation(inv[:], la[:, j, :], ACT.Exp, scale=-1.0)
                    done(act.activation(decb[:], lbef[:], ACT.Exp), "exps")
                features(0, None)
                with act.Fori(0, NH - 1) as i:
                    features(i + 1, i)

            @block.vector
            def _(v):
                lk = Link(v, link)
                for q in (KT_, RT_, kT_, bT_):
                    lk(v.memset(q[:, N:N3], 0.0))
                lk(v.memset(rkv[:, :, N:N3], 0.0))
                lk(v.memset(state[:, 0, :], 0.0))
                proj3 = projT[:, 0:24, :].rearrange("p (a j) n -> p a j n", j=NH)
                shift3 = shift[:, 0:24, :].rearrange("p (a j) b -> p a j b", j=NH)
                r_, k_, v_ = (rkv[:, n, 0:N] for n in range(3))

                def ft_done(ins, j, name):
                    ins.then_inc(ft_step, 1)
                    v.wait_ge(ft_step, at(ft_names, j, name))

                def products(j, part):
                    f = proj3[:, :, j, :]
                    if part == 0:
                        lk(v.tensor_copy(cs[:], cols[:, j, :]))
                        lk(v.tensor_tensor(df[:, :, 1:N], f[:, :, 0:N - 1], f[:, :, 1:N], ALU.subtract))
                        lk(v.tensor_scalar(df[:, :, 0:1], f[:, :, 0:1], -1.0, None, ALU.mult))
                        lk(v.tensor_tensor(df[:, :, TP:N:S], shift3[:, :, j, :], f[:, :, TP:N:S], ALU.subtract))
                    elif part == 1:
                        for n in range(2):
                            lk(v.scalar_tensor_tensor(rkv[:, n, 0:N], df[:, n, :], cs[:, n:n + 1], f[:, n, :],
                                                      ALU.mult, ALU.add))
                    elif part == 2:
                        lk(v.scalar_tensor_tensor(rkv[:, 2, 0:N], df[:, 2, :], cs[:, 2:3], f[:, 2, :],
                                                  ALU.mult, ALU.add))
                        lk(v.tensor_tensor(lbef[:], la[:, j, :], lw[:, j, :], ALU.subtract))
                    elif part == 3:
                        lk(v.tensor_scalar(kk[:], k_, cs[:, 3:4], None, ALU.mult))
                        lk(v.tensor_tensor(xx[:, 0, :], kk[:], kk[:], ALU.mult))
                    else:
                        lk(v.tensor_scalar(kh[:], ag[:, j, :], -1.0, cs[:, 4:5], ALU.add, ALU.mult))
                        lk(v.scalar_tensor_tensor(kh[:], kh[:], 1.0, k_, ALU.add, ALU.mult))
                        ft_done(v.scalar_tensor_tensor(xx[:, 1, :], r_, cs[:, 5:6], kh[:], ALU.mult, ALU.mult),
                                j, "products")

                def features(j):
                    v.wait_ge(ac_step, at(ac_names, j, "exps"))
                    lk(v.tensor_scalar(bh[:], bh[:], 1e-12, None, ALU.max))
                    lk(v.reciprocal(bh[:], bh[:]))
                    lk(v.tensor_tensor(kk[:], kk[:], bh[:], ALU.mult))
                    lk(v.tensor_tensor(mixT[:, 8:16][:, j, :], v_, pA[:, 1, 0:N], ALU.mult))
                    lk(v.tensor_tensor(KT_[:, 0:N], kk[:], decb[:], ALU.mult))
                    lk(v.tensor_tensor(bh[:], kk[:], ag[:, j, :], ALU.mult))
                    lk(v.tensor_tensor(RT_[:, 0:N], r_, dec[:], ALU.mult))
                    lk(v.tensor_tensor(kT_[:, 0:N], kh[:], inv[:], ALU.mult))
                    ft_done(v.tensor_tensor(bT_[:, 0:N], bh[:], inv[:], ALU.mult), j, "features")

                def turn(i, following):
                    signal, left = stepper(dv_step, dv_names)

                    def done(ins, name):
                        signal(ins, name)
                        cx.wait(v, dv_step, at(dv_names, i, name))
                    need = lambda name: v.wait_ge(pe_step, at(pe_names, i, name))
                    need("pairs")
                    lk(v.tensor_tensor(XT[:], mats(pA), mask(M_XT), ALU.mult))
                    lk(v.tensor_tensor(OFF[:], mats(pA), mask(M_OFF), ALU.mult))
                    lk(v.tensor_tensor(T0[:], XT[:], ident[:].rearrange("p (a b c) -> p a b c", a=1, b=1)
                                       .to_broadcast([P, 2, 3, P]), ALU.add))
                    done(v.tensor_tensor(X[:], mats(pB), mask(M_X), ALU.mult), "x")
                    need("lk")
                    done(v.tensor_tensor(LkT[:], mats(pC), mask(M_LT), ALU.mult), "lk")
                    need("x2")
                    lk(v.tensor_copy(X2[:], mats(pA)))
                    done(v.tensor_copy(X2T[:], mats(pB)), "x2")
                    need("x4")
                    lk(v.tensor_copy(X4[:], mats(pA)))
                    done(v.tensor_copy(X4T[:], mats(pB)), "x4")
                    done(v.tensor_tensor(T1[:], T0[:], mats(pC), ALU.add), "t2")
                    need("x8")
                    lk(v.tensor_copy(X2[:], mats(pA)))
                    done(v.tensor_tensor(T0[:], T1[:], mats(pC), ALU.add), "x8")
                    need("t8")
                    done(v.tensor_tensor(T1[:], T0[:], mats(pC), ALU.add), "t3")
                    need("rowsa")
                    both = flat(pB)[:, 0:6 * P].rearrange("p (n t c) -> p n t c", n=2, t=3)
                    done(v.tensor_copy(rows[:, 0:2], both), "rowsa")
                    need("rowsb")
                    done(v.tensor_copy(rows[:, 2:4], both), "rowsb")
                    need("pre")
                    lk(v.tensor_copy(KL[:, :, :, 0:HD], rows[:, 0].rearrange("p t (h c) -> p h t c", h=2)))
                    done(v.tensor_copy(KL[:, :, :, HD:P], mats(pA)[:, :, :, 0:HD]), "kl")
                    need("a1")
                    done(v.tensor_copy(A1[:], mats(pB)), "a1")
                    need("z2")
                    done(v.tensor_tensor(KL[:], KL[:], mats(pA), ALU.subtract), "z2")
                    need("wu")
                    w4 = WU.rearrange("p t a (h d) -> p a h t d", h=2)
                    lk(v.tensor_scalar(w4[:, 0], mats(pB)[:, :, :, 0:HD], -1.0, None, ALU.mult))
                    done(v.tensor_scalar(w4[:, 1], mats(pB)[:, :, :, HD:P], -1.0, None, ALU.mult), "wu")
                    seq = seqmask[:].rearrange("p (b o) -> p b o", o=1).to_broadcast([P, B, P])
                    for dst, src in ((bx, rows[:, 2, 2:3, :]), (vx, rows[:, 3, 2:3, :]), (ux, WU[:, 2:3, 1, :])):
                        lk(v.tensor_tensor(dst[:], src.to_broadcast([P, B, P]), seq, ALU.mult))
                    need("mix")
                    lk(v.tensor_tensor(MkT[:], mats(pC), mask(M_LE), ALU.mult))
                    done(v.tensor_tensor(MbT[:], mats(pA), mask(M_LE), ALU.mult), "mix")
                    lk(v.tensor_copy(dend[:, 0:8], dec[:, CH - 1:8 * CH:CH]))
                    lk(v.tensor_copy(dend[:, 8:9], dec[:, TP - 1:TP]))
                    lk(v.tensor_copy(dend[:, 9:9 + B], dec[:, TP + S - 1:N:S]))
                    need("q")
                    lk(v.tensor_tensor(QT[:], RT_[:], pS[:, 0:N3], ALU.add))
                    one = ident[:].rearrange("p (o d) -> p o d", o=1)
                    need("g")
                    for q, bank in enumerate((pB[:, 0], pB[:, 1], pC[:, 0], pC[:, 1])):
                        n = 3 if q == 0 else 2
                        ins = v.tensor_tensor(G[:, q:9:4, :], bank[:, 0:n * P].rearrange("p (c d) -> p c d", d=P),
                                              one.to_broadcast([P, n, P]), ALU.add)
                    done(ins, "g")
                    need("gs")
                    done(v.tensor_tensor(GS[:], pA[:].rearrange("p a (c d) -> p (a c) d", d=P),
                                         one.to_broadcast([P, B, P]), ALU.add), "gs")
                    cx.wait(v, stored, i * 64)
                    for c in range(9):
                        if c < PREPARED and following is not None:
                            products(following, c)
                        need(f"state{c}")
                        done(v.scalar_tensor_tensor(state[:, c + 1, :], (pS[:, 0:P], pB[:, 0, 0:P])[c % 2],
                                                    dend[:, c:c + 1], halves[:], ALU.mult, ALU.mult), f"state{c}")
                    need("samples")
                    lk(v.tensor_tensor(ss_out[:], pC[:].rearrange("p a (c d) -> p (a c) d", d=P),
                                       dend[:, 9:9 + B].rearrange("p (b o) -> p b o", o=1)
                                       .to_broadcast([P, B, P]), ALU.mult))
                    done(v.tensor_copy(mixT[:, 0:8][:, i, :], pY[:, 0:N]), "samples")
                    if following is not None:
                        features(following)
                    assert not left
                for part in range(PREPARED):
                    products(0, part)
                features(0)
                with v.Fori(0, NH - 1) as i:
                    lk.enter(i, LINKS_RW)
                    turn(i, i + 1)
                    lk.leave(NH - 1)
                turn(NH - 1, None)

            @block.sync
            def _(sp):
                with sp.Fori(0, NH) as i:
                    sp.dma_start(ss_in[:], a["wkvT"][i]).then_inc(ss_loaded, 16)
                    cx.wait(sp, dv_step, at(dv_names, i, "samples"))
                    for h, r in halves_of:
                        sp.dma_start(o["wkvT_s"][i, r], ss_out[r, :, r]).then_inc(stored, 16)
                        sp.dma_start(o["wkvT_p"][i, r], state[r, 9, r]).then_inc(stored, 16)
                    cx.wait(sp, stored, i * 64 + 64, gate)


LINKS_RW = 37


def rwkv_finish(cx, mixT, halves, cols, gg):
    nc = cx.nc
    with ExitStack() as st:
        sq = st.enter_context(nc.sbuf_tensor("rf_sq", [P, 2, N], F32))
        rs = st.enter_context(nc.sbuf_tensor("rf_rs", [P, 2, N], F32))
        pm = [st.enter_context(nc.psum_tensor(f"rf_m{k}", [P, 512], F32)) for k in range(2)]
        pv = [st.enter_context(nc.psum_tensor(f"rf_v{k}", [P, 512], F32)) for k in range(2)]
        mean, squared, var, inv, root, link, centered = (cx.sem(f"rf_{q}") for q in
            ("mean", "squared", "var", "inv", "root", "link", "centered"))
        with nc.Block() as block:
            @block.tensor
            def _(pe):
                for j in range(8):
                    if j >= 2:
                        pe.wait_ge(centered, j - 1)
                    pe.matmul(pm[j % 2][:, 0:N], halves[:], mixT[:, j, :], start=True, stop=True).then_inc(mean, 1)
                    pe.wait_ge(squared, j + 1)
                    if j >= 2:
                        pe.wait_ge(inv, j - 1)
                    pe.matmul(pv[j % 2][:, 0:N], halves[:], sq[:, j % 2, :], start=True, stop=True).then_inc(var, 1)

            @block.vector
            def _(v):
                lk = Link(v, link)
                for j in range(8):
                    y = mixT[:, j, :]
                    v.wait_ge(mean, j + 1)
                    v.scalar_tensor_tensor(y, pm[j % 2][:, 0:N], -1.0 / HD, y, ALU.mult, ALU.add).then_inc(centered, 1)
                    v.wait_ge(var, j + 1)
                    lk(v.tensor_scalar(rs[:, 0, :], pv[j % 2][:, 0:N], 1.0 / HD, GN_EPS, ALU.mult, ALU.add))
                    v.reciprocal(rs[:, 0, :], rs[:, 0, :]).then_inc(inv, 1)
                    v.wait_ge(root, j + 1)
                    lk(v.scalar_tensor_tensor(y, y, cols[:, j, 8:9], rs[:, 1, :], ALU.mult, ALU.mult))
                    lk(v.scalar_tensor_tensor(y, y, cols[:, j, 9:10], mixT[:, 8 + j, :], ALU.add, ALU.add))
                    lk(v.tensor_tensor(y, y, gg[:, j, :], ALU.mult))

            @block.scalar
            def _(act):
                for j in range(8):
                    act.wait_ge(centered, j + 1)
                    act.activation(sq[:, j % 2, :], mixT[:, j, :], ACT.Square).then_inc(squared, 1)
                    act.wait_ge(inv, j + 1)
                    act.activation(rs[:, 1, :], rs[:, 0, :], ACT.Sqrt).then_inc(root, 1)


FAR = PAST - PAGE
QT_TILES = ((0, 128), (128, 128), (256, 16))
WORK_S = PAST + S + 8


def bucket(dist):
    exact = NB_BUCKETS // 2
    d = np.maximum(dist, 0)
    far = exact + (np.log(np.maximum(d, 1).astype(np.float32) / exact) / np.log(MAX_DIST / exact)
                   * (NB_BUCKETS - exact)).astype(np.int32)
    return np.where(d < exact, d, np.minimum(far, NB_BUCKETS - 1))


def attention(cx, a, o, projT, mixT, ident):
    nc = cx.nc
    bias_rows = nc.dram_tensor("bias_rows", [16, 2 * TP], F32, kind="Internal").ap()
    with ExitStack() as st:
        def sb(name, shape, dt=F32):
            return st.enter_context(nc.sbuf_tensor(f"at_{name}", shape, dt))

        wrow = sb("wrow", [P, 3, IH])
        wsel = sb("wsel", [TS, B, TS])
        vrows = sb("vrows", [P, 3, 2 * P])
        vnew = sb("vnew", [S, B, 2 * P])
        mask_p = sb("mask_p", [P, 3, TP])
        mask_s = sb("mask_s", [TS + 1, PAST + S])
        sel = sb("sel", [TS + 1, B, 64])
        near = sb("near", [P, 64])
        rel = sb("rel", [P, 16])
        onehot = sb("onehot", [P, PAGE + S])
        cx.phase(attention_tables, a, projT, ident, bias_rows, wrow, wsel, vrows, vnew, sel, near, rel, onehot)
        cx.phase(index_prompt, a, projT, wrow, mask_p)
        cx.phase(attend_prompt, a, projT, mixT, ident, mask_p, vrows, bias_rows)
        cx.phase(index_sampled, a, projT, wsel, mask_s)
        cx.phase(attend_sampled, a, projT, mixT, ident, mask_s, sel, near, onehot, vnew)


def attention_tables(cx, a, projT, ident, bias_rows, wrow, wsel, vrows, vnew, sel, near, rel, onehot):
    nc = cx.nc
    with ExitStack() as st:
        def sb(name, shape, dt=F32):
            return st.enter_context(nc.sbuf_tensor(f"tb_{name}", shape, dt))

        pv = st.enter_context(nc.psum_tensor("tb_pv", [P, 2, 512], F32))
        pn = st.enter_context(nc.psum_tensor("tb_pn", [P, 4, 512], F32))
        pw = st.enter_context(nc.psum_tensor("tb_pw", [P, 512], F32))
        pr = st.enter_context(nc.psum_tensor("tb_pr", [P, 512], F32))
        spread = sb("spread", [IH, TS])
        wpick = sb("wpick", [TS, B, TS])
        spick = sb("spick", [P, 16, S])
        table = sb("table", [NB_BUCKETS, 2 * TP])
        brow = sb("brow", [16, 2 * TP])
        far = sb("far", [TS + 1, 16])
        loaded, turned, biased, moved, brow_done, stored = (cx.sem(f"tb_{x}") for x in
                                                    ("loaded", "turned", "biased", "moved", "brow", "stored"))
        with nc.Block() as block:
            @block.sync
            def _(sp):
                rb = a["rel_bias"]
                n = load_all(sp, nc, loaded, (
                    (spread[:], a["spread"]), (wpick[:], a["wpick"]), (spick[:], a["spick"]),
                    (table[:], a["bucket_table"]), (sel[0:TS], a["sel"]), (onehot[:], a["near_onehot"]),
                    (far[TS:TS + 1, :], rb[NB_BUCKETS - 1:NB_BUCKETS, :]),
                    *((rel[s * 32:s * 32 + 32, :], rb) for s in range(S))))
                assert n == 176
                sp.wait_ge(brow_done, 2)
                sp.dma_start(bias_rows, brow[:]).then_inc(stored, 16)
                sp.wait_ge(stored, 16)

            @block.tensor
            def _(pe):
                pe.wait_ge(loaded, 176)
                for t, (t0, m) in enumerate(QT_TILES):
                    pe.transpose(pw[0:m, t * 8:t * 8 + 8], projT[0:IH, C_WI, t0:t0 + m], ident[0:IH, 0:IH])
                pe.matmul(pw[0:TS, 64:64 + TS], spread[:], projT[0:IH, C_WI, TP:N], start=True, stop=True)
                for t, (t0, m) in enumerate(QT_TILES):
                    for p in range(2):
                        q = (2 * t + p) * P
                        pe.transpose(pv[0:m, q // 512, q % 512:q % 512 + P], projT[:, C_AV + p, t0:t0 + m], ident[:])
                for b in range(B):
                    for p in range(2):
                        q = (2 * b + p) * P
                        mm = pe.transpose(pn[0:S, q // 512, q % 512:q % 512 + P],
                                          projT[:, C_AV + p, TP + b * S:TP + b * S + S], ident[:])
                mm.then_inc(turned, 1)
                for h in range(2):
                    if h:
                        pe.wait_ge(brow_done, 1)
                    pe.matmul(pr[0:16, 0:TP], rel[0:NB_BUCKETS, :], table[:, h * TP:h * TP + TP],
                              start=True, stop=True).then_inc(biased, 1)

            @block.vector
            def _(v):
                v.wait_ge(turned, 1)
                for t, (t0, m) in enumerate(QT_TILES):
                    v.tensor_copy(wrow[0:m, t, :], pw[0:m, t * 8:t * 8 + 8])
                    for p in range(2):
                        q = (2 * t + p) * P
                        v.tensor_copy(vrows[0:m, t, p * P:p * P + P], pv[0:m, q // 512, q % 512:q % 512 + P])
                v.tensor_tensor(wsel[:], wpick[:], pw[0:TS, 64:64 + TS].rearrange("p (o n) -> p o n", o=1)
                                .to_broadcast([TS, B, TS]), ALU.mult)
                v.tensor_copy(vnew[:].rearrange("p b c -> p (b c)"), pn[0:S].rearrange("p a c -> p (a c)"))
                v.tensor_tensor(near[:].rearrange("p (h s) -> p h s", s=S), spick[:],
                                rel[:].rearrange("p (h o) -> p h o", o=1).to_broadcast([P, 16, S]), ALU.mult)
                for b in range(B):
                    v.tensor_copy(sel[TS:TS + 1, b, :].rearrange("p (h s) -> p h s", s=S),
                                  far[TS:TS + 1, :].rearrange("p (h o) -> p h o", o=1).to_broadcast([1, 16, S]))
                for h in range(2):
                    v.wait_ge(biased, h + 1)
                    v.tensor_copy(brow[:, h * TP:h * TP + TP], pr[0:16, 0:TP]).then_inc(brow_done, 1)


def take_top(v, lk, best, work, rounds, last=None):
    for n in range(rounds):
        lk(v.max(best, work))
        lk(v.match_replace(work, best, work, MARK))
    if last:
        lk(v.max(best, work))
        lk(v.memset(best[:, last:8], PAD))
        lk(v.match_replace(work, best, work, MARK))


def index_prompt(cx, a, projT, wrow, mask_p):
    nc = cx.nc
    with ExitStack() as st:
        def sb(name, shape, dt=F32):
            return st.enter_context(nc.sbuf_tensor(f"ip_{name}", shape, dt))

        relu = [sb(f"relu{k}", [P, TP]) for k in range(3)]
        work = sb("work", [P, 3, TP + 8])
        causal = sb("causal", [P, 3, TP])
        best = sb("best", [P, 8])
        banks = [st.enter_context(nc.psum_tensor(f"ip_p{k}", [P, 512], F32)) for k in range(4)]
        loaded, scored, relued, added, link = (cx.sem(f"ip_{x}") for x in
                                               ("loaded", "scored", "relued", "added", "link"))
        with nc.Block() as block:
            @block.sync
            def _(sp):
                sp.dma_start(causal[:], a["causal"]).then_inc(loaded, 16)

            @block.tensor
            def _(pe):
                for t, (t0, m) in enumerate(QT_TILES):
                    for h in range(IH):
                        u = t * IH + h
                        if u >= 4:
                            pe.wait_ge(relued, u - 3)
                        pe.matmul(banks[u % 4][0:m, 0:TP], projT[:, C_QI + h, t0:t0 + m], projT[:, C_KI, 0:TP],
                                  start=True, stop=True).then_inc(scored, 1)

            @block.scalar
            def _(act):
                for t, (t0, m) in enumerate(QT_TILES):
                    for h in range(IH):
                        u = t * IH + h
                        act.wait_ge(scored, u + 1)
                        if u >= 3:
                            act.wait_ge(added, u - 2)
                        act.activation(relu[u % 3][0:m, :], banks[u % 4][0:m, 0:TP], ACT.Relu).then_inc(relued, 1)

            @block.vector
            def _(v):
                lk = Link(v, link)
                v.wait_ge(loaded, 16)
                lk(v.memset(work[:, :, TP:TP + 8], PAD))
                for t, (t0, m) in enumerate(QT_TILES):
                    w = work[0:m, t, 0:TP]
                    for h in range(IH):
                        u = t * IH + h
                        v.wait_ge(relued, u + 1)
                        if h:
                            v.wait_ge(added, u)
                        prev = w if h else causal[0:m, t, :]
                        v.scalar_tensor_tensor(w, relu[u % 3][0:m, :], wrow[0:m, t, h:h + 1], prev,
                                               ALU.mult, ALU.add).then_inc(added, 1)
                    v.wait_ge(added, t * IH + IH)
                    take_top(v, lk, best[0:m, :], work[0:m, t, :], TOPK_P // 8, TOPK_P % 8)
                    lk(v.tensor_scalar(mask_p[0:m, t, :], w, MARK / 2, NEG, ALU.is_gt, ALU.mult))
                    lk(v.tensor_tensor(mask_p[0:m, t, :], mask_p[0:m, t, :], causal[0:m, t, :], ALU.add))


def attend_prompt(cx, a, projT, mixT, ident, mask_p, vrows, bias_rows):
    nc = cx.nc
    with ExitStack() as st:
        def sb(name, shape, dt=F32):
            return st.enter_context(nc.sbuf_tensor(f"pp_{name}", shape, dt))

        bias = sb("bias", [P, 3, 16, TP])
        flip = sb("flip", [P, 2, P])
        qs = [sb(f"q{k}", [P, TP]) for k in range(2)]
        prob = [sb(f"prob{k}", [P, TP]) for k in range(2)]
        stat = [sb(f"stat{k}", [P, 4]) for k in range(2)]
        pT = [sb(f"pT{k}", [P, 3, TP]) for k in range(2)]
        banks = [st.enter_context(nc.psum_tensor(f"pp_s{k}", [P, 512], F32)) for k in range(3)]
        tbank = [st.enter_context(nc.psum_tensor(f"pp_t{k}", [P, 512], F32)) for k in range(2)]
        obank = [st.enter_context(nc.psum_tensor(f"pp_o{k}", [P, 512], F32)) for k in range(2)]
        names = ("loaded", "staged", "scored", "maxed", "exped", "normed", "turned", "moved", "summed", "mixed", "link", "zeroed", "gate")
        loaded, staged, scored, maxed, exped, normed, turned, moved, summed, mixed, link, zeroed, gate = (
            (cx.count if x in ("scored", "exped") else cx.sem)(f"pp_{x}") for x in names)
        U = 6
        units = [(t, hf) for t in range(3) for hf in range(2)]

        def every_chunk(eng, one):
            for p in range(2):
                with eng.Fori(0, 2) as gi:
                    for k in range(2):
                        one(p, gi * 2 + k, gi * 2 + (p * 4 + k), k)

        with cx.block() as block:
            @block.sync
            def _(sp):
                sp.dma_start(flip[:], a["flip"]).then_inc(loaded, 16)
                sp.wait_ge(zeroed, 3)
                for t, (t0, m) in enumerate(QT_TILES):
                    base = bias_rows[:, TP - t0 - m:]
                    src = bass.AP(base.tensor, base.offset, [[1, m], [2 * TP, 16], [1, TP]])
                    sp.dma_start(bias[0:m, t], src).then_inc(loaded, 16)

            @block.vector
            def _(v):
                def one(p, g, n, k):
                    cx.wait(v, scored, n * U)
                    v.tensor_scalar(qs[k][:], projT[:, C_Q + p * 4:C_Q + p * 4 + 4, 0:TP][:, g, :], HD ** -0.5, None,
                                    ALU.mult).then_inc(staged, 1)
                    for u, (t, hf) in enumerate(units):
                        t0, m = QT_TILES[t]
                        w = t0 + m
                        at = n * U + u
                        s = banks[u % 3]
                        cx.wait(v, scored, at + 1)
                        v.tensor_reduce(stat[u % 2][0:m, 0:1], s[0:m, 0:w], AX, ALU.max).then_inc(link, 1)
                        v.wait_ge(link, at * 2 + 1)
                        v.tensor_scalar(stat[u % 2][0:m, 1:2], stat[u % 2][0:m, 0:1], -1.0, None,
                                        ALU.mult).then_inc(maxed, 1)
                        cx.wait(v, exped, at + 1)
                        v.reciprocal(stat[u % 2][0:m, 3:4], stat[u % 2][0:m, 2:3]).then_inc(link, 1)
                        v.wait_ge(link, at * 2 + 2)
                        v.tensor_scalar(prob[u % 2][0:m, 0:w], prob[u % 2][0:m, 0:w], stat[u % 2][0:m, 3:4], None,
                                        ALU.mult).then_inc(normed, 1)
                        v.wait_ge(turned, at + 1)
                        v.tensor_copy(pT[hf][:, 0:t + 1, t0:w],
                                      tbank[u % 2][:, 0:(t + 1) * m].rearrange("p (k q) -> p k q", q=m)) \
                            .then_inc(moved, 1)
                    v.wait_ge(summed, n + 1)
                    v.tensor_copy(mixT[:, 8 + p * 4:12 + p * 4, 0:TP][:, g, :], obank[k][:, 0:TP]).then_inc(mixed, 1)
                v.memset(bias[:, 2], 0.0).then_inc(zeroed, 1)
                for k in range(2):
                    v.memset(pT[k][:], 0.0).then_inc(zeroed, 1)
                v.wait_ge(zeroed, 3)
                every_chunk(v, one)

            @block.scalar
            def _(act):
                def one(p, g, n, k):
                    for u, (t, hf) in enumerate(units):
                        t0, m = QT_TILES[t]
                        act.wait_ge(maxed, n * U + u + 1)
                        act.activation(prob[u % 2][0:m, 0:t0 + m], banks[u % 3][0:m, 0:t0 + m], ACT.Exp,
                                       bias=stat[u % 2][0:m, 1:2], accum_out=stat[u % 2][0:m, 2:3]) \
                            .then_inc(exped, 1)
                every_chunk(act, one)

            @block.tensor
            def _(pe):
                pe.wait_ge(loaded, 64)
                pe.wait_ge(zeroed, 3)

                def score(p, g, n, k, u):
                    t, hf = units[u]
                    t0, m = QT_TILES[t]
                    w = t0 + m
                    r = slice(hf * HD, hf * HD + HD)
                    s = banks[u % 3][0:m, 0:w]
                    if u >= 3:
                        cx.wait(pe, exped, n * U + u - 2, gate)
                    fl = flip[:, t // 2, 0:m]
                    heads = bias[:, t].rearrange("p (n g) k -> p n g k", g=GROUP)
                    pe.matmul(s, fl, heads[:, 2 * p + hf, :, 0:w][:, g, :], start=True, stop=False)
                    pe.matmul(s, ident[0:m, 0:m], mask_p[0:m, t, 0:w], start=False, stop=False)
                    pe.matmul(s, qs[k][r, t0:w], projT[r, C_AK + p, 0:w], start=False, stop=True).then_inc(scored, 1)

                def turn(n, u):
                    t, hf = units[u]
                    t0, m = QT_TILES[t]
                    wait_loop(pe, normed, n * U + u + 1, gate)
                    for kt in range(t + 1):
                        kw = QT_TILES[kt][1]
                        mm = pe.transpose(tbank[u % 2][0:kw, kt * m:kt * m + m],
                                          prob[u % 2][0:m, kt * P:kt * P + kw], ident[0:m, 0:m])
                    mm.then_inc(turned, 1)

                def one(p, g, n, k):
                    pe.wait_ge(staged, n + 1)
                    cx.wait(pe, exped, n * U)
                    for u in range(U + 1):
                        if u < U:
                            score(p, g, n, k, u)
                        if u:
                            if u >= 3:
                                pe.wait_ge(moved, n * U + u - 2)
                            turn(n, u - 1)
                    pe.wait_ge(moved, n * U + U)
                    for hf in range(2):
                        r = slice(hf * HD, hf * HD + HD)
                        for kt, (k0, kw) in enumerate(QT_TILES):
                            mm = pe.matmul(obank[k][r, k0:TP], vrows[0:kw, kt, p * P + hf * HD:p * P + hf * HD + HD],
                                           pT[hf][0:kw, kt, k0:TP], start=kt == 0, stop=kt == 2)
                    mm.then_inc(summed, 1)
                every_chunk(pe, one)


def load_pages(eng, table, pool, b, place, sem):
    for j in range(PAGES):
        page = eng.value_load(table[0:1, bass.ds(b * PAGES + j, 1)], min_val=0, max_val=pool.shape[0] - 1)
        src = pool[bass.ds(page, 1)]
        eng.dma_start(place(j), src.rearrange("o p c -> (o p) c") if len(pool.shape) == 3
                      else src.rearrange("o p a c -> (o p) a c")).then_inc(sem, 16)


def index_sampled(cx, a, projT, wsel, mask_s):
    nc = cx.nc
    with ExitStack() as st:
        def sb(name, shape, dt=F32):
            return st.enter_context(nc.sbuf_tensor(f"is_{name}", shape, dt))

        keys = [sb(f"keys{k}", [P, PAST + S]) for k in range(2)]
        qi = [sb(f"qi{k}", [P, IH * S]) for k in range(2)]
        ws = [sb(f"ws{k}", [TS, TS]) for k in range(2)]
        relu = [sb(f"relu{k}", [TS, 512]) for k in range(2)]
        work = sb("work", [TS, WORK_S])
        best = sb("best", [TS, 8])
        newmask = sb("newmask", [TS, S])
        table = sb("table", [1, B * PAGES], I32)
        banks = [st.enter_context(nc.psum_tensor(f"is_s{k}", [P, 512], F32)) for k in range(2)]
        wbanks = [st.enter_context(nc.psum_tensor(f"is_w{k}", [P, 512], F32)) for k in range(2)]
        tabled, small, scored, relued, weighted, added, staged, link, gate = (
            (cx.count if x in ("scored", "relued", "weighted", "added") else cx.sem)(f"is_{x}") for x in ("tabled", "small", "scored", "relued", "weighted", "added", "staged", "link",
                                        "gate"))
        loaded = [cx.sem(f"is_loaded{k}") for k in range(2)]
        load_gate = cx.sem("is_load_gate")
        C = 5
        block_of = lambda c: slice(c * 512, min(c * 512 + 512, PAST + S))

        with cx.block() as block:
            def load_keys(eng, k):
                place = lambda j: keys[k][:, j * PAGE:j * PAGE + PAGE]
                eng.wait_ge(tabled, 16)
                load_pages(eng, table, a["kidxT"], k, place, loaded[k])
                with eng.Fori(0, B // 2 - 1) as i:
                    cx.wait(eng, scored, i * (2 * C) + (k + 1) * C, load_gate if k else None)
                    load_pages(eng, table, a["kidxT"], i * 2 + (k + 2), place, loaded[k])

            @block.sync
            def _(sp):
                sp.dma_start(newmask[:], a["newmask"]).then_inc(small, 16)
                sp.dma_start(table[:], a["page_table"]).then_inc(tabled, 16)
                load_keys(sp, 0)

            @block.gpsimd
            def _(pool):
                load_keys(pool, 1)

            @block.tensor
            def _(pe):
                with pe.Fori(0, B // 2) as i:
                    for k in range(2):
                        at = (i * 2 + k) * C
                        pe.wait_ge(loaded[k], i * 16 * PAGES + 16 * PAGES)
                        pe.wait_ge(staged, i * 2 + k + 1)
                        for c in range(C + 1):
                            if c < C:
                                cols = block_of(c)
                                cx.wait(pe, relued, at + c - 1 if c else at)
                                pe.matmul(banks[c % 2][0:TS, 0:cols.stop - cols.start], qi[k][:], keys[k][:, cols],
                                          start=True, stop=True).then_inc(scored, 1)
                            if c:
                                cols = block_of(c - 1)
                                cx.wait(pe, added, at + c - 2 if c > 1 else at)
                                cx.wait(pe, relued, at + c, gate)
                                w = cols.stop - cols.start
                                pe.matmul(wbanks[(c - 1) % 2][0:TS, 0:w], ws[k][:], relu[(c - 1) % 2][:, 0:w],
                                          start=True, stop=True).then_inc(weighted, 1)

            @block.scalar
            def _(act):
                with act.Fori(0, B // 2) as i:
                    for k in range(2):
                        at = (i * 2 + k) * C
                        for c in range(C):
                            w = block_of(c).stop - block_of(c).start
                            cx.wait(act, scored, at + c + 1)
                            cx.wait(act, weighted, at + c - 1 if c else at)
                            act.activation(relu[c % 2][:, 0:w], banks[c % 2][0:TS, 0:w], ACT.Relu).then_inc(relued, 1)

            @block.vector
            def _(v):
                lk = Link(v, link)
                lk(v.memset(work[:, 0:PAST + S], 0.0))
                lk(v.memset(work[:, PAST + S:WORK_S], PAD))
                lk(v.memset(mask_s[TS:TS + 1, 0:FAR], 1.0))
                lk(v.memset(mask_s[TS:TS + 1, FAR:PAST + S], 0.0))
                with v.Fori(0, B // 2) as i:
                    for k in range(2):
                        at = (i * 2 + k) * C
                        b = i * 2 + k
                        new = slice(TP, N)
                        cx.wait(v, weighted, (i * 2 + k - 1) * C if k else i * 2 * C)
                        v.tensor_copy(ws[k][:], wsel[:, b, :])
                        v.tensor_copy(keys[k][:, PAST:PAST + S], projT[:, C_KI, TP:N].rearrange(
                            "p (b s) -> p b s", s=S)[:, b, :])
                        v.tensor_copy(qi[k][:].rearrange("p (h s) -> p h s", s=S),
                                      projT[:, C_QI:C_QI + IH, TP:N].rearrange("p h (b s) -> p h b s", s=S)[:, :, b, :]) \
                            .then_inc(staged, 1)
                        for c in range(C):
                            cols = block_of(c)
                            cx.wait(v, weighted, at + c + 1)
                            if c == 0:
                                cx.wait(v, added, at)
                            v.tensor_tensor(work[:, cols], work[:, cols], wbanks[c % 2][0:TS, 0:cols.stop - cols.start],
                                            ALU.add).then_inc(added, 1)
                cx.wait(v, added, B * C)
                v.wait_ge(small, 16)
                lk(v.tensor_tensor(work[:, PAST:PAST + S], work[:, PAST:PAST + S], newmask[:], ALU.add))
                take_top(v, lk, best[:], work[:], TOPK_S // 8, TOPK_S % 8)
                lk(v.tensor_scalar(mask_s[0:TS, :], work[:, 0:PAST + S], MARK / 2, NEG, ALU.is_gt, ALU.mult))
                lk(v.tensor_tensor(mask_s[0:TS, PAST:PAST + S], mask_s[0:TS, PAST:PAST + S], newmask[:], ALU.add))


def attend_sampled(cx, a, projT, mixT, ident, mask_s, sel, near, onehot, vnew):
    nc = cx.nc
    Q = 64
    with ExitStack() as st:
        def sb(name, shape, dt=F32):
            return st.enter_context(nc.sbuf_tensor(f"as_{name}", shape, dt))

        pages = [sb(f"pages{k}", [P, PAGES, 4, P]) for k in range(2)]
        knew = [sb(f"knew{k}", [P, 2, S]) for k in range(2)]
        vn = [sb(f"vn{k}", [S, 2 * P]) for k in range(2)]
        qb = [sb(f"qb{k}", [P, 2, Q]) for k in range(2)]
        ss = [sb(f"sel{k}", [TS + 1, Q]) for k in range(2)]
        prob = sb("prob", [Q, PAST + S])
        stat = sb("stat", [Q, 10])
        out = sb("out", [Q, 2 * P])
        pT = sb("pT", [P, PAGES + 1, Q])
        table = sb("table", [1, B * PAGES], I32)
        sbank = st.enter_context(nc.psum_tensor("as_s", [P, 5, 512], F32))
        tbank = st.enter_context(nc.psum_tensor("as_t", [P, 2, 512], F32))
        obank = st.enter_context(nc.psum_tensor("as_o", [P, 512], F32))
        tabled, staged, scored, maxed, exped, normed, turned, moved, summed, mixed, link, gate = (
            (cx.count if x in ("exped", "moved", "summed", "mixed") else cx.sem)(f"as_{x}") for x in ("tabled", "staged", "scored", "maxed", "exped", "normed", "turned", "moved",
                                        "summed", "mixed", "link", "gate"))
        returned = cx.sem("as_returned")
        loaded = [cx.sem(f"as_loaded{k}") for k in range(2)]
        PER = 4
        FULL = 3 * PER
        REST = PAGE + S
        LK = 6

        with cx.block() as block:
            @block.sync
            def _(sp):
                sp.dma_start(table[:], a["page_table"]).then_inc(tabled, 16)
                sp.wait_ge(tabled, 16)
                for k in range(2):
                    load_pages(sp, table, a["kv_pages"], k, lambda j: pages[k][:, j], loaded[k])
                with sp.Fori(0, B // 2 - 1) as i:
                    for k in range(2):
                        cx.wait(sp, summed, i * 2 + (k + 1))
                        load_pages(sp, table, a["kv_pages"], i * 2 + (k + 2), lambda j: pages[k][:, j], loaded[k])

            @block.vector
            def _(v):
                lk = Link(v, link)
                for k in range(2):
                    lk(v.memset(qb[k][:], 0.0))
                new = projT[:, :, TP:N].rearrange("p c (b s) -> p c b s", s=S)
                with v.Fori(0, B // 2) as i:
                    lk.enter(i, 2 * LK)
                    for k in range(2):
                        b = i * 2 + k
                        cx.wait(v, summed, b - 1 if k else i * 2)
                        for p in range(2):
                            for hf in range(2):
                                r = slice(hf * HD, hf * HD + HD)
                                c0 = (2 * p + hf) * 16
                                v.tensor_scalar(qb[k][r, p, c0:c0 + 16].rearrange("p (g s) -> p g s", s=S),
                                                new[r, C_Q + p * 4:C_Q + p * 4 + 4, b, :], HD ** -0.5, None, ALU.mult)
                        v.tensor_copy(knew[k][:], new[:, C_AK:C_AK + 2, b, :])
                        v.tensor_copy(vn[k][:], vnew[:, b, :])
                        v.tensor_copy(ss[k][:], sel[:, b, :]).then_inc(staged, 1)
                        v.wait_ge(scored, b + 1)
                        lk(v.tensor_reduce(stat[:, 0:3], sbank[0:Q, 0:3, :], AX, ALU.max))
                        lk(v.tensor_reduce(stat[:, 3:4], sbank[0:Q, 3, 0:FAR - FULL * PAGE], AX, ALU.max))
                        lk(v.tensor_reduce(stat[:, 4:5], sbank[0:Q, 4, 0:REST], AX, ALU.max))
                        lk(v.tensor_reduce(stat[:, 5:6], stat[:, 0:5], AX, ALU.max))
                        v.tensor_scalar(stat[:, 5:6], stat[:, 5:6], -1.0, None, ALU.mult).then_inc(maxed, 1)
                        cx.wait(v, exped, b + 1)
                        lk(v.tensor_reduce(stat[:, 6:7], stat[:, 6:9], AX, ALU.add))
                        lk(v.reciprocal(stat[:, 6:7], stat[:, 6:7]))
                        v.wait_ge(turned, i * 6 + 3 * k + 2)
                        v.tensor_copy(pT[:, 0:PAGES, :], tbank[:].rearrange("p a (c q) -> p (a c) q", q=Q)) \
                            .then_inc(moved, 1)
                        v.wait_ge(turned, i * 6 + 3 * k + 3)
                        v.tensor_copy(pT[0:S, PAGES, :], tbank[0:S, 0, 0:Q]).then_inc(moved, 1)
                        cx.wait(v, summed, b + 1)
                        v.tensor_scalar(out[:], obank[0:Q, 0:2 * P], stat[:, 6:7], None, ALU.mult).then_inc(normed, 1)
                        v.wait_ge(returned, b + 1)
                        for p in range(2):
                            for hf in range(2):
                                r = slice(hf * HD, hf * HD + HD)
                                c0 = 2 * P + p * Q + (2 * p + hf) * 16
                                ins = v.tensor_copy(
                                    mixT[r, 8 + p * 4:12 + p * 4, TP:N].rearrange("p c (b s) -> p c b s", s=S)[:, :, b, :],
                                    obank[r, c0:c0 + 16].rearrange("p (g s) -> p g s", s=S))
                        ins.then_inc(mixed, 1)
                    lk.leave(B // 2)

            @block.scalar
            def _(act):
                with act.Fori(0, B // 2) as i:
                    for k in range(2):
                        b = i * 2 + k
                        act.wait_ge(maxed, b + 1)
                        act.activation(prob[:, 0:FULL * PAGE].rearrange("p (a c) -> p a c", a=3), sbank[0:Q, 0:3, :],
                                       ACT.Exp, bias=stat[:, 5:6], accum_out=stat[:, 6:7])
                        act.activation(prob[:, FULL * PAGE:FAR], sbank[0:Q, 3, 0:FAR - FULL * PAGE], ACT.Exp,
                                       bias=stat[:, 5:6], accum_out=stat[:, 7:8])
                        act.activation(prob[:, FAR:PAST + S], sbank[0:Q, 4, 0:REST], ACT.Exp,
                                       bias=stat[:, 5:6], accum_out=stat[:, 8:9]).then_inc(exped, 1)

            @block.tensor
            def _(pe):
                with pe.Fori(0, B // 2) as i:
                    for k in range(2):
                        b = i * 2 + k
                        pe.wait_ge(loaded[k], (i + 1) * (16 * PAGES))
                        cx.wait(pe, exped, b)
                        wait_loop(pe, staged, b + 1, gate)
                        for c in range(5):
                            c0 = c * PER * PAGE if c < 4 else FAR
                            n = (PER, PER, PER, PER - 1, 1)[c]
                            w = n * PAGE if c < 4 else REST
                            pe.matmul(sbank[0:Q, c, 0:w], ss[k][:], mask_s[:, c0:c0 + w], start=True, stop=False)
                            for p in range(2):
                                j = c0 // PAGE
                                pe.matmul(sbank[0:Q, c, 0:n * PAGE].rearrange("p (j c) -> p j c", j=n), qb[k][:, p, :],
                                          pages[k][:, j:j + n, p, :], start=False, stop=c < 4 and p == 1)
                        for p in range(2):
                            pe.matmul(sbank[0:Q, 4, PAGE:REST], qb[k][:, p, :], knew[k][:, p, :],
                                      start=False, stop=False)
                        pe.matmul(sbank[0:Q, 4, 0:REST], near[:], onehot[:], start=False, stop=True).then_inc(scored, 1)
                        cx.wait(pe, exped, b + 1)
                        cx.wait(pe, moved, b * 2, gate)
                        for j in range(PAGES):
                            mm = pe.transpose(tbank[:, j // 8, (j % 8) * Q:(j % 8) * Q + Q],
                                              prob[:, j * PAGE:j * PAGE + PAGE], ident[0:Q, 0:Q])
                        mm.then_inc(turned, 2)
                        cx.wait(pe, moved, b * 2 + 1, gate)
                        pe.transpose(tbank[0:S, 0, 0:Q], prob[:, PAST:PAST + S], ident[0:Q, 0:Q]).then_inc(turned, 1)
                        cx.wait(pe, moved, b * 2 + 2)
                        cx.wait(pe, mixed, b)
                        for j in range(PAGES):
                            pe.matmul(obank[0:Q, 0:2 * P].rearrange("q (p d) -> q p d", p=2), pT[:, j, :],
                                      pages[k][:, j, 2:4, :], start=j == 0, stop=False)
                        pe.matmul(obank[0:Q, 0:2 * P], pT[0:S, PAGES, :], vn[k][:], start=False, stop=True) \
                            .then_inc(summed, 1)
                        wait_loop(pe, normed, b + 1, gate)
                        for p in range(2):
                            mm = pe.transpose(obank[:, 2 * P + p * Q:2 * P + p * Q + Q], out[:, p * P:p * P + P],
                                              ident[0:Q, 0:Q])
                        mm.then_inc(returned, 1)


def peer(cx, a, xT, ident):
    nc = cx.nc
    with ExitStack() as st:
        picks = st.enter_context(nc.sbuf_tensor("pe_picks", [P, 3, N], F32))
        cx.phase(peer_select, a, xT, ident, picks)
        high = st.enter_context(nc.sbuf_tensor("pe_high", [P, KT, N], F32R))
        low = st.enter_context(nc.sbuf_tensor("pe_low", [P, KT, N], F32R))
        cx.phase(split, "pe_x", xT, high, low)
        cx.phase(peer_experts, a, xT, high, low, picks)


def peer_select(cx, a, xT, ident, picks):
    nc = cx.nc
    SL = 4
    with ExitStack() as st:
        def sb(name, shape, dt=F32):
            return st.enter_context(nc.sbuf_tensor(f"ps_{name}", shape, dt))[:]

        w = [sb(f"w{s}", [P, KT, P]) for s in range(SL)]
        sk = [sb(f"sk{s}", [P, P]) for s in range(SL)]
        q = [sb(f"q{s}", [P, 3 * P]) for s in range(SL)]
        score = sb("score", [P, 3, NK])
        top = [sb(f"top{h}", [P, 3, EK]) for h in range(2)]
        topi = sb("topi", [P, 3, EK], U32)
        keyf = [sb(f"keyf{h}", [P, 3, EK]) for h in range(2)]
        cand = sb("cand", [P, 3, EK * EK])
        best = sb("best", [P, 3, EK])
        diff = sb("diff", [P, 3, EK])
        bi = sb("bi", [P, 3, EK], U32)
        part = sb("part", [P, 3, EK], U32)
        partf = sb("partf", [P, 3, EK])
        hit = sb("hit", [P, 3 * EK, EK])
        total = sb("total", [P, 3, 1])
        iota = sb("iota", [P, EK])
        chosen = sb("chosen", [P, 3, 3, PH * EK])
        acc = [st.enter_context(nc.psum_tensor(f"ps_acc{s}", [P, 512], F32)) for s in range(SL)]
        sbank = [st.enter_context(nc.psum_tensor(f"ps_s{s}", [P, 512], F32)) for s in range(2)]
        tbank = [st.enter_context(nc.psum_tensor(f"ps_t{s}", [P, 512], F32)) for s in range(2)]
        loaded = [cx.sem(f"ps_loaded{s}") for s in range(SL)]
        summed = [cx.sem(f"ps_summed{s}") for s in range(SL)]
        emptied = [cx.count(f"ps_emptied{s}") for s in range(SL)]
        scored = [cx.count(f"ps_scored{s}") for s in range(SL)]
        read = [cx.count(f"ps_read{s}") for s in range(2)]
        small, gate, link, diffed, exped, turned, moved = (cx.sem(f"ps_{x}") for x in
                                                     ("small", "gate", "link", "diffed", "exped", "turned", "moved"))

        with cx.block() as block:
            @block.sync
            def _(sp):
                sp.dma_start(iota, a["iota"][:, 0:EK]).then_inc(small, 16)
                with sp.Fori(0, 2 * PH // SL) as i:
                    for s in range(SL):
                        cx.wait(sp, scored[s], i)
                        sp.dma_start(w[s], a["peer_wq"][i * SL + s]).then_inc(loaded[s], 16)
                        sp.dma_start(sk[s], a["subkeysT"][i * SL + s]).then_inc(loaded[s], 16)

            @block.tensor
            def _(pe):
                def project_chunk(i, s):
                    pe.wait_ge(loaded[s], i * 32 + 32)
                    cx.wait(pe, emptied[s], i)
                    for k in range(KT):
                        mm = pe.matmul(acc[s][:, 0:N], w[s][:, k, :], xT[:, k, :], start=k == 0, stop=k == KT - 1)
                    mm.then_inc(summed[s], 1)

                def score_chunk(i, s):
                    cx.wait(pe, emptied[s], i + 1)
                    cx.wait(pe, read[s % 2], i * 2 + s // 2)
                    for t in range(3):
                        mm = pe.matmul(sbank[s % 2][:, t * P:t * P + P], q[s][:, t * P:t * P + P], sk[s],
                                       start=True, stop=True)
                    mm.then_inc(scored[s], 1)

                with pe.Fori(0, 2 * PH // SL) as i:
                    for s in range(SL):
                        project_chunk(i, s)
                        if s:
                            score_chunk(i, s - 1)
                    score_chunk(i, SL - 1)
                pe.wait_ge(link, SL + (2 * PH // SL) * LINKS_PS)
                for which in range(3):
                    if which == 2:
                        pe.wait_ge(moved, 1)
                    for t in range(3):
                        mm = pe.transpose(tbank[which % 2][:, t * P:t * P + P], chosen[:, which, t, :], ident[:])
                    mm.then_inc(turned, 1)

            @block.scalar
            def _(act):
                act.wait_ge(link, SL)
                with act.Fori(0, 2 * PH // SL) as i:
                    for s in range(SL):
                        act.wait_ge(summed[s], i + 1)
                        cx.wait(act, scored[s], i)
                        act.activation(q[s][:, 0:N], acc[s][:, 0:N], ACT.Copy).then_inc(emptied[s], 1)
                        if s % 2:
                            act.wait_ge(diffed, i * 2 + s // 2 + 1)
                            act.activation(diff, diff, ACT.Exp).then_inc(exped, 1)

            @block.vector
            def _(v):
                lk = Link(v, link, gate)
                v.wait_ge(small, 16)
                for s in range(SL):
                    lk(v.memset(q[s][:, N:3 * P], 0.0))

                def half(i, s):
                    cx.wait(v, scored[s], i + 1)
                    v.tensor_copy(score.rearrange("p t k -> p (t k)"), sbank[s % 2][:, 0:3 * P]).then_inc(read[s % 2], 1)
                    cx.wait(v, read[s % 2], i * 2 + s // 2 + 1, gate)
                    tp = top[s % 2]
                    sixteen(lambda t: score[:, t, :], tp)
                    lk(v.tensor_copy(keyf[s % 2], topi))

                def sixteen(values, tp):
                    idx = topi
                    for n in range(2):
                        for t in range(3):
                            ins = v.max(tp[:, t, 8 * n:8 * n + 8], values(t))
                        lk(ins)
                        for t in range(3):
                            ins = v.max_index(idx[:, t, 8 * n:8 * n + 8], tp[:, t, 8 * n:8 * n + 8], values(t))
                        lk(ins)
                        if n == 0:
                            for t in range(3):
                                ins = v.match_replace(values(t), tp[:, t, 0:8], values(t), MARK)
                            lk(ins)

                def head(h):
                    ax = lambda q, where: q.rearrange("p t (k o) -> p t k o" if where else "p t (o k) -> p t o k", o=1)
                    grid = cand.rearrange("p t (x y) -> p t x y", y=EK)
                    for t in range(3):
                        ins = v.tensor_tensor(grid[:, t], ax(top[0], 1)[:, t].to_broadcast([P, EK, EK]),
                                              ax(top[1], 0)[:, t].to_broadcast([P, EK, EK]), ALU.add)
                    lk(ins)
                    sixteen(lambda t: cand[:, t, :], best)
                    lk(v.tensor_copy(bi, topi))
                    v.tensor_tensor(diff, best, best[:, :, 0:1].to_broadcast([P, 3, EK]), ALU.subtract) \
                        .then_inc(diffed, 1)
                    for half_, (op, by) in enumerate(((ALU.logical_shift_right, 4), (ALU.bitwise_and, EK - 1))):
                        lk(v.tensor_scalar(part, bi, by, None, op))
                        lk(v.tensor_copy(partf, part))
                        lk(v.tensor_tensor(hit, partf.rearrange("p t (k o) -> p (t k) o", o=1)
                                           .to_broadcast([P, 3 * EK, EK]),
                                           iota.rearrange("p (o k) -> p o k", o=1).to_broadcast([P, 3 * EK, EK]),
                                           ALU.is_equal))
                        hit4 = hit.rearrange("p (t k) x -> p t k x", t=3)
                        for t in range(3):
                            ins = v.tensor_tensor(hit4[:, t], hit4[:, t],
                                                  ax(keyf[half_], 0)[:, t].to_broadcast([P, EK, EK]), ALU.mult)
                        lk(ins)
                        lk(v.tensor_reduce(chosen[:, half_].rearrange("p t (h k) -> p t h k", h=PH)[:, :, h, :],
                                           hit4, AX, ALU.add))
                    v.wait_ge(exped, h + 1)
                    lk(v.tensor_reduce(total, diff, AX, ALU.add))
                    lk(v.reciprocal(total, total))
                    lk(v.tensor_tensor(chosen[:, 2].rearrange("p t (h k) -> p t h k", h=PH)[:, :, h, :], diff,
                                       total.to_broadcast([P, 3, EK]), ALU.mult))

                with v.Fori(0, 2 * PH // SL) as i:
                    lk.enter(i, LINKS_PS)
                    for s in range(SL):
                        half(i, s)
                        if s % 2:
                            head(i * 2 + s // 2)
                    lk.leave(2 * PH // SL)
                for which in range(3):
                    v.wait_ge(turned, which + 1)
                    v.tensor_copy(picks[:, which, :], tbank[which % 2][:, 0:N]).then_inc(moved, 1)


def peer_experts(cx, a, xT, high, low, picks):
    nc = cx.nc
    SL = 4
    EH = NK // 2
    E2 = 2
    HALF = D // 2
    G4 = 4
    UP, DOWN = EH // SL, EH // E2 // SL
    PER = UP + 2 * DOWN
    with ExitStack() as st:
        def sb(name, shape, dt=F32):
            return st.enter_context(nc.sbuf_tensor(f"px_{name}", shape, dt))

        gates = sb("gates", [P, EH, N])
        w, w_low = zip(*(sbuf_both(nc, st, f"px_w{s}", [P, 2048]) for s in range(SL)))
        w_high = [sb(f"wh{s}", [P, 2048], F32R) for s in range(2)]
        h = [sb(f"h{s}", [P, N]) for s in range(2)]
        g_high = [sb(f"gh{s}", [P, E2, N], F32R) for s in range(2)]
        g_low = [sb(f"gl{s}", [P, E2, N], F32R) for s in range(2)]
        iota = sb("iota", [P, NK])
        first = [sb(f"first{k}", [P, G4, EH]) for k in range(2)]
        second = [sb(f"second{k}", [P, G4, NK]) for k in range(2)]
        bank = [st.enter_context(nc.psum_tensor(f"px_bank{s}", [P, 512], F32)) for s in range(8)]
        iota_in = cx.sem("px_iota_in")
        loaded, raised, lowered = ([cx.sem(f"px_{x}{s}") for s in range(SL)] for x in ("loaded", "high", "low"))
        used = [cx.count(f"px_used{s}") for s in range(SL)]
        found, built = cx.sem("px_found"), cx.sem("px_built")
        placed, moved = cx.count("px_placed"), cx.count("px_moved")
        curved, weighed = ([cx.count(f"px_{x}{s}") for s in range(2)] for x in ("curved", "weighed"))
        g_raised, g_lowered, emptied = cx.sem("px_g_high"), cx.sem("px_g_low"), cx.sem("px_emptied")
        steps = N // (2 * G4)

        def stage(eng, base, turns, one, last=False):
            for s in range(SL):
                one(0, s, base, s == 0, False)
            with eng.Fori(0, turns - 1 - last) as i:
                for s in range(SL):
                    one(i + 1, s, i + (base + 1), False, False)
            if last:
                for s in range(SL):
                    one(turns - 1, s, base + turns - 1, False, s == SL - 1)

        def stages(eng, gate_step, up, down):
            for hf in range(2):
                gate_step(hf)
                stage(eng, hf * PER, UP, lambda *q: up(hf, *q))
                for dh in range(2):
                    stage(eng, hf * PER + UP + dh * DOWN, DOWN, lambda *q: down(hf, dh, *q), last=hf and dh)

        def gate_steps(eng, hf, one):
            for k in range(2):
                one(k, k * G4, hf * 2 * steps + k)
            with eng.Fori(0, steps - 1) as i:
                for k in range(2):
                    one(k, i * (2 * G4) + (2 + k) * G4, i * 2 + (hf * 2 * steps + 2 + k))

        def following(s, turn):
            return (s + 1, turn) if s < SL - 1 else (0, turn + 1)

        with cx.block() as block:
            @block.sync
            def _(sp):
                sp.dma_start(iota[:], a["iota"]).then_inc(iota_in, 16)

                def up(hf, i, s, turn, start, end):
                    cx.wait(sp, used[s], turn)
                    sp.dma_start(w[s][:].rearrange("p (k e) -> p k e", e=P), a["peer_u"][i * SL + (hf * EH + s)]) \
                        .then_inc(loaded[s], 16)

                def down(hf, dh, i, s, turn, start, end):
                    cx.wait(sp, used[s], turn)
                    g = i * SL + (hf * (EH // E2) + s)
                    src = a["peer_v"][:, :, dh]
                    src = src[g] if isinstance(g, int) else src[bass.ds(g, 1)].rearrange("o p e d -> (o p) e d")
                    sp.dma_start(w[s][:].rearrange("p (e d) -> p e d", e=E2), src).then_inc(loaded[s], 16)
                stages(sp, lambda hf: None, up, down)

            def raise_tile(act, s, turn):
                act.wait_ge(loaded[s], turn * 16 + 16)
                cx.wait(act, used[(s + 2) % SL], turn + 1 if s >= 2 else turn)
                act.activation(w_high[s % 2][:], w[s][:], ACT.Copy).then_inc(raised[s], 1)

            def lower_tile(v, s, turn):
                v.wait_ge(raised[s], turn + 1)
                v.tensor_tensor(w_low[s][:], w[s][:], w_high[s % 2][:], ALU.subtract).then_inc(lowered[s], 1)

            @block.scalar
            def _(act):
                def move_gates(hf):
                    if hf:
                        act.wait_ge(g_lowered, 2 * DOWN * SL)

                    def one(k, tok, n):
                        cx.wait(act, placed, n + 1)
                        act.activation(gates[:, :, bass.ds(tok, G4)],
                                       bank[6 + k][:, 0:G4 * EH].rearrange("p (n i) -> p i n", n=G4),
                                       ACT.Copy).then_inc(moved, 1)
                    gate_steps(act, hf, one)

                def up(hf, i, s, turn, start, end):
                    raise_tile(act, *following(s, turn))
                    cx.wait(act, used[s], turn + 1)
                    n = i * 2 + (hf * 2 * UP + s // 2)
                    cx.wait(act, weighed[s % 2], n)
                    act.activation(h[s % 2][:], bank[s][:, 0:N], ACT.Gelu).then_inc(curved[s % 2], 1)

                def down(hf, dh, i, s, turn, start, end):
                    if start:
                        for k in range(2):
                            cx.wait(act, weighed[k], (hf + 1) * 2 * UP)
                    cx.wait(act, used[(s + 2) % SL], turn + 1 if s >= 2 else turn)
                    act.activation(g_high[s % 2][:], gates[:, bass.ds(i * (SL * E2) + s * E2, E2), :]
                                   if not isinstance(i, int) else gates[:, (i * SL + s) * E2:(i * SL + s + 1) * E2, :],
                                   ACT.Copy).then_inc(g_raised, 1)
                    if not end:
                        raise_tile(act, *following(s, turn))
                raise_tile(act, 0, 0)
                stages(act, move_gates, up, down)

            @block.tensor
            def _(pe):
                def place_gates(hf):
                    if hf:
                        pe.wait_ge(emptied, 16)

                    def one(k, tok, n):
                        pe.wait_ge(built, n + 1)
                        cx.wait(pe, moved, max(n - 1, 0) if isinstance(n, int) else n - 1)
                        for q in range(G4):
                            mm = pe.matmul(bank[6 + k][:, q * EH:q * EH + EH], second[k][:, q, :],
                                           first[k][:, q, :], start=True, stop=True)
                        mm.then_inc(placed, 1)
                    gate_steps(pe, hf, one)

                def up(hf, i, s, turn, start, end):
                    pe.wait_ge(lowered[s], turn + 1)
                    n = i * 2 + (hf * 2 * UP + s // 2 - 1)
                    if isinstance(n, int) and n - 1 < 0 and hf == 0:
                        pass
                    else:
                        cx.wait(pe, curved[s % 2], n)
                    for k in range(KT):
                        mm = split_product(pe, bank[s][:, 0:N], w_high[s % 2][:, k * P:k * P + P],
                                           w_low[s][:, k * P:k * P + P], high[:, k, :], low[:, k, :],
                                           k == 0, k == KT - 1)
                    mm.then_inc(used[s], 1)

                def down(hf, dh, i, s, turn, start, end):
                    if start and dh:
                        pe.wait_ge(emptied, 16 * hf + 8)
                    if start and not dh:
                        for k in range(2):
                            cx.wait(pe, curved[k], (hf + 1) * 2 * UP)
                        cx.wait(pe, moved, (hf + 1) * 2 * steps)
                    pe.wait_ge(lowered[s], turn + 1)
                    pe.wait_ge(g_lowered, i * SL + ((hf * 2 + dh) * DOWN * SL + s + 1))
                    for e in range(E2):
                        for d in range(8):
                            c = e * HALF + d * P
                            mm = split_product(pe, bank[d][:, 0:N], w_high[s % 2][:, c:c + P], w_low[s][:, c:c + P],
                                               g_high[s % 2][:, e, :], g_low[s % 2][:, e, :], start and e == 0, end and e == 1)
                    mm.then_inc(used[s], 1)
                stages(pe, place_gates, up, down)

            @block.vector
            def _(v):
                def build_onehots(hf):

                    def picked(which, tok, width):
                        return picks[:, which, bass.ds(tok, G4)].rearrange("p (n o) -> p n o", o=1) \
                            .to_broadcast([P, G4, width])

                    def keys(start, width):
                        return iota[:, start:start + width].rearrange("p (o i) -> p o i", o=1) \
                            .to_broadcast([P, G4, width])

                    def one(k, tok, n):
                        cx.wait(v, placed, max(n - 1, 0) if isinstance(n, int) else n - 1)
                        v.tensor_tensor(first[k][:], keys(hf * EH, EH), picked(0, tok, EH),
                                        ALU.is_equal).then_inc(found, 1)
                        v.tensor_tensor(second[k][:], keys(0, NK), picked(1, tok, NK), ALU.is_equal)
                        v.wait_ge(found, n + 1)
                        v.tensor_tensor(first[k][:], first[k][:], picked(2, tok, EH), ALU.mult).then_inc(built, 1)
                    gate_steps(v, hf, one)

                def up(hf, i, s, turn, start, end):
                    if start:
                        cx.wait(v, moved, (hf + 1) * 2 * steps)
                    lower_tile(v, *following(s, turn))
                    n = i * 2 + (hf * 2 * UP + s // 2 + 1)
                    cx.wait(v, curved[s % 2], n)
                    g = gates[:, i * SL + s, :]
                    v.tensor_tensor(g, g, h[s % 2][:], ALU.mult).then_inc(weighed[s % 2], 1)

                def down(hf, dh, i, s, turn, start, end):
                    if start:
                        for k in range(2):
                            cx.wait(v, weighed[k], (hf + 1) * 2 * UP)
                    n = i * SL + ((hf * 2 + dh) * DOWN * SL + s + 1)
                    v.wait_ge(g_raised, n)
                    g = gates[:, bass.ds(i * (SL * E2) + s * E2, E2), :] \
                        if not isinstance(i, int) else gates[:, (i * SL + s) * E2:(i * SL + s + 1) * E2, :]
                    v.tensor_tensor(g_low[s % 2][:], g, g_high[s % 2][:], ALU.subtract).then_inc(g_lowered, 1)
                    if not end:
                        lower_tile(v, *following(s, turn))

                def drain(hf, dh):
                    for s in range(SL):
                        cx.wait(v, used[s], hf * PER + UP + (dh + 1) * DOWN)
                    for d in range(8):
                        x = xT[:, dh * 8 + d, :]
                        v.scalar_tensor_tensor(x, x, 1.0 if hf else ALPHA, bank[d][:, 0:N], ALU.mult,
                                               ALU.add).then_inc(emptied, 1)
                v.wait_ge(iota_in, 16)
                for hf in range(2):
                    build_onehots(hf)
                    if hf == 0:
                        lower_tile(v, 0, 0)
                    stage(v, hf * PER, UP, lambda *q: up(hf, *q))
                    for dh in range(2):
                        if hf or dh:
                            v.wait_ge(emptied, (2 * hf + dh) * 8)
                        stage(v, hf * PER + UP + dh * DOWN, DOWN, lambda *q: down(hf, dh, *q), last=hf and dh)
                        drain(hf, dh)


LINKS_PS = 64

def chunked(w, cols):
    w = np.asarray(w)
    out = np.zeros((w.shape[0], len(cols)), w.dtype)
    ok = cols >= 0
    out[:, ok] = w[:, cols[ok]]
    return np.ascontiguousarray(out.reshape(w.shape[0] // P, P, len(cols) // P, P).transpose(2, 1, 0, 3))


def in_columns():
    cols = list(range(RC)) + [-1] * (RWC * P - RC)
    cols += [RC + x for x in q_order()]
    cols += list(range(RC + 1024, RC + 1024 + 512 + IH * ID + ID + IH)) + [-1] * (P - IH)
    return np.array(cols)


def q_order():
    return [((2 * p + hf) * GROUP + g) * HD + d for p in range(2) for g in range(GROUP) for hf in range(2)
            for d in range(HD)]


def fold(v, chunks):
    v = np.asarray(v).reshape(-1)
    return np.ascontiguousarray(np.pad(v, (0, chunks * P - v.size)).reshape(chunks, P).T)


def across(s):
    out = np.zeros((8, 2, HD, B, 2, HD), s.dtype)
    for h in range(2):
        out[:, h, :, :, h, :] = s[:, h]
    return out.reshape(8, P, B, P)


def attention_layouts(x):
    f = np.float32
    e = np.eye
    hs = np.arange(TS)
    t = np.arange(2 * TP)
    s, key = np.arange(S)[:, None], FAR + np.arange(PAGE + S)[None, :]
    near = bucket(PAST + s - key)
    q, kpos = np.arange(3 * P), np.arange(TP)
    flip = np.zeros((P, 2, P), f)
    flip[:, 0] = e(P)[::-1]
    flip[:16, 1, :16] = e(16)[::-1]
    n_pool = x["cache_k"].shape[1]
    qn = np.arange(64)
    return {
        "spread": (np.arange(IH)[:, None] == hs[None, :] // S).astype(f),
        "wpick": ((hs[:, None, None] % S == hs[None, None, :] % S)
                  & (np.arange(B)[None, :, None] == hs[None, None, :] // S)).astype(f),
        "spick": np.broadcast_to(np.arange(P)[:, None, None] // 32 == np.arange(S)[None, None, :], (P, 16, S)).astype(f),
        "bucket_table": (np.arange(NB_BUCKETS)[:, None] == bucket(TP - 1 - t)[None, :]).astype(f),
        "near_onehot": (near[:, None, :] == np.arange(NB_BUCKETS)[None, :, None]).reshape(P, PAGE + S).astype(f),
        "sel": ((hs[:, None, None] // S == np.arange(B)[None, :, None])
                & (hs[:, None, None] % S == qn[None, None, :] % S)).astype(f),
        "rel_bias": x["rel_bias"],
        "causal": np.where(kpos[None, :] <= q[:, None], 0, NEG).reshape(3, P, TP).transpose(1, 0, 2).astype(f),
        "newmask": np.where(np.arange(S)[None, :] <= (hs % S)[:, None], 0, NEG).astype(f),
        "flip": flip,
        "page_table": x["page_table"].reshape(1, -1).astype(np.int32),
        "kidxT": x["cache_kidx"][0].transpose(0, 2, 1),
        "kv_pages": np.concatenate([x["cache_k"][0].reshape(n_pool, PAGE, 2, P).transpose(0, 3, 2, 1),
                                    x["cache_v"][0].reshape(n_pool, PAGE, 2, P)], 2),
    }


def layouts(x):
    f = np.float32
    rows = np.concatenate([x["meta_tokens"], x["x_prompt"][0], x["x_sample"].reshape(TS, D)])
    a = {
        "xT": rows.T.reshape(KT, P, N).transpose(1, 0, 2),
        "ones": np.full((P, P), 1 / D, f),
        "ident": np.eye(P, dtype=f),
        "ln_gb": np.stack([np.stack([fold(x[g], KT), fold(x[b], KT)], 1)
                           for g, b in (("ln_in_g", "ln_in_b"), ("ln1_g", "ln1_b"), ("ln2_g", "ln2_b"))], 1),
        "rw_masks": rwkv_masks(),
        "seqmask": (np.arange(P)[:, None] // S - CH // 2 // S == np.arange(B)[None, :]).astype(f),
        "halves": (np.arange(P)[:, None] // HD == np.arange(P)[None, :] // HD).astype(f),
        "rw_cols": np.stack([fold(x["mu_shift"][0][:RW], 8), fold(x["mu_shift"][0][RW:2 * RW], 8),
                             fold(x["mu_shift"][0][2 * RW:3 * RW], 8)]
                            + [fold(x[q], 8) for q in ("k_k", "k_a", "r_k", "w0", "a0", "gn_g", "gn_b")], 2),
        "mu": fold(x["mu_shift"], RWC),
        "shiftT_in": np.stack([fold(x["state_shift"][0, b], RWC) for b in range(B)], 2),
        "wa_up": np.concatenate([x["w_up"][0], x["a_up"][0]]),
        "g_up": x["g_up"][0],
        "wkvT": across(x["state_wkv"][0].reshape(B, 8, 2, HD, HD).transpose(1, 2, 4, 0, 3)),
        **attention_layouts(x),
        "iota": np.broadcast_to(np.arange(NK), (P, NK)).astype(f),
        "peer_wq": chunked(x["peer_wq"][0], np.arange(D)),
        "subkeysT": x["peer_subkeys"][0].reshape(2 * PH, NK, P).transpose(0, 2, 1),
        "peer_u": x["peer_u"][0].reshape(NK, NK, KT, P).transpose(0, 3, 2, 1),
        "peer_v": x["peer_v"][0].reshape(NK // 2, 2, NK, 2, D // 2).transpose(0, 2, 3, 1, 4),
        "w_in": chunked(x["w_in"][0], in_columns()),
        "w_o": chunked(np.concatenate([x["w_o"][0][:RW], x["w_o"][0][RW:][q_order()]]), np.arange(D)),
    }
    return a


def outputs():
    return {"yT": (P, KT, N), "kvT": (P, 4, N), "kiT": (P, N), "shiftT": (P, RWC, B + 1),
            "wkvT_p": (8, P, HD), "wkvT_s": (8, P, B, HD)}


def kernel(**inputs):
    import concourse.bacc as bacc
    from concourse.bass_utils import run_bass_kernel_spmd as run

    x = {k: np.asarray(v) for k, v in inputs.items()}
    arrays = {k: np.ascontiguousarray(v) for k, v in layouts(x).items()}
    nc = bacc.Bacc("TRN2", target_bir_lowering=False, num_devices=1)
    a = {k: nc.dram_tensor(f"in_{k}", v.shape, mybir.dt.from_np(v.dtype), kind="ExternalInput").ap()
         for k, v in arrays.items()}
    o = {k: nc.dram_tensor(f"out_{k}", s, F32, kind="ExternalOutput").ap() for k, s in outputs().items()}
    build(nc, a, o)
    r = run(nc, [{f"in_{k}": v for k, v in arrays.items()}], core_ids=[0]).results[0]
    r = {k: np.asarray(r[f"out_{k}"]) for k in o}

    y = r["yT"].transpose(2, 1, 0).reshape(N, D)
    kv = r["kvT"].transpose(2, 1, 0).reshape(N, 2, KVH, HD)
    ki = r["kiT"].T
    shift = r["shiftT"].transpose(2, 1, 0).reshape(B + 1, RWC * P)[:, :RC]
    wkv_p = r["wkvT_p"].reshape(16, HD, HD).transpose(0, 2, 1)
    wkv_s = r["wkvT_s"].reshape(16, HD, B, HD).transpose(2, 0, 3, 1)
    c = np.ascontiguousarray
    return (c(y[META:TP])[None], c(y[TP:]).reshape(B, S, D),
            c(kv[:TP, 0])[None, None], c(kv[:TP, 1])[None, None], c(ki[:TP])[None, None],
            c(wkv_p)[None, None], c(shift[0])[None, None],
            c(kv[TP:, 0]).reshape(1, B, S, KVH, HD), c(kv[TP:, 1]).reshape(1, B, S, KVH, HD),
            c(ki[TP:]).reshape(1, B, S, ID), c(wkv_s)[None], c(shift[1:])[None])
```

```python
from contextlib import ExitStack, contextmanager

import numpy as np
import concourse.bass as bass
from concourse import mybir

F32 = mybir.dt.float32
F32R = mybir.dt.float32r
U32 = mybir.dt.uint32
I32 = mybir.dt.int32
ALU = mybir.AluOpType
ACT = mybir.ActivationFunctionType
AX = mybir.AxisListType.X

P = 128
D = 2048
KT = D // P
META, SEQ = 16, 256
TP = META + SEQ
B, S = 8, 4
TS = B * S
N = TP + TS
NY = N - META
PAST, PAGE = 2048, 128
PAGES = PAST // PAGE
HD = 64
RW = 1024
RC = 3 * RW + 64 + 64 + 160
KVH, GROUP = 4, 4
IH, ID = 8, 128
TOPK_P = min(256, TP // 4)
TOPK_S = min(256, (PAST + S) // 4)
NB_BUCKETS, MAX_DIST = 32, 128
PH, NK, EK = 8, 128, 16
ALPHA = 2 ** 0.25
LN_EPS, GN_EPS = 1e-5, 64e-5
DECAY = float(np.exp(-0.5))

C_R, C_K, C_V, C_WA, C_G = 0, 8, 16, 24, 25
RWC = 27
C_Q, C_AK, C_AV, C_QI, C_KI, C_WI = 27, 35, 37, 39, 47, 48
NC_IN = 49

CH = 32
NEG = -1e30
PAD = -1e38
MARK = -3e38


class Ctx:

    def __init__(self, nc):
        self.nc = nc
        self.own = None

    def sem(self, name):
        s = self.own.enter_context(self.nc.semaphore(name))
        self.used.append(s)
        return s

    def count(self, name):
        s = self.sem(name)
        self.counts.append(s)
        return s

    def wait(self, eng, s, value, gate=None):
        assert any(s is c for c in self.counts)
        if gate is None:
            eng.wait_ge(s, value + 1)
        else:
            wait_loop(eng, s, value + 1, gate)

    @contextmanager
    def block(self):
        with self.nc.Block() as block:
            if self.counts:
                @block.gpsimd
                def _(pool):
                    for s in self.counts:
                        pool.sem_inc(s, 1)
            yield block

    def phase(self, build, *args, **kwargs):
        with ExitStack() as own:
            self.own, self.used, self.counts = own, [], []
            build(self, *args, **kwargs)
            used = self.used
            with self.nc.Block() as block:
                @block.sync
                def _(sp):
                    for s in used:
                        sp.sem_clear(s)


def wait_loop(eng, sem, value, gate):
    eng.wait_ge(sem, value)
    eng.sem_inc(gate, 1)


class Link:

    def __init__(self, eng, sem, gate=None):
        self.eng, self.sem, self.n, self.at, self.gate = eng, sem, 0, None, gate

    def value(self):
        return self.n if self.at is None else self.at + self.n

    def __call__(self, ins):
        ins.then_inc(self.sem, 1)
        self.n += 1
        if self.gate and self.at is not None:
            wait_loop(self.eng, self.sem, self.value(), self.gate)
        else:
            self.eng.wait_ge(self.sem, self.value())

    def enter(self, i, per):
        self.start, self.per = self.n, per
        self.at = i * per + self.start
        self.n = 0

    def leave(self, turns):
        assert self.n == self.per, (self.n, self.per)
        self.n, self.at = self.start + turns * self.per, None


def load_all(eng, sem, pairs):
    n = 0
    for dst, src in pairs:
        eng.dma_start(dst, src).then_inc(sem, 16)
        n += 16
    return n


def load(cx, name, pairs):
    loaded = cx.sem(f"{name}_loaded")
    with cx.nc.Block() as block:
        @block.sync
        def _(sp):
            sp.wait_ge(loaded, load_all(sp, loaded, pairs))


def layer_norm(cx, name, xT, gb, ones, out=None, into=None):
    into = xT if into is None else into
    n = xT.shape[-1]
    nc = cx.nc
    with ExitStack() as st:
        sq = st.enter_context(nc.sbuf_tensor(f"{name}_sq", [P, KT, n], F32))
        rs = st.enter_context(nc.sbuf_tensor(f"{name}_rs", [P, 3, n], F32))
        mean = st.enter_context(nc.psum_tensor(f"{name}_mean", [P, 512], F32))
        var = st.enter_context(nc.psum_tensor(f"{name}_var", [P, 512], F32))
        mean_done, centered, squared, var_done = (cx.sem(f"{name}_{x}") for x in
                                                  ("mean_done", "centered", "squared", "var_done"))
        inv_done, rstd_done, link = cx.sem(f"{name}_inv"), cx.sem(f"{name}_rstd"), cx.sem(f"{name}_link")
        stored = cx.sem(f"{name}_stored")
        scaled = cx.sem(f"{name}_scaled")
        with nc.Block() as block:
            @block.tensor
            def _(pe):
                for k in range(KT):
                    mm = pe.matmul(mean[:, 0:n], ones[:], xT[:, k, :], start=k == 0, stop=k == KT - 1)
                mm.then_inc(mean_done, 1)
                for k in range(KT):
                    pe.wait_ge(squared, k // 4 + 1)
                    mm = pe.matmul(var[:, 0:n], ones[:], sq[:, k, :], start=k == 0, stop=k == KT - 1)
                mm.then_inc(var_done, 1)

            @block.vector
            def _(v):
                lk = Link(v, link)
                v.wait_ge(mean_done, 1)
                lk(v.tensor_copy(rs[:, 2, :], mean[:, 0:n]))
                for q in range(4):
                    v.tensor_tensor(xT[:, 4 * q:4 * q + 4, :], xT[:, 4 * q:4 * q + 4, :],
                                    rs[:, 2:3, :].to_broadcast([P, 4, n]), ALU.subtract).then_inc(centered, 1)
                v.wait_ge(var_done, 1)
                lk(v.tensor_scalar(rs[:, 0, :], var[:, 0:n], LN_EPS, None, ALU.add))
                v.reciprocal(rs[:, 0, :], rs[:, 0, :]).then_inc(inv_done, 1)
                v.wait_ge(rstd_done, 1)
                v.wait_ge(centered, 4)
                for k in range(KT):
                    ins = v.scalar_tensor_tensor(xT[:, k, :], xT[:, k, :], gb[:, 0, k:k + 1], rs[:, 1, :],
                                                 ALU.mult, ALU.mult)
                lk(ins)
                for k in range(KT):
                    v.tensor_scalar(into[:, k, :], xT[:, k, :], gb[:, 1, k:k + 1], None,
                                    ALU.add).then_inc(scaled, 1)

            @block.scalar
            def _(act):
                for q in range(4):
                    act.wait_ge(centered, q + 1)
                    act.activation(sq[:, 4 * q:4 * q + 4, :], xT[:, 4 * q:4 * q + 4, :],
                                   ACT.Square).then_inc(squared, 1)
                act.wait_ge(inv_done, 1)
                act.activation(rs[:, 1, :], rs[:, 0, :], ACT.Sqrt).then_inc(rstd_done, 1)

            if out is not None:
                @block.sync
                def _(sp):
                    sp.wait_ge(scaled, KT)
                    sp.dma_start(out, into[:]).then_inc(stored, 16)
                    sp.wait_ge(stored, 16)


def sbuf_both(nc, st, name, shape):
    at = -(-nc.sbuf_base // 32) * 32
    whole = st.enter_context(nc.sbuf_tensor(name, shape, F32))
    return whole, nc.alloc_sbuf_tensor_at(f"{name}_r", shape, F32R, offset=at)


def split(cx, name, whole, high, low):
    written, done = cx.sem(f"{name}_high"), cx.sem(f"{name}_low")
    with cx.nc.Block() as block:
        @block.scalar
        def _(act):
            for q in range(4):
                act.activation(high[:, 4 * q:4 * q + 4, :], whole[:, 4 * q:4 * q + 4, :], ACT.Copy).then_inc(written, 1)

        @block.vector
        def _(v):
            for q in range(4):
                v.wait_ge(written, q + 1)
                v.tensor_tensor(low[:, 4 * q:4 * q + 4, :], whole[:, 4 * q:4 * q + 4, :],
                                high[:, 4 * q:4 * q + 4, :], ALU.subtract).then_inc(done, 1)
            v.wait_ge(done, 4)


def split_product(pe, out, w_high, w_low, high, low, start, stop):
    pe.matmul(out, w_high, high, start=start, stop=False, skip_group_check=True)
    pe.matmul(out, w_high, low, start=False, stop=False, skip_group_check=True)
    return pe.matmul(out, w_low, high, start=False, stop=stop, skip_group_check=True)


def project(cx, name, chunks, w_dram, high, low, evacuate):
    nc = cx.nc
    n = high.shape[-1]
    SL = 4
    with ExitStack() as st:
        w, w_low = zip(*(sbuf_both(nc, st, f"{name}_w{s}", [P, KT, P]) for s in range(SL)))
        w_high = [st.enter_context(nc.sbuf_tensor(f"{name}_wh{s}", [P, KT, P], F32R)) for s in range(2)]
        acc = [st.enter_context(nc.psum_tensor(f"{name}_acc{s}", [P, 512], F32)) for s in range(SL)]
        loaded = [cx.sem(f"{name}_loaded{s}") for s in range(SL)]
        summed = [cx.count(f"{name}_summed{s}") for s in range(SL)]
        emptied = [cx.count(f"{name}_emptied{s}") for s in range(SL)]
        raised = [cx.sem(f"{name}_high{s}") for s in range(SL)]
        lowered = [cx.sem(f"{name}_low{s}") for s in range(SL)]

        def body(one, eng, count):
            full = count // SL
            with eng.Fori(0, full) as i:
                for s in range(SL):
                    one(i, s)
            for s in range(count % SL):
                one(full, s)

        with cx.block() as block:
            @block.sync
            def _(sp):
                def one(i, s):
                    cx.wait(sp, summed[s], i)
                    sp.dma_start(w[s][:], w_dram[i * SL + s]).then_inc(loaded[s], 16)
                body(one, sp, chunks)

            @block.scalar
            def _(act):
                def one(i, s):
                    act.wait_ge(loaded[s], i * 16 + 16)
                    cx.wait(act, summed[(s + 2) % SL], i + 1 if s >= 2 else i)
                    act.activation(w_high[s % 2][:], w[s][:], ACT.Copy).then_inc(raised[s], 1)
                body(one, act, chunks)

            @block.tensor
            def _(pe):
                def one(i, s):
                    pe.wait_ge(lowered[s], i + 1)
                    cx.wait(pe, emptied[s], i)
                    for k in range(KT):
                        mm = split_product(pe, acc[s][:, 0:n], w_high[s % 2][:, k, :], w_low[s][:, k, :],
                                           high[:, k, :], low[:, k, :], k == 0, k == KT - 1)
                    mm.then_inc(summed[s], 1)
                body(one, pe, chunks)

            @block.vector
            def _(v):
                def lower(i, s):
                    v.wait_ge(raised[s], i + 1)
                    v.tensor_tensor(w_low[s][:], w[s][:], w_high[s % 2][:], ALU.subtract).then_inc(lowered[s], 1)

                def out(i, s):
                    cx.wait(v, summed[s], i + 1)
                    evacuate(v, i * SL + s, acc[s][:, 0:n]).then_inc(emptied[s], 1)

                def one(i, s):
                    lower(*((i, s + 1) if s < SL - 1 else (i + 1, 0)))
                    out(i, s)
                lower(0, 0)
                body(one, v, chunks - 1)
                out((chunks - 1) // SL, (chunks - 1) % SL)


def build(nc, a, o):
    cx = Ctx(nc)
    with ExitStack() as top:
        def sb(name, shape, dt=F32, stack=top):
            return stack.enter_context(nc.sbuf_tensor(name, shape, dt))

        x_rest = nc.dram_tensor("x_rest", [P, KT, N], F32, kind="Internal").ap()
        mixT, before_mix = sbuf_both(nc, top, "mixT", [P, KT, N])
        ones = sb("ones", [P, P])
        ident = sb("ident", [P, P])
        ln_gb = sb("ln_gb", [P, 3, 2, KT])
        with ExitStack() as mixer:
            projT = sb("projT", [P, NC_IN, N], stack=mixer)
            with ExitStack() as early:
                xT, x_low = sbuf_both(nc, early, "x_inT", [P, KT, N])
                cx.phase(load, "first", ((xT[:], a["xT"]), (ones[:], a["ones"]), (ident[:], a["ident"]),
                                   (ln_gb[:], a["ln_gb"])))
                cx.phase(layer_norm, "ln_in", xT, ln_gb[:, 0], ones, out=x_rest)
                cx.phase(split, "x_in", xT, before_mix, x_low)
                cx.phase(project, "in", NC_IN, a["w_in"], before_mix, x_low,
                        lambda v, c, acc: v.tensor_copy(projT[:, c, :], acc))
            cx.phase(store_projection, projT, o)
            rwkv(cx, a, o, projT, mixT, ident)
            attention(cx, a, o, projT, mixT, ident)
        with ExitStack() as late:
            xT = sb("x_midT", [P, KT, NY], stack=late)
            cx.phase(load, "rest", ((xT[:], x_rest[:, :, META:N]),))
            high, low = sb("mix_high", [P, KT, NY], F32R, late), sb("mix_low", [P, KT, NY], F32R, late)
            cx.phase(split, "mix", mixT[:, :, META:N], high, low)
            cx.phase(project, "out", KT, a["w_o"], high, low,
                    lambda v, c, acc: v.scalar_tensor_tensor(xT[:, c, :], xT[:, c, :], ALPHA, acc,
                                                             ALU.mult, ALU.add))
            cx.phase(layer_norm, "ln1", xT, ln_gb[:, 1], ones, into=mixT[:, :, META:N])
        xT = mixT[:, :, META:N]
        peer(cx, a, xT, ident)
        cx.phase(layer_norm, "ln2", xT, ln_gb[:, 2], ones, out=o["yT"])


def store_projection(cx, projT, o):
    nc = cx.nc
    with ExitStack() as st:
        last = st.enter_context(nc.sbuf_tensor("last_rows", [P, RWC, B + 1], F32))
        picked, stored = cx.sem("last_rows_picked"), cx.sem("projection_stored")
        with nc.Block() as block:
            @block.vector
            def _(v):
                v.tensor_copy(last[:], projT[:, 0:RWC, TP - 1:N:S]).then_inc(picked, 1)

            @block.sync
            def _(sp):
                sp.dma_start(o["kvT"], projT[:, C_AK:C_QI, :]).then_inc(stored, 16)
                sp.dma_start(o["kiT"], projT[:, C_KI, :]).then_inc(stored, 16)
                sp.wait_ge(picked, 1)
                sp.dma_start(o["shiftT"], last[:]).then_inc(stored, 16)
                sp.wait_ge(stored, 48)


def block_mask(seq):
    return (seq[:, None] == seq[None, :]).astype(np.float32)


def rwkv_masks():
    main = np.arange(P) // CH
    tail = np.concatenate([np.zeros(CH // 2), 10 + np.arange(TS) // S, 100 + np.arange(P - CH // 2 - TS)])
    whole = np.stack([block_mask(main), block_mask(main), block_mask(tail)])
    half = np.stack([block_mask(np.arange(P) // (CH // 2))] * 2 + [block_mask(tail)])
    s, t = np.arange(P)[:, None], np.arange(P)[None, :]
    which = [-half * (s < t), -half * (s > t), (whole - half) * (s < t), whole * (s < t), whole * (s <= t)]
    return np.stack(which).transpose(2, 0, 1, 3).astype(np.float32)


M_XT, M_X, M_OFF, M_LT, M_LE = range(5)

def rwkv_features(cx, a, projT, masks, seqmask, halves, cols, mu, shift, lw, la, ag, gg):
    nc = cx.nc
    NH = 8
    loaded, mixed, squashed, up_done, up_read = (cx.sem(f"rw_{x}") for x in
                                                 ("loaded", "mixed", "squashed", "up_done", "up_read"))
    link0 = cx.sem("rw_link0")

    def shifted(v, lk, out, feat, c0, nch):
        lk(v.tensor_tensor(out[:, :, 1:N], feat[:, :, 0:N - 1], feat[:, :, 1:N], ALU.subtract))
        lk(v.tensor_scalar(out[:, :, 0:1], feat[:, :, 0:1], -1.0, None, ALU.mult))
        lk(v.tensor_tensor(out[:, :, TP:N:S], shift[:, c0:c0 + nch, :], feat[:, :, TP:N:S], ALU.subtract))

    with ExitStack() as ps:
        def early(name, shape):
            return ps.enter_context(nc.sbuf_tensor(f"rw_{name}", shape, F32))

        w_up, g_up, g_up2 = early("w_up", [P, RW]), early("g_up", [P, RW]), early("g_up2", [32, RW])
        xl, dl = early("xl", [P, 3, N]), early("dl", [P, 3, N])
        lb = early("lb", [P, NH, N])
        block = ps.enter_context(nc.Block())
        up = [ps.enter_context(nc.psum_tensor(f"rw_up{i}", [P, 512], F32)) for i in range(2)]

        @block.sync
        def _(sp):
            n = load_all(sp, loaded, (
                (masks[:], a["rw_masks"]), (seqmask[:], a["seqmask"]), (halves[:], a["halves"]),
                (cols[:], a["rw_cols"]), (mu[:], a["mu"]), (shift[:], a["shiftT_in"]),
                (w_up[:], a["wa_up"]), (g_up[:], a["g_up"][0:P]), (g_up2[:], a["g_up"][P:P + 32])))
            assert n == 144

        @block.vector
        def _(v):
            lk = Link(v, link0)
            v.wait_ge(loaded, 144)
            shifted(v, lk, dl, projT[:, C_WA:RWC, :], C_WA, 3)
            for c in range(3):
                v.scalar_tensor_tensor(xl[:, c, :], dl[:, c, :], mu[:, C_WA + c:C_WA + c + 1],
                                       projT[:, C_WA + c, :], ALU.mult, ALU.add).then_inc(mixed, 1)
            v.wait_ge(up_read, 3 * NH)
            lk(v.tensor_scalar(lw[:], lw[:], -DECAY, None, ALU.mult))
            src, dst = lw, la
            for step in (1, 2, 4, 8, 16):
                parts = []
                for j in range(NH):
                    parts.append((lambda q, j=j: q[:, j, 0:256].rearrange("p (c t) -> p c t", t=CH)))
                if step < 16:
                    parts.append(lambda q: q[:, :, 256:TP])
                if step < 4:
                    for j in range(NH):
                        parts.append((lambda q, j=j: q[:, j, TP:N].rearrange("p (c t) -> p c t", t=S)))
                lk(v.tensor_copy(dst[:], src[:]))
                for part in parts:
                    a_, b_ = part(dst), part(src)
                    lk(v.tensor_tensor(a_[:, :, step:], b_[:, :, step:], b_[:, :, :a_.shape[2] - step], ALU.add))
                src, dst = dst, (lb if dst is la else la)
            assert src is la

        @block.scalar
        def _(act):
            act.wait_ge(mixed, 3)
            act.activation(xl[0:HD, 0, :], xl[0:HD, 0, :], ACT.Tanh).then_inc(squashed, 1)
            act.activation(xl[:, 1, :], xl[:, 1, :], ACT.Sigmoid).then_inc(squashed, 1)
            act.activation(xl[0:32, 2, :], xl[0:32, 2, :], ACT.Sigmoid).then_inc(squashed, 1)
            for j in range(NH):
                for n, (dst, bias) in enumerate(((lw, 6), (ag, 7), (gg, None))):
                    u = 3 * j + n
                    act.wait_ge(up_done, u + 1)
                    if bias is None:
                        ins = act.activation(dst[:, j, :], up[u % 2][:, 0:N], ACT.Copy)
                    else:
                        ins = act.activation(dst[:, j, :], up[u % 2][:, 0:N], ACT.Sigmoid,
                                             bias=cols[:, j, bias:bias + 1])
                    ins.then_inc(up_read, 1)

        @block.tensor
        def _(pe):
            pe.wait_ge(loaded, 144)
            pe.wait_ge(squashed, 3)
            for j in range(NH):
                c = slice(j * P, j * P + P)
                for n in range(3):
                    u = 3 * j + n
                    if u >= 2:
                        pe.wait_ge(up_read, u - 1)
                    if n == 0:
                        mm = pe.matmul(up[u % 2][:, 0:N], w_up[0:HD, c], xl[0:HD, 0, :], start=True, stop=True)
                    elif n == 1:
                        mm = pe.matmul(up[u % 2][:, 0:N], w_up[HD:P, c], xl[HD:P, 0, :], start=True, stop=True)
                    else:
                        pe.matmul(up[u % 2][:, 0:N], g_up[:, c], xl[:, 1, :], start=True, stop=False)
                        mm = pe.matmul(up[u % 2][:, 0:N], g_up2[:, c], xl[0:32, 2, :], start=False, stop=True)
                    mm.then_inc(up_done, 1)


def rwkv(cx, a, o, projT, mixT, ident):
    nc = cx.nc
    NH = 8
    with ExitStack() as st:
        def sb(name, shape, dt=F32):
            return st.enter_context(nc.sbuf_tensor(f"rw_{name}", shape, dt))

        masks = sb("masks", [P, 5, 3, P])
        seqmask = sb("seqmask", [P, B])
        halves = sb("halves", [P, P])
        cols = sb("cols", [P, 8, 10])
        mu = sb("mu", [P, RWC])
        shift = sb("shift", [P, RWC, B])
        lw, ag, gg = sb("lw", [P, NH, N]), sb("ag", [P, NH, N]), sb("gg", [P, NH, N])
        la = sb("la", [P, NH, N])
        cx.phase(rwkv_features, a, projT, masks, seqmask, halves, cols, mu, shift, lw, la, ag, gg)
        cx.phase(rwkv_heads, a, o, projT, mixT, ident, masks, seqmask, halves, cols, shift, lw, la, ag)
        cx.phase(rwkv_finish, mixT, halves, cols, gg)


def rwkv_heads(cx, a, o, projT, mixT, ident, masks, seqmask, halves, cols, shift, lw, la, ag):
    nc = cx.nc
    NH = 8
    N3 = 3 * P
    pe_names = ["pairs", "lk", "x2", "x4", "x8", "rowsa", "t8", "rowsb", "pre", "a1", "z2", "wu", "mix",
                "q", "g", "gs"] + [f"state{c}" for c in range(9)] + ["samples"]
    dv_names = ["x", "lk", "x2", "x4", "t2", "x8", "t3", "rowsa", "rowsb", "kl", "a1",
                "z2", "wu", "mix", "g", "gs"] + [f"state{c}" for c in range(9)] + ["samples"]
    ft_names = ["products", "features"]
    ac_names = ["roots", "exps"]
    PREPARED = 5
    with ExitStack() as st:
        def sb(name, shape, dt=F32):
            return st.enter_context(nc.sbuf_tensor(f"rh_{name}", shape, dt))

        df = sb("df", [P, 3, N])
        rkv = sb("rkv", [P, 3, N3])
        xx = sb("xx", [P, 2, N])
        kk, kh, bh = sb("kk", [P, N]), sb("kh", [P, N]), sb("bh", [P, N])
        lbef = sb("lbef", [P, N])
        dec, decb, inv = sb("dec", [P, N]), sb("decb", [P, N]), sb("inv", [P, N])
        KT_, RT_, kT_, bT_ = sb("K", [P, N3]), sb("R", [P, N3]), sb("k", [P, N3]), sb("b", [P, N3])
        cs = sb("colsj", [P, 10])
        dend = sb("dend", [P, 9 + B])
        arena = sb("arena", [P, 11, 6 * P])
        X, XT, X4, WU, X4T, X2, X2T, T0, T1, OFF, LkT = (
            arena[:, n, :].rearrange("p (h t c) -> p h t c", h=2, t=3) for n in range(11))
        MkT, MbT = X, XT
        WU = arena[:, 3, :].rearrange("p (t a c) -> p t a c", t=3, a=2)
        late = arena[:].rearrange("p n c -> p (n c)")[:, 4 * 6 * P:]
        rows = sb("rows", [P, 4, 3, P])
        KL, A1 = X2, X2T
        QT = sb("QT", [P, N3])
        G = late[:, 0:9 * P].rearrange("p (c d) -> p c d", d=P)
        GS, bx, vx, ux = (late[:, (9 + 8 * n) * P:(17 + 8 * n) * P].rearrange("p (b d) -> p b d", d=P)
                          for n in range(4))
        state = sb("state", [P, 10, P])
        ss_in, ss_out = sb("ss_in", [P, B, P]), sb("ss_out", [P, B, P])
        twice = lambda name: st.enter_context(nc.psum_tensor(f"rh_{name}", [P, 2, 512], F32))
        once = lambda name: st.enter_context(nc.psum_tensor(f"rh_{name}", [P, 512], F32))
        pA, pB, pC, pY, pS = twice("pA"), twice("pB"), twice("pC"), once("pY"), once("pS")
        flat = lambda bank: bank[:].rearrange("p a c -> p (a c)")
        mats = lambda bank: bank[:, :, 0:3 * P].rearrange("p h (t c) -> p h t c", t=3)
        mat = lambda bank, t, h: bank[:, h, t * P:t * P + P]
        mask = lambda which: masks[:, which:which + 1, :, :].to_broadcast([P, 2, 3, P])
        pe_step, dv_step, ac_step = cx.sem("rh_pe_step"), cx.count("rh_dve_step"), cx.sem("rh_act_step")
        ft_step, normed = cx.sem("rh_feature_step"), cx.sem("rh_norms")
        link, gate = cx.sem("rh_link"), cx.sem("rh_gate")
        ss_loaded, stored = cx.sem("rh_ss_loaded"), cx.count("rh_stored")
        copied = cx.sem("rh_copied")

        def at(names, i, name):
            return i * len(names) + names.index(name) + 1

        def stepper(sem, names):
            left = list(names)

            def done(ins, name):
                assert left.pop(0) == name, name
                ins.then_inc(sem, 1)
            return done, left

        halves_of = [(0, slice(0, HD)), (1, slice(HD, P))]
        tiles = range(3)

        def chunk_rows(c):
            n = CH if c < 8 else CH // 2
            return slice(c * CH, c * CH + n), c // 4, slice((c % 4) * CH, (c % 4) * CH + n)

        def every_pair(eng, turn):
            with eng.Fori(0, NH - 1) as i:
                turn(i, i + 1)
            turn(NH - 1, None)

        with cx.block() as block:
            @block.tensor
            def _(pe):
                def norms(j):
                    pe.wait_ge(ft_step, at(ft_names, j, "products"))
                    pe.matmul(pA[:, 0, 0:N], halves[:], xx[:, 0, :], start=True, stop=True)
                    pe.matmul(pA[:, 1, 0:N], halves[:], xx[:, 1, :], start=True, stop=True).then_inc(normed, 1)

                def turn(i, following):
                    done, left = stepper(pe_step, pe_names)
                    need = lambda name: cx.wait(pe, dv_step, at(dv_names, i, name))

                    def every(bank, lhs, rhs):
                        for t in tiles:
                            for h, r in halves_of:
                                mm = pe.matmul(mat(bank, t, h), lhs(t, h, r), rhs(t, h, r), start=True, stop=True)
                        return mm

                    feat = lambda q: (lambda t, h, r: q[r, t * P:t * P + P])
                    sq = lambda q: (lambda t, h, r: q[:, h, t, :])
                    pe.wait_ge(ft_step, at(ft_names, i, "features"))
                    every(pA, feat(bT_), feat(KT_))
                    done(every(pB, feat(KT_), feat(bT_)), "pairs")
                    done(every(pC, feat(kT_), feat(KT_)), "lk")
                    need("x")
                    every(pA, sq(XT), sq(X))
                    done(every(pB, sq(X), sq(XT)), "x2")
                    need("x2")
                    pe.wait_ge(copied, i * 2 + 1)
                    every(pA, sq(X2T), sq(X2))
                    every(pB, sq(X2), sq(X2T))
                    done(every(pC, sq(X2), sq(T0)), "x4")
                    need("x4")
                    need("t2")
                    pe.wait_ge(copied, i * 2 + 2)
                    every(pA, sq(X4T), sq(X4))
                    done(every(pC, sq(X4), sq(T1)), "x8")
                    for n, src in enumerate((KT_, kT_)):
                        for t in tiles:
                            at_ = (n * 3 + t) * P
                            mm = pe.transpose(pB[:, at_ // 512, at_ % 512:at_ % 512 + P], src[:, t * P:t * P + P],
                                              ident[:])
                    done(mm, "rowsa")
                    need("x8")
                    done(every(pC, sq(X2), sq(T0)), "t8")
                    need("rowsa")
                    for n, src in enumerate((bT_, rkv[:, 2, :])):
                        for t in tiles:
                            at_ = (n * 3 + t) * P
                            mm = pe.transpose(pB[:, at_ // 512, at_ % 512:at_ % 512 + P], src[:, t * P:t * P + P],
                                              ident[:])
                    done(mm, "rowsb")
                    need("rowsb")
                    for t in tiles:
                        for h, r in halves_of:
                            mm = pe.matmul(mat(pA, t, h)[:, 0:HD], LkT[:, h, t, :], rows[:, 3, t, r],
                                           start=True, stop=True)
                    done(mm, "pre")
                    need("t3")
                    need("kl")
                    done(every(pB, sq(T1), sq(KL)), "a1")
                    need("a1")
                    done(every(pA, sq(OFF), sq(A1)), "z2")
                    need("z2")
                    done(every(pB, sq(T1), sq(KL)), "wu")
                    every(pC, feat(kT_), feat(RT_))
                    done(every(pA, feat(bT_), feat(RT_)), "mix")
                    need("wu")
                    need("mix")
                    for h, r in halves_of:
                        for t in tiles:
                            mm = pe.matmul(pS[r, t * P:t * P + P], WU[:, t, 0, r], MbT[:, h, t, :],
                                           start=t == 0, stop=True, skip_group_check=True)
                    done(mm, "q")
                    gbank = (pB[:, 0], pB[:, 1], pC[:, 0], pC[:, 1])
                    for c in range(9):
                        _, t, cr = chunk_rows(c)
                        mm = pe.matmul(gbank[c % 4][:, (c // 4) * P:(c // 4) * P + P], WU[cr, t, 0, :],
                                       rows[cr, 2, t, :], start=True, stop=True)
                    done(mm, "g")
                    for q in range(2):
                        mm = pe.matmul(pA[:, q, :], WU[:, 2, 0, :], bx[:, 4 * q:4 * q + 4, :].rearrange("p b d -> p (b d)"),
                                       start=True, stop=True)
                    done(mm, "gs")
                    for h, r in halves_of:
                        for t in tiles:
                            pe.matmul(pY[r, t * P:t * P + P], rows[:, 3, t, r], MkT[:, h, t, :],
                                      start=t == 0, stop=False, skip_group_check=True)
                            pe.matmul(pY[r, t * P:t * P + P], WU[:, t, 1, r], MbT[:, h, t, :],
                                      start=False, stop=False, skip_group_check=True)
                    sums = (pS[:, 0:P], pB[:, 0, 0:P])

                    def begin(c):
                        _, t, cr = chunk_rows(c)
                        pe.matmul(sums[c % 2], rows[cr, 1, t, :], rows[cr, 3, t, :], start=True, stop=False)
                        pe.matmul(sums[c % 2], rows[cr, 2, t, :], WU[cr, t, 1, :], start=False, stop=False)

                    def samples(c):
                        if c == 0:
                            need("gs")
                            pe.wait_ge(ss_loaded, i * 16 + 16)
                        if c < 2:
                            four = lambda x: x[:, 4 * c:4 * c + 4, :].rearrange("p b d -> p (b d)")
                            pe.matmul(pC[:, c, :], rows[:, 1, 2, :], four(vx), start=True, stop=False,
                                      skip_group_check=True)
                            pe.matmul(pC[:, c, :], rows[:, 2, 2, :], four(ux), start=False, stop=False,
                                      skip_group_check=True)
                        elif c < 6:
                            for b in (2 * c - 4, 2 * c - 3):
                                toks = slice(TP + b * S, TP + b * S + S)
                                pe.matmul(pC[:, b // 4, (b % 4) * P:(b % 4) * P + P], GS[:, b, :], ss_in[:, b, :],
                                          start=False, stop=True, skip_group_check=True)
                                pe.matmul(pY[:, toks], ss_in[:, b, :], QT[:, toks], start=False, stop=True,
                                          skip_group_check=True)

                    need("g")
                    begin(0)
                    for c in range(9):
                        toks, t, cr = chunk_rows(c)
                        if c:
                            need(f"state{c - 1}")
                        done(pe.matmul(sums[c % 2], G[:, c, :], state[:, c, :], start=False, stop=True), f"state{c}")
                        mm = pe.matmul(pY[:, toks], state[:, c, :], QT[:, toks], start=False, stop=True,
                                       skip_group_check=True)
                        if c < 8:
                            begin(c + 1)
                            samples(c)
                        if c == PREPARED - 1 and following is not None:
                            norms(following)
                    done(mm, "samples")
                    assert not left
                norms(0)
                every_pair(pe, turn)

            @block.scalar
            def _(act):
                def features(j, before):
                    done, _ = stepper(ac_step, ac_names)
                    act.wait_ge(normed, j + 1)
                    done(act.activation(bh[:], pA[:, 0, 0:N], ACT.Sqrt), "roots")
                    if before is not None:
                        cx.wait(act, dv_step, at(dv_names, before, "g"))
                    act.activation(dec[:], la[:, j, :], ACT.Exp)
                    act.activation(inv[:], la[:, j, :], ACT.Exp, scale=-1.0)
                    done(act.activation(decb[:], lbef[:], ACT.Exp), "exps")

                def copies(i):
                    for name, power in (("x2", X2T), ("x4", X4T)):
                        act.wait_ge(pe_step, at(pe_names, i, name))
                        act.activation(power[:], mats(pB), ACT.Copy).then_inc(copied, 1)
                features(0, None)
                with act.Fori(0, NH - 1) as i:
                    copies(i)
                    features(i + 1, i)
                copies(NH - 1)

            @block.vector
            def _(v):
                lk = Link(v, link)
                for q in (KT_, RT_, kT_, bT_):
                    lk(v.memset(q[:, N:N3], 0.0))
                lk(v.memset(rkv[:, :, N:N3], 0.0))
                lk(v.memset(state[:, 0, :], 0.0))
                proj3 = projT[:, 0:24, :].rearrange("p (a j) n -> p a j n", j=NH)
                shift3 = shift[:, 0:24, :].rearrange("p (a j) b -> p a j b", j=NH)
                r_, k_, v_ = (rkv[:, n, 0:N] for n in range(3))

                def ft_done(ins, j, name):
                    ins.then_inc(ft_step, 1)
                    v.wait_ge(ft_step, at(ft_names, j, name))

                def products(j, part):
                    f = proj3[:, :, j, :]
                    if part == 0:
                        lk(v.tensor_copy(cs[:], cols[:, j, :]))
                        lk(v.tensor_tensor(df[:, :, 1:N], f[:, :, 0:N - 1], f[:, :, 1:N], ALU.subtract))
                        lk(v.tensor_scalar(df[:, :, 0:1], f[:, :, 0:1], -1.0, None, ALU.mult))
                        lk(v.tensor_tensor(df[:, :, TP:N:S], shift3[:, :, j, :], f[:, :, TP:N:S], ALU.subtract))
                    elif part == 1:
                        for n in range(2):
                            lk(v.scalar_tensor_tensor(rkv[:, n, 0:N], df[:, n, :], cs[:, n:n + 1], f[:, n, :],
                                                      ALU.mult, ALU.add))
                    elif part == 2:
                        lk(v.scalar_tensor_tensor(rkv[:, 2, 0:N], df[:, 2, :], cs[:, 2:3], f[:, 2, :],
                                                  ALU.mult, ALU.add))
                        lk(v.tensor_tensor(lbef[:], la[:, j, :], lw[:, j, :], ALU.subtract))
                    elif part == 3:
                        lk(v.tensor_scalar(kk[:], k_, cs[:, 3:4], None, ALU.mult))
                        lk(v.tensor_tensor(xx[:, 0, :], kk[:], kk[:], ALU.mult))
                    else:
                        lk(v.tensor_scalar(kh[:], ag[:, j, :], -1.0, cs[:, 4:5], ALU.add, ALU.mult))
                        lk(v.scalar_tensor_tensor(kh[:], kh[:], 1.0, k_, ALU.add, ALU.mult))
                        ft_done(v.scalar_tensor_tensor(xx[:, 1, :], r_, cs[:, 5:6], kh[:], ALU.mult, ALU.mult),
                                j, "products")

                def features(j):
                    v.wait_ge(ac_step, at(ac_names, j, "exps"))
                    lk(v.tensor_scalar(bh[:], bh[:], 1e-12, None, ALU.max))
                    lk(v.reciprocal(bh[:], bh[:]))
                    lk(v.tensor_tensor(kk[:], kk[:], bh[:], ALU.mult))
                    lk(v.tensor_tensor(mixT[:, 8:16][:, j, :], v_, pA[:, 1, 0:N], ALU.mult))
                    lk(v.tensor_tensor(KT_[:, 0:N], kk[:], decb[:], ALU.mult))
                    lk(v.tensor_tensor(bh[:], kk[:], ag[:, j, :], ALU.mult))
                    lk(v.tensor_tensor(RT_[:, 0:N], r_, dec[:], ALU.mult))
                    lk(v.tensor_tensor(kT_[:, 0:N], kh[:], inv[:], ALU.mult))
                    ft_done(v.tensor_tensor(bT_[:, 0:N], bh[:], inv[:], ALU.mult), j, "features")

                def turn(i, following):
                    signal, left = stepper(dv_step, dv_names)

                    def done(ins, name):
                        signal(ins, name)
                        cx.wait(v, dv_step, at(dv_names, i, name))
                    need = lambda name: v.wait_ge(pe_step, at(pe_names, i, name))
                    need("pairs")
                    lk(v.tensor_tensor(XT[:], mats(pA), mask(M_XT), ALU.mult))
                    lk(v.tensor_tensor(OFF[:], mats(pA), mask(M_OFF), ALU.mult))
                    lk(v.tensor_tensor(T0[:], XT[:], ident[:].rearrange("p (a b c) -> p a b c", a=1, b=1)
                                       .to_broadcast([P, 2, 3, P]), ALU.add))
                    done(v.tensor_tensor(X[:], mats(pB), mask(M_X), ALU.mult), "x")
                    need("lk")
                    done(v.tensor_tensor(LkT[:], mats(pC), mask(M_LT), ALU.mult), "lk")
                    need("x2")
                    done(v.tensor_copy(X2[:], mats(pA)), "x2")
                    need("x4")
                    done(v.tensor_copy(X4[:], mats(pA)), "x4")
                    done(v.tensor_tensor(T1[:], T0[:], mats(pC), ALU.add), "t2")
                    need("x8")
                    lk(v.tensor_copy(X2[:], mats(pA)))
                    done(v.tensor_tensor(T0[:], T1[:], mats(pC), ALU.add), "x8")
                    need("t8")
                    done(v.tensor_tensor(T1[:], T0[:], mats(pC), ALU.add), "t3")
                    need("rowsa")
                    both = flat(pB)[:, 0:6 * P].rearrange("p (n t c) -> p n t c", n=2, t=3)
                    done(v.tensor_copy(rows[:, 0:2], both), "rowsa")
                    need("rowsb")
                    done(v.tensor_copy(rows[:, 2:4], both), "rowsb")
                    need("pre")
                    lk(v.tensor_copy(KL[:, :, :, 0:HD], rows[:, 0].rearrange("p t (h c) -> p h t c", h=2)))
                    done(v.tensor_copy(KL[:, :, :, HD:P], mats(pA)[:, :, :, 0:HD]), "kl")
                    need("a1")
                    done(v.tensor_copy(A1[:], mats(pB)), "a1")
                    need("z2")
                    done(v.tensor_tensor(KL[:], KL[:], mats(pA), ALU.subtract), "z2")
                    need("wu")
                    w4 = WU.rearrange("p t a (h d) -> p a h t d", h=2)
                    lk(v.tensor_scalar(w4[:, 0], mats(pB)[:, :, :, 0:HD], -1.0, None, ALU.mult))
                    done(v.tensor_scalar(w4[:, 1], mats(pB)[:, :, :, HD:P], -1.0, None, ALU.mult), "wu")
                    seq = seqmask[:].rearrange("p (b o) -> p b o", o=1).to_broadcast([P, B, P])
                    for dst, src in ((bx, rows[:, 2, 2:3, :]), (vx, rows[:, 3, 2:3, :]), (ux, WU[:, 2:3, 1, :])):
                        lk(v.tensor_tensor(dst[:], src.to_broadcast([P, B, P]), seq, ALU.mult))
                    need("mix")
                    lk(v.tensor_tensor(MkT[:], mats(pC), mask(M_LE), ALU.mult))
                    done(v.tensor_tensor(MbT[:], mats(pA), mask(M_LE), ALU.mult), "mix")
                    lk(v.tensor_copy(dend[:, 0:8], dec[:, CH - 1:8 * CH:CH]))
                    lk(v.tensor_copy(dend[:, 8:9], dec[:, TP - 1:TP]))
                    lk(v.tensor_copy(dend[:, 9:9 + B], dec[:, TP + S - 1:N:S]))
                    need("q")
                    lk(v.tensor_tensor(QT[:], RT_[:], pS[:, 0:N3], ALU.add))
                    one = ident[:].rearrange("p (o d) -> p o d", o=1)
                    need("g")
                    for q, bank in enumerate((pB[:, 0], pB[:, 1], pC[:, 0], pC[:, 1])):
                        n = 3 if q == 0 else 2
                        ins = v.tensor_tensor(G[:, q:9:4, :], bank[:, 0:n * P].rearrange("p (c d) -> p c d", d=P),
                                              one.to_broadcast([P, n, P]), ALU.add)
                    done(ins, "g")
                    need("gs")
                    done(v.tensor_tensor(GS[:], pA[:].rearrange("p a (c d) -> p (a c) d", d=P),
                                         one.to_broadcast([P, B, P]), ALU.add), "gs")
                    cx.wait(v, stored, i * 64)
                    for c in range(9):
                        if c < PREPARED and following is not None:
                            products(following, c)
                        need(f"state{c}")
                        done(v.scalar_tensor_tensor(state[:, c + 1, :], (pS[:, 0:P], pB[:, 0, 0:P])[c % 2],
                                                    dend[:, c:c + 1], halves[:], ALU.mult, ALU.mult), f"state{c}")
                    need("samples")
                    lk(v.tensor_tensor(ss_out[:], pC[:].rearrange("p a (c d) -> p (a c) d", d=P),
                                       dend[:, 9:9 + B].rearrange("p (b o) -> p b o", o=1)
                                       .to_broadcast([P, B, P]), ALU.mult))
                    done(v.tensor_copy(mixT[:, 0:8][:, i, :], pY[:, 0:N]), "samples")
                    if following is not None:
                        features(following)
                    assert not left
                for part in range(PREPARED):
                    products(0, part)
                features(0)
                with v.Fori(0, NH - 1) as i:
                    lk.enter(i, LINKS_RW)
                    turn(i, i + 1)
                    lk.leave(NH - 1)
                turn(NH - 1, None)

            @block.sync
            def _(sp):
                with sp.Fori(0, NH) as i:
                    sp.dma_start(ss_in[:], a["wkvT"][i]).then_inc(ss_loaded, 16)
                    cx.wait(sp, dv_step, at(dv_names, i, "samples"))
                    for h, r in halves_of:
                        sp.dma_start(o["wkvT_s"][i, r], ss_out[r, :, r]).then_inc(stored, 16)
                        sp.dma_start(o["wkvT_p"][i, r], state[r, 9, r]).then_inc(stored, 16)
                    cx.wait(sp, stored, i * 64 + 64, gate)


LINKS_RW = 35


def rwkv_finish(cx, mixT, halves, cols, gg):
    nc = cx.nc
    with ExitStack() as st:
        sq = st.enter_context(nc.sbuf_tensor("rf_sq", [P, 2, N], F32))
        rs = st.enter_context(nc.sbuf_tensor("rf_rs", [P, 2, N], F32))
        pm = [st.enter_context(nc.psum_tensor(f"rf_m{k}", [P, 512], F32)) for k in range(2)]
        pv = [st.enter_context(nc.psum_tensor(f"rf_v{k}", [P, 512], F32)) for k in range(2)]
        mean, squared, var, inv, root, link, centered = (cx.sem(f"rf_{q}") for q in
            ("mean", "squared", "var", "inv", "root", "link", "centered"))
        with nc.Block() as block:
            @block.tensor
            def _(pe):
                for j in range(8):
                    if j >= 2:
                        pe.wait_ge(centered, j - 1)
                    pe.matmul(pm[j % 2][:, 0:N], halves[:], mixT[:, j, :], start=True, stop=True).then_inc(mean, 1)
                    pe.wait_ge(squared, j + 1)
                    if j >= 2:
                        pe.wait_ge(inv, j - 1)
                    pe.matmul(pv[j % 2][:, 0:N], halves[:], sq[:, j % 2, :], start=True, stop=True).then_inc(var, 1)

            @block.vector
            def _(v):
                lk = Link(v, link)
                for j in range(8):
                    y = mixT[:, j, :]
                    v.wait_ge(mean, j + 1)
                    v.scalar_tensor_tensor(y, pm[j % 2][:, 0:N], -1.0 / HD, y, ALU.mult, ALU.add).then_inc(centered, 1)
                    v.wait_ge(var, j + 1)
                    lk(v.tensor_scalar(rs[:, 0, :], pv[j % 2][:, 0:N], 1.0 / HD, GN_EPS, ALU.mult, ALU.add))
                    v.reciprocal(rs[:, 0, :], rs[:, 0, :]).then_inc(inv, 1)
                    v.wait_ge(root, j + 1)
                    lk(v.scalar_tensor_tensor(y, y, cols[:, j, 8:9], rs[:, 1, :], ALU.mult, ALU.mult))
                    lk(v.scalar_tensor_tensor(y, y, cols[:, j, 9:10], mixT[:, 8 + j, :], ALU.add, ALU.add))
                    lk(v.tensor_tensor(y, y, gg[:, j, :], ALU.mult))

            @block.scalar
            def _(act):
                for j in range(8):
                    act.wait_ge(centered, j + 1)
                    act.activation(sq[:, j % 2, :], mixT[:, j, :], ACT.Square).then_inc(squared, 1)
                    act.wait_ge(inv, j + 1)
                    act.activation(rs[:, 1, :], rs[:, 0, :], ACT.Sqrt).then_inc(root, 1)


FAR = PAST - PAGE
QT_TILES = ((0, 128), (128, 128), (256, 16))
WORK_S = PAST + S + 8


def bucket(dist):
    exact = NB_BUCKETS // 2
    d = np.maximum(dist, 0)
    far = exact + (np.log(np.maximum(d, 1).astype(np.float32) / exact) / np.log(MAX_DIST / exact)
                   * (NB_BUCKETS - exact)).astype(np.int32)
    return np.where(d < exact, d, np.minimum(far, NB_BUCKETS - 1))


def attention(cx, a, o, projT, mixT, ident):
    nc = cx.nc
    bias_rows = nc.dram_tensor("bias_rows", [16, 2 * TP], F32, kind="Internal").ap()
    with ExitStack() as st:
        def sb(name, shape, dt=F32):
            return st.enter_context(nc.sbuf_tensor(f"at_{name}", shape, dt))

        wrow = sb("wrow", [P, 3, IH])
        wsel = sb("wsel", [TS, B, TS])
        vrows = sb("vrows", [P, 3, 2 * P])
        vnew = sb("vnew", [S, B, 2 * P])
        mask_p = sb("mask_p", [P, 3, TP])
        mask_s = sb("mask_s", [TS + 1, PAST + S])
        sel = sb("sel", [TS + 1, B, 64])
        near = sb("near", [P, 64])
        rel = sb("rel", [P, 16])
        onehot = sb("onehot", [P, PAGE + S])
        cx.phase(attention_tables, a, projT, ident, bias_rows, wrow, wsel, vrows, vnew, sel, near, rel, onehot)
        cx.phase(index_prompt, a, projT, wrow, mask_p)
        with ExitStack() as picking:
            work_s = picking.enter_context(nc.sbuf_tensor("at_work_s", [TS, WORK_S], F32))
            newmask = picking.enter_context(nc.sbuf_tensor("at_newmask", [TS, S], F32))
            cx.phase(index_sampled, a, projT, wsel, mask_s, work_s, newmask)
            cx.phase(attend_prompt, a, projT, mixT, ident, mask_p, vrows, bias_rows, mask_s, work_s, newmask)
        cx.phase(attend_sampled, a, projT, mixT, ident, mask_s, sel, near, onehot, vnew)


def attention_tables(cx, a, projT, ident, bias_rows, wrow, wsel, vrows, vnew, sel, near, rel, onehot):
    nc = cx.nc
    with ExitStack() as st:
        def sb(name, shape, dt=F32):
            return st.enter_context(nc.sbuf_tensor(f"tb_{name}", shape, dt))

        pv = st.enter_context(nc.psum_tensor("tb_pv", [P, 2, 512], F32))
        pn = st.enter_context(nc.psum_tensor("tb_pn", [P, 4, 512], F32))
        pw = st.enter_context(nc.psum_tensor("tb_pw", [P, 512], F32))
        pr = st.enter_context(nc.psum_tensor("tb_pr", [P, 512], F32))
        spread = sb("spread", [IH, TS])
        wpick = sb("wpick", [TS, B, TS])
        spick = sb("spick", [P, 16, S])
        table = sb("table", [NB_BUCKETS, 2 * TP])
        brow = sb("brow", [16, 2 * TP])
        far = sb("far", [TS + 1, 16])
        loaded, turned, biased, brow_done, stored = (cx.sem(f"tb_{x}") for x in
                                                     ("loaded", "turned", "biased", "brow", "stored"))
        with nc.Block() as block:
            @block.sync
            def _(sp):
                rb = a["rel_bias"]
                n = load_all(sp, loaded, (
                    (spread[:], a["spread"]), (wpick[:], a["wpick"]), (spick[:], a["spick"]),
                    (table[:], a["bucket_table"]), (sel[0:TS], a["sel"]), (onehot[:], a["near_onehot"]),
                    (far[TS:TS + 1, :], rb[NB_BUCKETS - 1:NB_BUCKETS, :]),
                    *((rel[s * 32:s * 32 + 32, :], rb) for s in range(S))))
                assert n == 176
                sp.wait_ge(brow_done, 2)
                sp.dma_start(bias_rows, brow[:]).then_inc(stored, 16)
                sp.wait_ge(stored, 16)

            @block.tensor
            def _(pe):
                pe.wait_ge(loaded, 176)
                for t, (t0, m) in enumerate(QT_TILES):
                    pe.transpose(pw[0:m, t * 8:t * 8 + 8], projT[0:IH, C_WI, t0:t0 + m], ident[0:IH, 0:IH])
                pe.matmul(pw[0:TS, 64:64 + TS], spread[:], projT[0:IH, C_WI, TP:N], start=True, stop=True)
                for t, (t0, m) in enumerate(QT_TILES):
                    for p in range(2):
                        q = (2 * t + p) * P
                        pe.transpose(pv[0:m, q // 512, q % 512:q % 512 + P], projT[:, C_AV + p, t0:t0 + m], ident[:])
                for b in range(B):
                    for p in range(2):
                        q = (2 * b + p) * P
                        mm = pe.transpose(pn[0:S, q // 512, q % 512:q % 512 + P],
                                          projT[:, C_AV + p, TP + b * S:TP + b * S + S], ident[:])
                mm.then_inc(turned, 1)
                for h in range(2):
                    if h:
                        pe.wait_ge(brow_done, 1)
                    pe.matmul(pr[0:16, 0:TP], rel[0:NB_BUCKETS, :], table[:, h * TP:h * TP + TP],
                              start=True, stop=True).then_inc(biased, 1)

            @block.vector
            def _(v):
                v.wait_ge(turned, 1)
                for t, (t0, m) in enumerate(QT_TILES):
                    v.tensor_copy(wrow[0:m, t, :], pw[0:m, t * 8:t * 8 + 8])
                    for p in range(2):
                        q = (2 * t + p) * P
                        v.tensor_copy(vrows[0:m, t, p * P:p * P + P], pv[0:m, q // 512, q % 512:q % 512 + P])
                v.tensor_tensor(wsel[:], wpick[:], pw[0:TS, 64:64 + TS].rearrange("p (o n) -> p o n", o=1)
                                .to_broadcast([TS, B, TS]), ALU.mult)
                v.tensor_copy(vnew[:].rearrange("p b c -> p (b c)"), pn[0:S].rearrange("p a c -> p (a c)"))
                v.tensor_tensor(near[:].rearrange("p (h s) -> p h s", s=S), spick[:],
                                rel[:].rearrange("p (h o) -> p h o", o=1).to_broadcast([P, 16, S]), ALU.mult)
                for b in range(B):
                    v.tensor_copy(sel[TS:TS + 1, b, :].rearrange("p (h s) -> p h s", s=S),
                                  far[TS:TS + 1, :].rearrange("p (h o) -> p h o", o=1).to_broadcast([1, 16, S]))
                for h in range(2):
                    v.wait_ge(biased, h + 1)
                    v.tensor_copy(brow[:, h * TP:h * TP + TP], pr[0:16, 0:TP]).then_inc(brow_done, 1)


def take_top(v, lk, best, work, rounds, last=None):
    for n in range(rounds):
        lk(v.max(best, work))
        lk(v.match_replace(work, best, work, MARK))
    if last:
        lk(v.max(best, work))
        lk(v.memset(best[:, last:8], PAD))
        lk(v.match_replace(work, best, work, MARK))


def index_prompt(cx, a, projT, wrow, mask_p):
    nc = cx.nc
    with ExitStack() as st:
        def sb(name, shape, dt=F32):
            return st.enter_context(nc.sbuf_tensor(f"ip_{name}", shape, dt))

        relu = [sb(f"relu{k}", [P, TP]) for k in range(3)]
        work = sb("work", [P, 3, TP + 8])
        causal = sb("causal", [P, 3, TP])
        best = sb("best", [P, 8])
        banks = [st.enter_context(nc.psum_tensor(f"ip_p{k}", [P, 512], F32)) for k in range(4)]
        loaded, scored, relued, added, link = (cx.sem(f"ip_{x}") for x in
                                               ("loaded", "scored", "relued", "added", "link"))
        with nc.Block() as block:
            @block.sync
            def _(sp):
                sp.dma_start(causal[:], a["causal"]).then_inc(loaded, 16)

            @block.tensor
            def _(pe):
                for t, (t0, m) in enumerate(QT_TILES):
                    for h in range(IH):
                        u = t * IH + h
                        if u >= 4:
                            pe.wait_ge(relued, u - 3)
                        pe.matmul(banks[u % 4][0:m, 0:TP], projT[:, C_QI + h, t0:t0 + m], projT[:, C_KI, 0:TP],
                                  start=True, stop=True).then_inc(scored, 1)

            @block.scalar
            def _(act):
                for t, (t0, m) in enumerate(QT_TILES):
                    for h in range(IH):
                        u = t * IH + h
                        act.wait_ge(scored, u + 1)
                        if u >= 3:
                            act.wait_ge(added, u - 2)
                        act.activation(relu[u % 3][0:m, :], banks[u % 4][0:m, 0:TP], ACT.Relu).then_inc(relued, 1)

            @block.vector
            def _(v):
                lk = Link(v, link)
                v.wait_ge(loaded, 16)
                lk(v.memset(work[:, :, TP:TP + 8], PAD))
                for t, (t0, m) in enumerate(QT_TILES):
                    w = work[0:m, t, 0:TP]
                    for h in range(IH):
                        u = t * IH + h
                        v.wait_ge(relued, u + 1)
                        if h:
                            v.wait_ge(added, u)
                        prev = w if h else causal[0:m, t, :]
                        v.scalar_tensor_tensor(w, relu[u % 3][0:m, :], wrow[0:m, t, h:h + 1], prev,
                                               ALU.mult, ALU.add).then_inc(added, 1)
                    v.wait_ge(added, t * IH + IH)
                    take_top(v, lk, best[0:m, :], work[0:m, t, :], TOPK_P // 8, TOPK_P % 8)
                    lk(v.tensor_scalar(mask_p[0:m, t, :], w, MARK / 2, NEG, ALU.is_gt, ALU.mult))
                    lk(v.tensor_tensor(mask_p[0:m, t, :], mask_p[0:m, t, :], causal[0:m, t, :], ALU.add))


def attend_prompt(cx, a, projT, mixT, ident, mask_p, vrows, bias_rows, mask_s, work_s, newmask):
    nc = cx.nc
    with ExitStack() as st:
        def sb(name, shape, dt=F32):
            return st.enter_context(nc.sbuf_tensor(f"pp_{name}", shape, dt))

        bias = sb("bias", [P, 3, 16, TP])
        flip = sb("flip", [P, 2, P])
        qs = [sb(f"q{k}", [P, TP]) for k in range(2)]
        prob = [sb(f"prob{k}", [P, TP]) for k in range(3)]
        stat = [sb(f"stat{k}", [P, 4]) for k in range(2)]
        pT = [sb(f"pT{k}", [P, 3, TP]) for k in range(2)]
        banks = [st.enter_context(nc.psum_tensor(f"pp_s{k}", [P, 512], F32)) for k in range(3)]
        tbank = [st.enter_context(nc.psum_tensor(f"pp_t{k}", [P, 512], F32)) for k in range(2)]
        obank = [st.enter_context(nc.psum_tensor(f"pp_o{k}", [P, 512], F32)) for k in range(2)]
        names = ("loaded", "staged", "scored", "maxed", "exped", "normed", "turned", "moved", "summed", "mixed", "link", "zeroed", "gate")
        loaded, staged, scored, maxed, exped, normed, turned, moved, summed, mixed, link, zeroed, gate = (
            (cx.count if x in ("scored", "exped") else cx.sem)(f"pp_{x}") for x in names)
        inverted = cx.sem("pp_inverted")
        best = sb("best", [TS, 8])
        picked, pick_gate = cx.count("pp_picked"), cx.sem("pp_pick_gate")
        U = 6
        units = [(t, hf) for t in range(3) for hf in range(2)]
        PICKS = U + 2
        assert 8 * PICKS == 2 * (TOPK_S // 8) and TOPK_S % 8 == 0

        def every_chunk(eng, one):
            for p in range(2):
                with eng.Fori(0, 2) as gi:
                    for k in range(2):
                        one(p, gi * 2 + k, gi * 2 + (p * 4 + k), k)

        with cx.block() as block:
            @block.sync
            def _(sp):
                sp.dma_start(flip[:], a["flip"]).then_inc(loaded, 16)
                sp.wait_ge(zeroed, 3)
                for t, (t0, m) in enumerate(QT_TILES):
                    base = bias_rows[:, TP - t0 - m:]
                    src = bass.AP(base.tensor, base.offset, [[1, m], [2 * TP, 16], [1, TP]])
                    sp.dma_start(bias[0:m, t], src).then_inc(loaded, 16)

            @block.vector
            def _(v):
                def one(p, g, n, k):
                    cx.wait(v, scored, n * U)
                    v.tensor_scalar(qs[k][:], projT[:, C_Q + p * 4:C_Q + p * 4 + 4, 0:TP][:, g, :], HD ** -0.5, None,
                                    ALU.mult).then_inc(staged, 1)
                    def greatest(u):
                        t, hf = units[u]
                        m, w = QT_TILES[t][1], sum(QT_TILES[t])
                        cx.wait(v, scored, n * U + u + 1)
                        v.tensor_reduce(stat[u % 2][0:m, 0:1], banks[u % 3][0:m, 0:w], AX, ALU.max).then_inc(link, 1)
                        v.wait_ge(link, n * U + u + 1)
                        v.tensor_scalar(stat[u % 2][0:m, 1:2], stat[u % 2][0:m, 0:1], -1.0, None,
                                        ALU.mult).then_inc(maxed, 1)

                    def normalize(u):
                        t, hf = units[u]
                        m, w = QT_TILES[t][1], sum(QT_TILES[t])
                        cx.wait(v, exped, n * U + u + 1)
                        v.reciprocal(stat[u % 2][0:m, 3:4], stat[u % 2][0:m, 2:3]).then_inc(inverted, 1)
                        v.wait_ge(inverted, n * U + u + 1)
                        v.tensor_scalar(prob[u % 3][0:m, 0:w], prob[u % 3][0:m, 0:w], stat[u % 2][0:m, 3:4], None,
                                        ALU.mult).then_inc(normed, 1)

                    def collect(u):
                        t, hf = units[u]
                        m, w = QT_TILES[t][1], sum(QT_TILES[t])
                        v.wait_ge(turned, n * U + u + 1)
                        v.tensor_copy(pT[hf][:, 0:t + 1, w - m:w],
                                      tbank[u % 2][:, 0:(t + 1) * m].rearrange("p (k q) -> p k q", q=m)) \
                            .then_inc(moved, 1)
                    def pick(step):
                        cx.wait(v, picked, n * PICKS + step, pick_gate)
                        if step % 2:
                            v.match_replace(work_s[:], best[:], work_s[:], MARK).then_inc(picked, 1)
                        else:
                            v.max(best[:], work_s[:]).then_inc(picked, 1)
                    for u in range(U + 2):
                        if u < U:
                            greatest(u)
                        if 1 <= u <= U:
                            normalize(u - 1)
                        if u >= 2:
                            collect(u - 2)
                        pick(u)
                    v.wait_ge(summed, n + 1)
                    v.tensor_copy(mixT[:, 8 + p * 4:12 + p * 4, 0:TP][:, g, :], obank[k][:, 0:TP]).then_inc(mixed, 1)
                v.memset(bias[:, 2], 0.0).then_inc(zeroed, 1)
                for k in range(2):
                    v.memset(pT[k][:], 0.0).then_inc(zeroed, 1)
                v.wait_ge(zeroed, 3)
                every_chunk(v, one)
                cx.wait(v, picked, 8 * PICKS)
                v.tensor_scalar(mask_s[0:TS, :], work_s[:, 0:PAST + S], MARK / 2, NEG, ALU.is_gt,
                                ALU.mult).then_inc(picked, 1)
                cx.wait(v, picked, 8 * PICKS + 1)
                v.tensor_tensor(mask_s[0:TS, PAST:PAST + S], mask_s[0:TS, PAST:PAST + S], newmask[:], ALU.add)

            @block.scalar
            def _(act):
                def one(p, g, n, k):
                    for u, (t, hf) in enumerate(units):
                        t0, m = QT_TILES[t]
                        act.wait_ge(maxed, n * U + u + 1)
                        act.activation(prob[u % 3][0:m, 0:t0 + m], banks[u % 3][0:m, 0:t0 + m], ACT.Exp,
                                       bias=stat[u % 2][0:m, 1:2], accum_out=stat[u % 2][0:m, 2:3]) \
                            .then_inc(exped, 1)
                every_chunk(act, one)

            @block.tensor
            def _(pe):
                pe.wait_ge(loaded, 64)
                pe.wait_ge(zeroed, 3)

                def score(p, g, n, k, u):
                    t, hf = units[u]
                    t0, m = QT_TILES[t]
                    w = t0 + m
                    r = slice(hf * HD, hf * HD + HD)
                    s = banks[u % 3][0:m, 0:w]
                    if u >= 3:
                        cx.wait(pe, exped, n * U + u - 2, gate)
                    fl = flip[:, t // 2, 0:m]
                    heads = bias[:, t].rearrange("p (n g) k -> p n g k", g=GROUP)
                    pe.matmul(s, fl, heads[:, 2 * p + hf, :, 0:w][:, g, :], start=True, stop=False)
                    pe.matmul(s, ident[0:m, 0:m], mask_p[0:m, t, 0:w], start=False, stop=False)
                    pe.matmul(s, qs[k][r, t0:w], projT[r, C_AK + p, 0:w], start=False, stop=True).then_inc(scored, 1)

                def turn(n, u):
                    t, hf = units[u]
                    t0, m = QT_TILES[t]
                    wait_loop(pe, normed, n * U + u + 1, gate)
                    for kt in range(t + 1):
                        kw = QT_TILES[kt][1]
                        mm = pe.transpose(tbank[u % 2][0:kw, kt * m:kt * m + m],
                                          prob[u % 3][0:m, kt * P:kt * P + kw], ident[0:m, 0:m])
                    mm.then_inc(turned, 1)

                def one(p, g, n, k):
                    pe.wait_ge(staged, n + 1)
                    cx.wait(pe, exped, n * U)
                    for u in range(U + 2):
                        if u < U:
                            score(p, g, n, k, u)
                        if u >= 2:
                            if u >= 4:
                                pe.wait_ge(moved, n * U + u - 3)
                            turn(n, u - 2)
                    pe.wait_ge(moved, n * U + U)
                    for hf in range(2):
                        r = slice(hf * HD, hf * HD + HD)
                        for kt, (k0, kw) in enumerate(QT_TILES):
                            mm = pe.matmul(obank[k][r, k0:TP], vrows[0:kw, kt, p * P + hf * HD:p * P + hf * HD + HD],
                                           pT[hf][0:kw, kt, k0:TP], start=kt == 0, stop=kt == 2)
                    mm.then_inc(summed, 1)
                every_chunk(pe, one)


def load_pages(eng, table, pool, b, place, sem):
    for j in range(PAGES):
        page = eng.value_load(table[0:1, bass.ds(b * PAGES + j, 1)], min_val=0, max_val=pool.shape[0] - 1)
        src = pool[bass.ds(page, 1)]
        eng.dma_start(place(j), src.rearrange("o p c -> (o p) c") if len(pool.shape) == 3
                      else src.rearrange("o p a c -> (o p) a c")).then_inc(sem, 16)


def index_sampled(cx, a, projT, wsel, mask_s, work, newmask):
    nc = cx.nc
    SL = 4
    with ExitStack() as st:
        def sb(name, shape, dt=F32):
            return st.enter_context(nc.sbuf_tensor(f"is_{name}", shape, dt))

        keys = [sb(f"keys{k}", [P, PAST + S]) for k in range(SL)]
        qi = [sb(f"qi{k}", [P, IH * S]) for k in range(2)]
        ws = [sb(f"ws{k}", [TS, TS]) for k in range(2)]
        relu = [sb(f"relu{k}", [TS, 512]) for k in range(2)]
        table = sb("table", [1, B * PAGES], I32)
        banks = [st.enter_context(nc.psum_tensor(f"is_s{k}", [P, 512], F32)) for k in range(2)]
        wbanks = [st.enter_context(nc.psum_tensor(f"is_w{k}", [P, 512], F32)) for k in range(2)]
        tabled, small, scored, relued, weighted, added, staged, link, gate = (
            (cx.count if x in ("scored", "relued", "weighted", "added") else cx.sem)(f"is_{x}") for x in ("tabled", "small", "scored", "relued", "weighted", "added", "staged", "link",
                                        "gate"))
        loaded = [cx.sem(f"is_loaded{k}") for k in range(SL)]
        load_gate = cx.sem("is_load_gate")
        C = 5
        block_of = lambda c: slice(c * 512, min(c * 512 + 512, PAST + S))

        with cx.block() as block:
            def load_keys(eng, odd):
                place = lambda k: (lambda j: keys[k][:, j * PAGE:j * PAGE + PAGE])
                eng.wait_ge(tabled, 16)
                for k in range(odd, SL, 2):
                    load_pages(eng, table, a["kidxT"], k, place(k), loaded[k])
                with eng.Fori(0, B // SL - 1) as i:
                    for k in range(odd, SL, 2):
                        cx.wait(eng, scored, i * (SL * C) + (k + 1) * C, load_gate if odd else None)
                        load_pages(eng, table, a["kidxT"], i * SL + (k + SL), place(k), loaded[k])

            @block.sync
            def _(sp):
                sp.dma_start(newmask[:], a["newmask"]).then_inc(small, 16)
                sp.dma_start(table[:], a["page_table"]).then_inc(tabled, 16)
                load_keys(sp, 0)

            @block.gpsimd
            def _(pool):
                load_keys(pool, 1)

            @block.tensor
            def _(pe):
                with pe.Fori(0, B // SL) as i:
                    for k in range(SL):
                        at = (i * SL + k) * C
                        pe.wait_ge(loaded[k], i * 16 * PAGES + 16 * PAGES)
                        pe.wait_ge(staged, i * SL + k + 1)
                        for c in range(C + 1):
                            if c < C:
                                cols = block_of(c)
                                cx.wait(pe, relued, at + c - 1 if c else at)
                                pe.matmul(banks[c % 2][0:TS, 0:cols.stop - cols.start], qi[k % 2][:], keys[k][:, cols],
                                          start=True, stop=True).then_inc(scored, 1)
                            if c:
                                cols = block_of(c - 1)
                                cx.wait(pe, added, at + c - 2 if c > 1 else at)
                                cx.wait(pe, relued, at + c, gate)
                                w = cols.stop - cols.start
                                pe.matmul(wbanks[(c - 1) % 2][0:TS, 0:w], ws[k % 2][:], relu[(c - 1) % 2][:, 0:w],
                                          start=True, stop=True).then_inc(weighted, 1)

            @block.scalar
            def _(act):
                with act.Fori(0, B // SL) as i:
                    for k in range(SL):
                        at = (i * SL + k) * C
                        for c in range(C):
                            w = block_of(c).stop - block_of(c).start
                            cx.wait(act, scored, at + c + 1)
                            cx.wait(act, weighted, at + c - 1 if c else at)
                            act.activation(relu[c % 2][:, 0:w], banks[c % 2][0:TS, 0:w], ACT.Relu).then_inc(relued, 1)

            @block.vector
            def _(v):
                lk = Link(v, link)
                lk(v.memset(work[:, 0:PAST + S], 0.0))
                lk(v.memset(work[:, PAST + S:WORK_S], PAD))
                lk(v.memset(mask_s[TS:TS + 1, 0:FAR], 1.0))
                lk(v.memset(mask_s[TS:TS + 1, FAR:PAST + S], 0.0))
                with v.Fori(0, B // SL) as i:
                    for k in range(SL):
                        at = (i * SL + k) * C
                        b = i * SL + k
                        cx.wait(v, weighted, (i * SL + k - 1) * C if k else i * SL * C)
                        v.tensor_copy(ws[k % 2][:], wsel[:, b, :])
                        v.tensor_copy(keys[k][:, PAST:PAST + S], projT[:, C_KI, TP:N].rearrange(
                            "p (b s) -> p b s", s=S)[:, b, :])
                        v.tensor_copy(qi[k % 2][:].rearrange("p (h s) -> p h s", s=S),
                                      projT[:, C_QI:C_QI + IH, TP:N].rearrange("p h (b s) -> p h b s", s=S)[:, :, b, :]) \
                            .then_inc(staged, 1)
                        for c in range(C):
                            cols = block_of(c)
                            cx.wait(v, weighted, at + c + 1)
                            if c == 0:
                                cx.wait(v, added, at)
                            v.tensor_tensor(work[:, cols], work[:, cols], wbanks[c % 2][0:TS, 0:cols.stop - cols.start],
                                            ALU.add).then_inc(added, 1)
                cx.wait(v, added, B * C)
                v.wait_ge(small, 16)
                lk(v.tensor_tensor(work[:, PAST:PAST + S], work[:, PAST:PAST + S], newmask[:], ALU.add))


def attend_sampled(cx, a, projT, mixT, ident, mask_s, sel, near, onehot, vnew):
    nc = cx.nc
    Q = 64
    with ExitStack() as st:
        def sb(name, shape, dt=F32):
            return st.enter_context(nc.sbuf_tensor(f"as_{name}", shape, dt))

        pages = [sb(f"pages{k}", [P, PAGES, 4, P]) for k in range(2)]
        knew = [sb(f"knew{k}", [P, 2, S]) for k in range(2)]
        vn = [sb(f"vn{k}", [S, 2 * P]) for k in range(2)]
        qb = [sb(f"qb{k}", [P, 2, Q]) for k in range(2)]
        ss = [sb(f"sel{k}", [TS + 1, Q]) for k in range(2)]
        prob = [sb(f"prob{k}", [Q, PAST + S]) for k in range(2)]
        stat = [sb(f"stat{k}", [Q, 10]) for k in range(2)]
        out = sb("out", [Q, 2 * P])
        pT = sb("pT", [P, PAGES + 1, Q])
        table = sb("table", [1, B * PAGES], I32)
        sbank = st.enter_context(nc.psum_tensor("as_s", [P, 5, 512], F32))
        tbank = st.enter_context(nc.psum_tensor("as_t", [P, 2, 512], F32))
        obank = st.enter_context(nc.psum_tensor("as_o", [P, 512], F32))
        tabled, staged, scored, maxed, exped, normed, turned, moved, summed, mixed, link, gate = (
            (cx.count if x in ("exped", "moved", "summed", "mixed") else cx.sem)(f"as_{x}") for x in ("tabled", "staged", "scored", "maxed", "exped", "normed", "turned", "moved",
                                        "summed", "mixed", "link", "gate"))
        returned = cx.sem("as_returned")
        keys_in, values_in = ([cx.sem(f"as_{x}{k}") for k in range(2)] for x in ("keys", "values"))
        load_gate = cx.sem("as_load_gate")
        PER = 4
        FULL = 3 * PER
        REST = PAGE + S
        LK = 6

        with cx.block() as block:
            def load_half(eng, half, arrived, used_up):
                place = lambda k: (lambda j: pages[k][:, j, half])
                source = a["kv_pages"][:, :, half]
                eng.wait_ge(tabled, 16)
                for k in range(2):
                    load_pages(eng, table, source, k, place(k), arrived[k])
                with eng.Fori(0, B // 2 - 1) as i:
                    for k in range(2):
                        used_up(i * 2 + k)
                        load_pages(eng, table, source, i * 2 + (k + 2), place(k), arrived[k])

            @block.sync
            def _(sp):
                sp.dma_start(table[:], a["page_table"]).then_inc(tabled, 16)
                load_half(sp, slice(0, 2), keys_in, lambda b: sp.wait_ge(scored, b + 1))

            @block.gpsimd
            def _(pool):
                load_half(pool, slice(2, 4), values_in, lambda b: cx.wait(pool, summed, b + 1, load_gate))

            @block.vector
            def _(v):
                lk = Link(v, link)
                for k in range(2):
                    lk(v.memset(qb[k][:], 0.0))
                new = projT[:, :, TP:N].rearrange("p c (b s) -> p c b s", s=S)

                def stage(b, k):
                    for p in range(2):
                        for hf in range(2):
                            r = slice(hf * HD, hf * HD + HD)
                            c0 = (2 * p + hf) * 16
                            v.tensor_scalar(qb[k][r, p, c0:c0 + 16].rearrange("p (g s) -> p g s", s=S),
                                            new[r, C_Q + p * 4:C_Q + p * 4 + 4, :, :][:, :, b, :], HD ** -0.5, None,
                                            ALU.mult)
                    v.tensor_copy(knew[k][:], new[:, C_AK:C_AK + 2, :, :][:, :, b, :])
                    v.tensor_copy(vn[k][:], vnew[:, b, :])
                    v.tensor_copy(ss[k][:], sel[:, b, :]).then_inc(staged, 1)

                def greatest(b, k):
                    st = stat[k]
                    v.wait_ge(scored, b + 1)
                    lk(v.tensor_reduce(st[:, 0:3], sbank[0:Q, 0:3, :], AX, ALU.max))
                    lk(v.tensor_reduce(st[:, 3:4], sbank[0:Q, 3, 0:FAR - FULL * PAGE], AX, ALU.max))
                    lk(v.tensor_reduce(st[:, 4:5], sbank[0:Q, 4, 0:REST], AX, ALU.max))
                    lk(v.tensor_reduce(st[:, 5:6], st[:, 0:5], AX, ALU.max))
                    v.tensor_scalar(st[:, 5:6], st[:, 5:6], -1.0, None, ALU.mult).then_inc(maxed, 1)

                def sequence(b, k, nxt, after):
                    st = stat[k]
                    cx.wait(v, exped, b + 1)
                    lk(v.tensor_reduce(st[:, 6:7], st[:, 6:9], AX, ALU.add))
                    lk(v.reciprocal(st[:, 6:7], st[:, 6:7]))
                    v.wait_ge(turned, b + 1)
                    v.tensor_copy(pT[0:S, PAGES, :], obank[0:S, 2 * P + 2 * Q:2 * P + 3 * Q])
                    v.tensor_copy(pT[:, 0:PAGES, :], tbank[:].rearrange("p a (c q) -> p (a c) q", q=Q)) \
                        .then_inc(moved, 1)
                    if nxt:
                        greatest(b + 1, 1 - k)
                    cx.wait(v, summed, b + 1)
                    v.tensor_scalar(out[:], obank[0:Q, 0:2 * P], st[:, 6:7], None, ALU.mult).then_inc(normed, 1)
                    v.wait_ge(returned, b + 1)
                    for p in range(2):
                        for hf in range(2):
                            r = slice(hf * HD, hf * HD + HD)
                            c0 = 2 * P + p * Q + (2 * p + hf) * 16
                            ins = v.tensor_copy(
                                mixT[r, 8 + p * 4:12 + p * 4, TP:N].rearrange("p c (b s) -> p c b s", s=S)[:, :, b, :],
                                obank[r, c0:c0 + 16].rearrange("p (g s) -> p g s", s=S))
                    ins.then_inc(mixed, 1)
                    if after:
                        stage(b + 2, k)
                stage(0, 0)
                stage(1, 1)
                greatest(0, 0)
                with v.Fori(0, B // 2 - 1) as i:
                    lk.enter(i, 2 * LK)
                    for k in range(2):
                        sequence(i * 2 + k, k, True, True)
                    lk.leave(B // 2 - 1)
                sequence(B - 2, 0, True, False)
                sequence(B - 1, 1, False, False)

            @block.scalar
            def _(act):
                with act.Fori(0, B // 2) as i:
                    for k in range(2):
                        b = i * 2 + k
                        act.wait_ge(maxed, b + 1)
                        act.activation(prob[k][:, 0:FULL * PAGE].rearrange("p (a c) -> p a c", a=3),
                                       sbank[0:Q, 0:3, :], ACT.Exp, bias=stat[k][:, 5:6], accum_out=stat[k][:, 6:7])
                        act.activation(prob[k][:, FULL * PAGE:FAR], sbank[0:Q, 3, 0:FAR - FULL * PAGE], ACT.Exp,
                                       bias=stat[k][:, 5:6], accum_out=stat[k][:, 7:8])
                        act.activation(prob[k][:, FAR:PAST + S], sbank[0:Q, 4, 0:REST], ACT.Exp,
                                       bias=stat[k][:, 5:6], accum_out=stat[k][:, 8:9]).then_inc(exped, 1)

            @block.tensor
            def _(pe):
                def scores(b, k, turn):
                    pe.wait_ge(keys_in[k], (turn + 1) * (16 * PAGES))
                    cx.wait(pe, exped, b)
                    wait_loop(pe, staged, b + 1, gate)
                    for c in range(5):
                        c0 = c * PER * PAGE if c < 4 else FAR
                        n = (PER, PER, PER, PER - 1, 1)[c]
                        w = n * PAGE if c < 4 else REST
                        pe.matmul(sbank[0:Q, c, 0:w], ss[k][:], mask_s[:, c0:c0 + w], start=True, stop=False)
                        for p in range(2):
                            j = c0 // PAGE
                            pe.matmul(sbank[0:Q, c, 0:n * PAGE].rearrange("p (j c) -> p j c", j=n), qb[k][:, p, :],
                                      pages[k][:, j:j + n, p, :], start=False, stop=c < 4 and p == 1)
                    for p in range(2):
                        pe.matmul(sbank[0:Q, 4, PAGE:REST], qb[k][:, p, :], knew[k][:, p, :], start=False, stop=False)
                    pe.matmul(sbank[0:Q, 4, 0:REST], near[:], onehot[:], start=False, stop=True).then_inc(scored, 1)

                def sequence(b, k, turn, nxt):
                    cx.wait(pe, exped, b + 1)
                    cx.wait(pe, moved, b, gate)
                    for j in range(PAGES):
                        pe.transpose(tbank[:, j // 8, (j % 8) * Q:(j % 8) * Q + Q],
                                     prob[k][:, j * PAGE:j * PAGE + PAGE], ident[0:Q, 0:Q])
                    cx.wait(pe, mixed, b, gate)
                    pe.transpose(obank[0:S, 2 * P + 2 * Q:2 * P + 3 * Q], prob[k][:, PAST:PAST + S],
                                 ident[0:Q, 0:Q]).then_inc(turned, 1)
                    if nxt:
                        scores(b + 1, 1 - k, turn + k)
                    cx.wait(pe, moved, b + 1)
                    pe.wait_ge(values_in[k], (turn + 1) * (16 * PAGES))
                    for j in range(PAGES):
                        pe.matmul(obank[0:Q, 0:2 * P].rearrange("q (p d) -> q p d", p=2), pT[:, j, :],
                                  pages[k][:, j, 2:4, :], start=j == 0, stop=False)
                    pe.matmul(obank[0:Q, 0:2 * P], pT[0:S, PAGES, :], vn[k][:], start=False, stop=True) \
                        .then_inc(summed, 1)
                    wait_loop(pe, normed, b + 1, gate)
                    for p in range(2):
                        mm = pe.transpose(obank[:, 2 * P + p * Q:2 * P + p * Q + Q], out[:, p * P:p * P + P],
                                          ident[0:Q, 0:Q])
                    mm.then_inc(returned, 1)
                scores(0, 0, 0)
                with pe.Fori(0, B // 2 - 1) as i:
                    for k in range(2):
                        sequence(i * 2 + k, k, i, True)
                sequence(B - 2, 0, B // 2 - 1, True)
                sequence(B - 1, 1, B // 2 - 1, False)


def peer(cx, a, xT, ident):
    nc = cx.nc
    with ExitStack() as st:
        picks = st.enter_context(nc.sbuf_tensor("pe_picks", [P, 3, NY], F32))
        cx.phase(peer_select, a, xT, ident, picks)
        high = st.enter_context(nc.sbuf_tensor("pe_high", [P, KT, NY], F32R))
        low = st.enter_context(nc.sbuf_tensor("pe_low", [P, KT, NY], F32R))
        cx.phase(split, "pe_x", xT, high, low)
        cx.phase(peer_experts, a, xT, high, low, picks)


def peer_select(cx, a, xT, ident, picks):
    nc = cx.nc
    SL = 4
    with ExitStack() as st:
        def sb(name, shape, dt=F32):
            return st.enter_context(nc.sbuf_tensor(f"ps_{name}", shape, dt))[:]

        w = [sb(f"w{s}", [P, KT, P]) for s in range(SL)]
        sk = [sb(f"sk{s}", [P, P]) for s in range(SL)]
        q = [sb(f"q{s}", [P, 3 * P]) for s in range(SL)]
        score = sb("score", [P, 3, NK])
        top = [sb(f"top{h}", [P, 3, EK]) for h in range(2)]
        topi = sb("topi", [P, 3, EK], U32)
        keyf = [sb(f"keyf{h}", [P, 3, EK]) for h in range(2)]
        cand = sb("cand", [P, 3, EK * EK])
        best = sb("best", [P, 3, EK])
        diff = sb("diff", [P, 3, EK])
        bi = sb("bi", [P, 3, EK], U32)
        part = sb("part", [P, 3, EK], U32)
        partf = sb("partf", [P, 3, EK])
        hit = sb("hit", [P, 3 * EK, EK])
        total = sb("total", [P, 3, 1])
        iota = sb("iota", [P, EK])
        chosen = sb("chosen", [P, 3, 3, PH * EK])
        acc = [st.enter_context(nc.psum_tensor(f"ps_acc{s}", [P, 512], F32)) for s in range(SL)]
        sbank = [st.enter_context(nc.psum_tensor(f"ps_s{s}", [P, 512], F32)) for s in range(2)]
        tbank = [st.enter_context(nc.psum_tensor(f"ps_t{s}", [P, 512], F32)) for s in range(2)]
        loaded = [cx.sem(f"ps_loaded{s}") for s in range(SL)]
        summed = [cx.sem(f"ps_summed{s}") for s in range(SL)]
        emptied = [cx.count(f"ps_emptied{s}") for s in range(SL)]
        scored = [cx.count(f"ps_scored{s}") for s in range(SL)]
        read = [cx.count(f"ps_read{s}") for s in range(2)]
        small, gate, link, diffed, exped, turned, moved = (cx.sem(f"ps_{x}") for x in
                                                     ("small", "gate", "link", "diffed", "exped", "turned", "moved"))

        with cx.block() as block:
            @block.sync
            def _(sp):
                sp.dma_start(iota, a["iota"][:, 0:EK]).then_inc(small, 16)
                with sp.Fori(0, 2 * PH // SL) as i:
                    for s in range(SL):
                        cx.wait(sp, scored[s], i)
                        sp.dma_start(w[s], a["peer_wq"][i * SL + s]).then_inc(loaded[s], 16)
                        sp.dma_start(sk[s], a["subkeysT"][i * SL + s]).then_inc(loaded[s], 16)

            @block.tensor
            def _(pe):
                def project_chunk(i, s):
                    pe.wait_ge(loaded[s], i * 32 + 32)
                    cx.wait(pe, emptied[s], i)
                    for k in range(KT):
                        mm = pe.matmul(acc[s][:, 0:NY], w[s][:, k, :], xT[:, k, :], start=k == 0, stop=k == KT - 1)
                    mm.then_inc(summed[s], 1)

                def score_chunk(i, s):
                    cx.wait(pe, emptied[s], i + 1)
                    cx.wait(pe, read[s % 2], i * 2 + s // 2)
                    for t in range(3):
                        mm = pe.matmul(sbank[s % 2][:, t * P:t * P + P], q[s][:, t * P:t * P + P], sk[s],
                                       start=True, stop=True)
                    mm.then_inc(scored[s], 1)

                with pe.Fori(0, 2 * PH // SL) as i:
                    for s in range(SL):
                        project_chunk(i, s)
                        if s:
                            score_chunk(i, s - 1)
                    score_chunk(i, SL - 1)
                pe.wait_ge(link, SL + (2 * PH // SL) * LINKS_PS)
                for which in range(3):
                    if which == 2:
                        pe.wait_ge(moved, 1)
                    for t in range(3):
                        mm = pe.transpose(tbank[which % 2][:, t * P:t * P + P], chosen[:, which, t, :], ident[:])
                    mm.then_inc(turned, 1)

            @block.scalar
            def _(act):
                act.wait_ge(link, SL)
                def take(i, s):
                    act.wait_ge(summed[s], i + 1)
                    cx.wait(act, scored[s], i)
                    act.activation(q[s][:, 0:NY], acc[s][:, 0:NY], ACT.Copy).then_inc(emptied[s], 1)

                def weigh(h):
                    act.wait_ge(diffed, h + 1)
                    act.activation(diff, diff, ACT.Exp).then_inc(exped, 1)

                def turn(i, last):
                    take(i, 1)
                    take(i, 2)
                    weigh(i * 2)
                    take(i, 3)
                    if not last:
                        take(i + 1, 0)
                    weigh(i * 2 + 1)
                take(0, 0)
                with act.Fori(0, 2 * PH // SL - 1) as i:
                    turn(i, False)
                turn(2 * PH // SL - 1, True)

            @block.vector
            def _(v):
                lk = Link(v, link, gate)
                v.wait_ge(small, 16)
                for s in range(SL):
                    lk(v.memset(q[s][:, NY:3 * P], 0.0))

                def half(i, s):
                    cx.wait(v, scored[s], i + 1)
                    v.tensor_copy(score.rearrange("p t k -> p (t k)"), sbank[s % 2][:, 0:3 * P]).then_inc(read[s % 2], 1)
                    cx.wait(v, read[s % 2], i * 2 + s // 2 + 1, gate)
                    tp = top[s % 2]
                    sixteen(lambda t: score[:, t, :], tp)
                    lk(v.tensor_copy(keyf[s % 2], topi))

                def sixteen(values, tp):
                    idx = topi
                    for n in range(2):
                        for t in range(3):
                            ins = v.max(tp[:, t, 8 * n:8 * n + 8], values(t))
                        lk(ins)
                        for t in range(3):
                            ins = v.max_index(idx[:, t, 8 * n:8 * n + 8], tp[:, t, 8 * n:8 * n + 8], values(t))
                        lk(ins)
                        if n == 0:
                            for t in range(3):
                                ins = v.match_replace(values(t), tp[:, t, 0:8], values(t), MARK)
                            lk(ins)

                def head(h):
                    ax = lambda q, where: q.rearrange("p t (k o) -> p t k o" if where else "p t (o k) -> p t o k", o=1)
                    grid = cand.rearrange("p t (x y) -> p t x y", y=EK)
                    for t in range(3):
                        ins = v.tensor_tensor(grid[:, t], ax(top[0], 1)[:, t].to_broadcast([P, EK, EK]),
                                              ax(top[1], 0)[:, t].to_broadcast([P, EK, EK]), ALU.add)
                    lk(ins)
                    sixteen(lambda t: cand[:, t, :], best)
                    lk(v.tensor_copy(bi, topi))
                    v.tensor_tensor(diff, best, best[:, :, 0:1].to_broadcast([P, 3, EK]), ALU.subtract) \
                        .then_inc(diffed, 1)
                    for half_, (op, by) in enumerate(((ALU.logical_shift_right, 4), (ALU.bitwise_and, EK - 1))):
                        lk(v.tensor_scalar(part, bi, by, None, op))
                        lk(v.tensor_copy(partf, part))
                        lk(v.tensor_tensor(hit, partf.rearrange("p t (k o) -> p (t k) o", o=1)
                                           .to_broadcast([P, 3 * EK, EK]),
                                           iota.rearrange("p (o k) -> p o k", o=1).to_broadcast([P, 3 * EK, EK]),
                                           ALU.is_equal))
                        hit4 = hit.rearrange("p (t k) x -> p t k x", t=3)
                        for t in range(3):
                            ins = v.tensor_tensor(hit4[:, t], hit4[:, t],
                                                  ax(keyf[half_], 0)[:, t].to_broadcast([P, EK, EK]), ALU.mult)
                        lk(ins)
                        lk(v.tensor_reduce(chosen[:, half_].rearrange("p t (h k) -> p t h k", h=PH)[:, :, h, :],
                                           hit4, AX, ALU.add))
                    v.wait_ge(exped, h + 1)
                    lk(v.tensor_reduce(total, diff, AX, ALU.add))
                    lk(v.reciprocal(total, total))
                    lk(v.tensor_tensor(chosen[:, 2].rearrange("p t (h k) -> p t h k", h=PH)[:, :, h, :], diff,
                                       total.to_broadcast([P, 3, EK]), ALU.mult))

                with v.Fori(0, 2 * PH // SL) as i:
                    lk.enter(i, LINKS_PS)
                    for s in range(SL):
                        half(i, s)
                        if s % 2:
                            head(i * 2 + s // 2)
                    lk.leave(2 * PH // SL)
                for which in range(3):
                    v.wait_ge(turned, which + 1)
                    v.tensor_copy(picks[:, which, :], tbank[which % 2][:, 0:NY]).then_inc(moved, 1)


def peer_experts(cx, a, xT, high, low, picks):
    nc = cx.nc
    SL = 4
    EH = NK // 2
    E2 = 2
    HALF = D // 2
    G8 = 8
    UP, DOWN = EH // SL, EH // E2 // SL
    PER = UP + 2 * DOWN
    with ExitStack() as st:
        def sb(name, shape, dt=F32):
            return st.enter_context(nc.sbuf_tensor(f"px_{name}", shape, dt))

        gates = sb("gates", [P, EH, NY])
        w, w_low = zip(*(sbuf_both(nc, st, f"px_w{s}", [P, 2048]) for s in range(SL)))
        w_high = [sb(f"wh{s}", [P, 2048], F32R) for s in range(2)]
        h = [sb(f"h{s}", [P, NY]) for s in range(2)]
        g_high = [sb(f"gh{s}", [P, E2, NY], F32R) for s in range(2)]
        g_low = [sb(f"gl{s}", [P, E2, NY], F32R) for s in range(2)]
        iota = sb("iota", [P, NK])
        first = [sb(f"first{k}", [P, G8, EH]) for k in range(2)]
        second = [sb(f"second{k}", [P, G8, NK]) for k in range(2)]
        bank = [st.enter_context(nc.psum_tensor(f"px_bank{s}", [P, 512], F32)) for s in range(8)]
        iota_in = cx.sem("px_iota_in")
        loaded, raised, lowered = ([cx.sem(f"px_{x}{s}") for s in range(SL)] for x in ("loaded", "high", "low"))
        used = [cx.count(f"px_used{s}") for s in range(SL)]
        found, built = cx.sem("px_found"), cx.sem("px_built")
        placed, moved = cx.count("px_placed"), cx.count("px_moved")
        curved, weighed = ([cx.count(f"px_{x}{s}") for s in range(2)] for x in ("curved", "weighed"))
        g_raised, g_lowered, emptied = cx.sem("px_g_high"), cx.sem("px_g_low"), cx.sem("px_emptied")
        steps = NY // (2 * G8)

        def stage(eng, base, turns, one, last=False):
            for s in range(SL):
                one(0, s, base, s == 0, False)
            with eng.Fori(0, turns - 1 - last) as i:
                for s in range(SL):
                    one(i + 1, s, i + (base + 1), False, False)
            if last:
                for s in range(SL):
                    one(turns - 1, s, base + turns - 1, False, s == SL - 1)

        def stages(eng, gate_step, up, down):
            for hf in range(2):
                gate_step(hf)
                stage(eng, hf * PER, UP, lambda *q: up(hf, *q))
                for dh in range(2):
                    stage(eng, hf * PER + UP + dh * DOWN, DOWN, lambda *q: down(hf, dh, *q), last=hf and dh)

        def gate_steps(eng, hf, one):
            for k in range(2):
                one(k, k * G8, hf * 2 * steps + k)
            with eng.Fori(0, steps - 1) as i:
                for k in range(2):
                    one(k, i * (2 * G8) + (2 + k) * G8, i * 2 + (hf * 2 * steps + 2 + k))

        def following(s, turn):
            return (s + 1, turn) if s < SL - 1 else (0, turn + 1)

        with cx.block() as block:
            @block.sync
            def _(sp):
                sp.dma_start(iota[:], a["iota"]).then_inc(iota_in, 16)

                def up(hf, i, s, turn, start, end):
                    cx.wait(sp, used[s], turn)
                    sp.dma_start(w[s][:].rearrange("p (k e) -> p k e", e=P), a["peer_u"][i * SL + (hf * EH + s)]) \
                        .then_inc(loaded[s], 16)

                def down(hf, dh, i, s, turn, start, end):
                    cx.wait(sp, used[s], turn)
                    g = i * SL + (hf * (EH // E2) + s)
                    src = a["peer_v"][:, :, dh]
                    src = src[g] if isinstance(g, int) else src[bass.ds(g, 1)].rearrange("o p e d -> (o p) e d")
                    sp.dma_start(w[s][:].rearrange("p (e d) -> p e d", e=E2), src).then_inc(loaded[s], 16)
                stages(sp, lambda hf: None, up, down)

            def raise_tile(act, s, turn):
                act.wait_ge(loaded[s], turn * 16 + 16)
                cx.wait(act, used[(s + 2) % SL], turn + 1 if s >= 2 else turn)
                act.activation(w_high[s % 2][:], w[s][:], ACT.Copy).then_inc(raised[s], 1)

            def lower_tile(v, s, turn):
                v.wait_ge(raised[s], turn + 1)
                v.tensor_tensor(w_low[s][:], w[s][:], w_high[s % 2][:], ALU.subtract).then_inc(lowered[s], 1)

            @block.scalar
            def _(act):
                def move_gates(hf):
                    if hf:
                        act.wait_ge(g_lowered, 2 * DOWN * SL)

                    def one(k, tok, n):
                        cx.wait(act, placed, n + 1)
                        act.activation(gates[:, :, bass.ds(tok, G8)],
                                       bank[6 + k][:, 0:G8 * EH].rearrange("p (n i) -> p i n", n=G8),
                                       ACT.Copy).then_inc(moved, 1)
                    gate_steps(act, hf, one)

                def up(hf, i, s, turn, start, end):
                    raise_tile(act, *following(s, turn))
                    cx.wait(act, used[s], turn + 1)
                    n = i * 2 + (hf * 2 * UP + s // 2)
                    cx.wait(act, weighed[s % 2], n)
                    act.activation(h[s % 2][:], bank[s][:, 0:NY], ACT.Gelu).then_inc(curved[s % 2], 1)

                def down(hf, dh, i, s, turn, start, end):
                    if start:
                        for k in range(2):
                            cx.wait(act, weighed[k], (hf + 1) * 2 * UP)
                    cx.wait(act, used[(s + 2) % SL], turn + 1 if s >= 2 else turn)
                    act.activation(g_high[s % 2][:], gates[:, bass.ds(i * (SL * E2) + s * E2, E2), :]
                                   if not isinstance(i, int) else gates[:, (i * SL + s) * E2:(i * SL + s + 1) * E2, :],
                                   ACT.Copy).then_inc(g_raised, 1)
                    if not end:
                        raise_tile(act, *following(s, turn))
                raise_tile(act, 0, 0)
                stages(act, move_gates, up, down)

            @block.tensor
            def _(pe):
                def place_gates(hf):
                    if hf:
                        pe.wait_ge(emptied, 16)

                    def one(k, tok, n):
                        pe.wait_ge(built, n + 1)
                        cx.wait(pe, moved, max(n - 1, 0) if isinstance(n, int) else n - 1)
                        for q in range(G8):
                            mm = pe.matmul(bank[6 + k][:, q * EH:q * EH + EH], second[k][:, q, :],
                                           first[k][:, q, :], start=True, stop=True)
                        mm.then_inc(placed, 1)
                    gate_steps(pe, hf, one)

                def up(hf, i, s, turn, start, end):
                    pe.wait_ge(lowered[s], turn + 1)
                    n = i * 2 + (hf * 2 * UP + s // 2 - 1)
                    if not (isinstance(n, int) and n < 0):
                        cx.wait(pe, curved[s % 2], n)
                    for k in range(KT):
                        mm = split_product(pe, bank[s][:, 0:NY], w_high[s % 2][:, k * P:k * P + P],
                                           w_low[s][:, k * P:k * P + P], high[:, k, :], low[:, k, :],
                                           k == 0, k == KT - 1)
                    mm.then_inc(used[s], 1)

                def down(hf, dh, i, s, turn, start, end):
                    if start and dh:
                        pe.wait_ge(emptied, 16 * hf + 8)
                    if start and not dh:
                        for k in range(2):
                            cx.wait(pe, curved[k], (hf + 1) * 2 * UP)
                        cx.wait(pe, moved, (hf + 1) * 2 * steps)
                    pe.wait_ge(lowered[s], turn + 1)
                    pe.wait_ge(g_lowered, i * SL + ((hf * 2 + dh) * DOWN * SL + s + 1))
                    for e in range(E2):
                        for d in range(8):
                            c = e * HALF + d * P
                            mm = split_product(pe, bank[d][:, 0:NY], w_high[s % 2][:, c:c + P], w_low[s][:, c:c + P],
                                               g_high[s % 2][:, e, :], g_low[s % 2][:, e, :], start and e == 0, end and e == 1)
                    mm.then_inc(used[s], 1)
                stages(pe, place_gates, up, down)

            @block.vector
            def _(v):
                def build_onehots(hf):

                    def picked(which, tok, width):
                        return picks[:, which, bass.ds(tok, G8)].rearrange("p (n o) -> p n o", o=1) \
                            .to_broadcast([P, G8, width])

                    def keys(start, width):
                        return iota[:, start:start + width].rearrange("p (o i) -> p o i", o=1) \
                            .to_broadcast([P, G8, width])

                    def one(k, tok, n):
                        cx.wait(v, placed, max(n - 1, 0) if isinstance(n, int) else n - 1)
                        v.tensor_tensor(first[k][:], keys(hf * EH, EH), picked(0, tok, EH),
                                        ALU.is_equal).then_inc(found, 1)
                        v.tensor_tensor(second[k][:], keys(0, NK), picked(1, tok, NK), ALU.is_equal)
                        v.wait_ge(found, n + 1)
                        v.tensor_tensor(first[k][:], first[k][:], picked(2, tok, EH), ALU.mult).then_inc(built, 1)
                    gate_steps(v, hf, one)

                def up(hf, i, s, turn, start, end):
                    if start:
                        cx.wait(v, moved, (hf + 1) * 2 * steps)
                    lower_tile(v, *following(s, turn))
                    n = i * 2 + (hf * 2 * UP + s // 2 + 1)
                    cx.wait(v, curved[s % 2], n)
                    g = gates[:, i * SL + s, :]
                    v.tensor_tensor(g, g, h[s % 2][:], ALU.mult).then_inc(weighed[s % 2], 1)

                def down(hf, dh, i, s, turn, start, end):
                    if start:
                        for k in range(2):
                            cx.wait(v, weighed[k], (hf + 1) * 2 * UP)
                    n = i * SL + ((hf * 2 + dh) * DOWN * SL + s + 1)
                    v.wait_ge(g_raised, n)
                    g = gates[:, bass.ds(i * (SL * E2) + s * E2, E2), :] \
                        if not isinstance(i, int) else gates[:, (i * SL + s) * E2:(i * SL + s + 1) * E2, :]
                    v.tensor_tensor(g_low[s % 2][:], g, g_high[s % 2][:], ALU.subtract).then_inc(g_lowered, 1)
                    if not end:
                        lower_tile(v, *following(s, turn))

                def drain(hf, dh):
                    for s in range(SL):
                        cx.wait(v, used[s], hf * PER + UP + (dh + 1) * DOWN)
                    for d in range(8):
                        x = xT[:, dh * 8 + d, :]
                        v.scalar_tensor_tensor(x, x, 1.0 if hf else ALPHA, bank[d][:, 0:NY], ALU.mult,
                                               ALU.add).then_inc(emptied, 1)
                v.wait_ge(iota_in, 16)
                for hf in range(2):
                    build_onehots(hf)
                    if hf == 0:
                        lower_tile(v, 0, 0)
                    stage(v, hf * PER, UP, lambda *q: up(hf, *q))
                    for dh in range(2):
                        if hf or dh:
                            v.wait_ge(emptied, (2 * hf + dh) * 8)
                        stage(v, hf * PER + UP + dh * DOWN, DOWN, lambda *q: down(hf, dh, *q), last=hf and dh)
                        drain(hf, dh)


LINKS_PS = 64

def chunked(w, cols):
    w = np.asarray(w)
    out = np.zeros((w.shape[0], len(cols)), w.dtype)
    ok = cols >= 0
    out[:, ok] = w[:, cols[ok]]
    return np.ascontiguousarray(out.reshape(w.shape[0] // P, P, len(cols) // P, P).transpose(2, 1, 0, 3))


def in_columns():
    cols = list(range(RC)) + [-1] * (RWC * P - RC)
    cols += [RC + x for x in q_order()]
    cols += list(range(RC + 1024, RC + 1024 + 512 + IH * ID + ID + IH)) + [-1] * (P - IH)
    return np.array(cols)


def q_order():
    return [((2 * p + hf) * GROUP + g) * HD + d for p in range(2) for g in range(GROUP) for hf in range(2)
            for d in range(HD)]


def fold(v, chunks):
    v = np.asarray(v).reshape(-1)
    return np.ascontiguousarray(np.pad(v, (0, chunks * P - v.size)).reshape(chunks, P).T)


def across(s):
    out = np.zeros((8, 2, HD, B, 2, HD), s.dtype)
    for h in range(2):
        out[:, h, :, :, h, :] = s[:, h]
    return out.reshape(8, P, B, P)


def attention_layouts(x):
    f = np.float32
    e = np.eye
    hs = np.arange(TS)
    t = np.arange(2 * TP)
    s, key = np.arange(S)[:, None], FAR + np.arange(PAGE + S)[None, :]
    near = bucket(PAST + s - key)
    q, kpos = np.arange(3 * P), np.arange(TP)
    flip = np.zeros((P, 2, P), f)
    flip[:, 0] = e(P)[::-1]
    flip[:16, 1, :16] = e(16)[::-1]
    n_pool = x["cache_k"].shape[1]
    qn = np.arange(64)
    return {
        "spread": (np.arange(IH)[:, None] == hs[None, :] // S).astype(f),
        "wpick": ((hs[:, None, None] % S == hs[None, None, :] % S)
                  & (np.arange(B)[None, :, None] == hs[None, None, :] // S)).astype(f),
        "spick": np.broadcast_to(np.arange(P)[:, None, None] // 32 == np.arange(S)[None, None, :], (P, 16, S)).astype(f),
        "bucket_table": (np.arange(NB_BUCKETS)[:, None] == bucket(TP - 1 - t)[None, :]).astype(f),
        "near_onehot": (near[:, None, :] == np.arange(NB_BUCKETS)[None, :, None]).reshape(P, PAGE + S).astype(f),
        "sel": ((hs[:, None, None] // S == np.arange(B)[None, :, None])
                & (hs[:, None, None] % S == qn[None, None, :] % S)).astype(f),
        "rel_bias": x["rel_bias"],
        "causal": np.where(kpos[None, :] <= q[:, None], 0, NEG).reshape(3, P, TP).transpose(1, 0, 2).astype(f),
        "newmask": np.where(np.arange(S)[None, :] <= (hs % S)[:, None], 0, NEG).astype(f),
        "flip": flip,
        "page_table": x["page_table"].reshape(1, -1).astype(np.int32),
        "kidxT": x["cache_kidx"][0].transpose(0, 2, 1),
        "kv_pages": np.concatenate([x["cache_k"][0].reshape(n_pool, PAGE, 2, P).transpose(0, 3, 2, 1),
                                    x["cache_v"][0].reshape(n_pool, PAGE, 2, P)], 2),
    }


def layouts(x):
    f = np.float32
    rows = np.concatenate([x["meta_tokens"], x["x_prompt"][0], x["x_sample"].reshape(TS, D)])
    a = {
        "xT": rows.T.reshape(KT, P, N).transpose(1, 0, 2),
        "ones": np.full((P, P), 1 / D, f),
        "ident": np.eye(P, dtype=f),
        "ln_gb": np.stack([np.stack([fold(x[g], KT), fold(x[b], KT)], 1)
                           for g, b in (("ln_in_g", "ln_in_b"), ("ln1_g", "ln1_b"), ("ln2_g", "ln2_b"))], 1),
        "rw_masks": rwkv_masks(),
        "seqmask": (np.arange(P)[:, None] // S - CH // 2 // S == np.arange(B)[None, :]).astype(f),
        "halves": (np.arange(P)[:, None] // HD == np.arange(P)[None, :] // HD).astype(f),
        "rw_cols": np.stack([fold(x["mu_shift"][0][:RW], 8), fold(x["mu_shift"][0][RW:2 * RW], 8),
                             fold(x["mu_shift"][0][2 * RW:3 * RW], 8)]
                            + [fold(x[q], 8) for q in ("k_k", "k_a", "r_k", "w0", "a0", "gn_g", "gn_b")], 2),
        "mu": fold(x["mu_shift"], RWC),
        "shiftT_in": np.stack([fold(x["state_shift"][0, b], RWC) for b in range(B)], 2),
        "wa_up": np.concatenate([x["w_up"][0], x["a_up"][0]]),
        "g_up": x["g_up"][0],
        "wkvT": across(x["state_wkv"][0].reshape(B, 8, 2, HD, HD).transpose(1, 2, 4, 0, 3)),
        **attention_layouts(x),
        "iota": np.broadcast_to(np.arange(NK), (P, NK)).astype(f),
        "peer_wq": chunked(x["peer_wq"][0], np.arange(D)),
        "subkeysT": x["peer_subkeys"][0].reshape(2 * PH, NK, P).transpose(0, 2, 1),
        "peer_u": x["peer_u"][0].reshape(NK, NK, KT, P).transpose(0, 3, 2, 1),
        "peer_v": x["peer_v"][0].reshape(NK // 2, 2, NK, 2, D // 2).transpose(0, 2, 3, 1, 4),
        "w_in": chunked(x["w_in"][0], in_columns()),
        "w_o": chunked(np.concatenate([x["w_o"][0][:RW], x["w_o"][0][RW:][q_order()]]), np.arange(D)),
    }
    return a


def outputs():
    return {"yT": (P, KT, NY), "kvT": (P, 4, N), "kiT": (P, N), "shiftT": (P, RWC, B + 1),
            "wkvT_p": (8, P, HD), "wkvT_s": (8, P, B, HD)}


def kernel(**inputs):
    import concourse.bacc as bacc
    from concourse.bass_utils import run_bass_kernel_spmd as run

    x = {k: np.asarray(v) for k, v in inputs.items()}
    arrays = {k: np.ascontiguousarray(v) for k, v in layouts(x).items()}
    nc = bacc.Bacc("TRN2", target_bir_lowering=False, num_devices=1)
    a = {k: nc.dram_tensor(f"in_{k}", v.shape, mybir.dt.from_np(v.dtype), kind="ExternalInput").ap()
         for k, v in arrays.items()}
    o = {k: nc.dram_tensor(f"out_{k}", s, F32, kind="ExternalOutput").ap() for k, s in outputs().items()}
    build(nc, a, o)
    r = run(nc, [{f"in_{k}": v for k, v in arrays.items()}], core_ids=[0]).results[0]
    r = {k: np.asarray(r[f"out_{k}"]) for k in o}

    y = r["yT"].transpose(2, 1, 0).reshape(NY, D)
    kv = r["kvT"].transpose(2, 1, 0).reshape(N, 2, KVH, HD)
    ki = r["kiT"].T
    shift = r["shiftT"].transpose(2, 1, 0).reshape(B + 1, RWC * P)[:, :RC]
    wkv_p = r["wkvT_p"].reshape(16, HD, HD).transpose(0, 2, 1)
    wkv_s = r["wkvT_s"].reshape(16, HD, B, HD).transpose(2, 0, 3, 1)
    c = np.ascontiguousarray
    return (c(y[:SEQ])[None], c(y[SEQ:]).reshape(B, S, D),
            c(kv[:TP, 0])[None, None], c(kv[:TP, 1])[None, None], c(ki[:TP])[None, None],
            c(wkv_p)[None, None], c(shift[0])[None, None],
            c(kv[TP:, 0]).reshape(1, B, S, KVH, HD), c(kv[TP:, 1]).reshape(1, B, S, KVH, HD),
            c(ki[TP:]).reshape(1, B, S, ID), c(wkv_s)[None], c(shift[1:])[None])
```
